# Optimizing a Trainium2 kernel written in Bass

```python
import jax, jax.numpy as jnp
from jax import lax
import numpy as np
import math

D_MODEL = 1024
BATCH = 1
SEQ = 512
DEPTH = 2

CHUNK = 64
N_MEM = 256
NORM_EPS = 1e-6
NEG_BIG = -1e30
GATE_CLIP = 60.0
MIX_WIDTH = D_MODEL
POOL_WIDTH = MIX_WIDTH // 2
POOL_WINDOWS = (2, 4, 8, 16)
POOL_GROUPS = len(POOL_WINDOWS)
POOL_GROUP_DIM = POOL_WIDTH // POOL_GROUPS
REC_WIDTH = MIX_WIDTH - POOL_WIDTH
REC_EXPAND = 128
REC_HEADS = REC_WIDTH // REC_EXPAND
REC_HEAD_DIM = REC_WIDTH // REC_HEADS
ATT_HEADS = 16
ATT_HEAD_DIM = MIX_WIDTH // ATT_HEADS
BAND_CHUNKS = 8
BAND = (BAND_CHUNKS + 1) * CHUNK
REL_CLIP = 256
MEM_HEADS = 4
MEM_HEAD_DIM = D_MODEL // MEM_HEADS
FF_DIM = 4 * D_MODEL
N_EVEN = (DEPTH + 1) // 2
N_ODD = DEPTH // 2


def rmsnorm(x, g):
    xf = x.astype(jnp.float32)
    y = xf * lax.rsqrt(jnp.mean(xf * xf, axis=-1, keepdims=True) + NORM_EPS)
    return y.astype(x.dtype) * g

def causal_multiscale_pool(u):
    S_ = u.shape[1]
    uf = u.astype(jnp.float32)
    cs = jnp.cumsum(uf, axis=1)
    pos = jnp.arange(1, S_ + 1, dtype=jnp.float32)
    outs = []
    for g, w in enumerate(POOL_WINDOWS):
        c = cs[:, :, g]
        lag = jnp.pad(c, ((0, 0), (w, 0), (0, 0)))[:, :S_]
        outs.append((c - lag) / jnp.minimum(pos, w)[:, None])
    mean = jnp.stack(outs, axis=2)
    return (mean - uf).astype(u.dtype)

def hgrn2_chunkwise(q, k, v, logf):
    B_, S_, H, dk = q.shape
    dv = v.shape[-1]
    N = S_ // CHUNK

    def to_chunks(a):
        return a.reshape(B_, N, CHUNK, H, a.shape[-1]).transpose(1, 0, 3, 2, 4)

    causal = jnp.tril(jnp.ones((CHUNK, CHUNK), dtype=bool))[None, None, :, :, None]

    def step(state, inp):
        qc, kc, vc, lc = inp
        b = jnp.cumsum(lc, axis=2)
        o_inter = jnp.einsum('bhtd,bhde->bhte', qc * jnp.exp(b), state)
        diff = b[:, :, :, None, :] - b[:, :, None, :, :]
        decay = jnp.where(causal, jnp.exp(jnp.where(causal, diff, 0.0)), 0.0)
        scores = jnp.einsum('bhtd,bhsd,bhtsd->bhts', qc, kc, decay)
        o = o_inter + jnp.einsum('bhts,bhse->bhte', scores, vc)
        b_last = b[:, :, -1:, :]
        new_state = jnp.exp(b_last[:, :, 0, :])[..., None] * state + jnp.einsum(
            'bhsd,bhse->bhde', kc * jnp.exp(b_last - b), vc)
        return new_state, o

    init = jnp.zeros((B_, H, dk, dv), jnp.float32)
    _, o = lax.scan(step, init, (to_chunks(q), to_chunks(k), to_chunks(v), to_chunks(logf)))
    return o.transpose(1, 0, 3, 2, 4).reshape(B_, S_, H, dv)

def even_mixer(h, w_in, pool_w, pool_scale, lb, out_gain, w_out):
    B_, S_, _ = h.shape
    z = h @ w_in
    cuts = [POOL_WIDTH + r * REC_WIDTH for r in range(4)]
    u, q, fz, i, g = jnp.split(z, cuts, axis=-1)
    pooled = causal_multiscale_pool(u.reshape(B_, S_, POOL_GROUPS, POOL_GROUP_DIM))
    a_out = jnp.einsum('bsgc,gcd->bsgd', pooled, pool_w).reshape(B_, S_, POOL_WIDTH) * pool_scale
    fz32 = jnp.clip(fz.astype(jnp.float32), -GATE_CLIP, GATE_CLIP)
    logf = jax.nn.log_sigmoid(fz32) + jnp.log1p(lb * jnp.exp(-fz32))
    k = (1.0 - lb) * jax.nn.sigmoid(-fz32)
    hs = lambda a: a.reshape(B_, S_, REC_HEADS, -1)
    o = hgrn2_chunkwise(hs(q.astype(jnp.float32)), hs(k), hs(i.astype(jnp.float32)), hs(logf))
    o = rmsnorm(o, out_gain.astype(jnp.float32)) * jax.nn.silu(hs(g.astype(jnp.float32)))
    b_out = o.reshape(B_, S_, REC_WIDTH).astype(h.dtype)
    return jnp.concatenate([a_out.astype(h.dtype), b_out], axis=-1) @ w_out

def chunk_band_attention(q, k, v, rel_bias):
    B_, S_, H, dh = q.shape
    N = S_ // CHUNK
    pad = ((0, 0), (BAND_CHUNKS * CHUNK, 0), (0, 0), (0, 0))
    kp = jnp.pad(k, pad)
    vp = jnp.pad(v, pad)
    t = jnp.arange(CHUNK)[:, None]
    j = jnp.arange(BAND)[None, :]
    rel = BAND_CHUNKS * CHUNK + t - j
    idx = jnp.clip(rel, -REL_CLIP, REL_CLIP) + REL_CLIP
    bias = rel_bias[:, idx].astype(jnp.float32)
    scale = dh ** -0.5

    def per_chunk(n):
        qn = lax.dynamic_slice_in_dim(q, n * CHUNK, CHUNK, axis=1)
        kn = lax.dynamic_slice_in_dim(kp, n * CHUNK, BAND, axis=1)
        vn = lax.dynamic_slice_in_dim(vp, n * CHUNK, BAND, axis=1)
        s = jnp.einsum('bthd,bjhd->bhtj', qn, kn).astype(jnp.float32) * scale + bias
        valid = (n - BAND_CHUNKS) * CHUNK + jnp.arange(BAND) >= 0
        s = jnp.where(valid[None, None, None, :], s, NEG_BIG)
        p = jax.nn.softmax(s, axis=-1).astype(v.dtype)
        return jnp.einsum('bhtj,bjhd->bthd', p, vn)

    out = lax.map(per_chunk, jnp.arange(N))
    return jnp.moveaxis(out, 0, 1).reshape(B_, S_, H, dh)

def odd_mixer(h, w_qkv, rel_bias, w_o):
    B_, S_, _ = h.shape
    qkv = (h @ w_qkv).reshape(B_, S_, 3, ATT_HEADS, ATT_HEAD_DIM)
    o = chunk_band_attention(qkv[:, :, 0], qkv[:, :, 1], qkv[:, :, 2], rel_bias)
    return o.reshape(B_, S_, MIX_WIDTH) @ w_o

def memory_cross_attention(h, mem_n, w_q, w_kv, w_o):
    B_, S_, _ = h.shape
    M = mem_n.shape[1]
    q = (h @ w_q).reshape(B_, S_, MEM_HEADS, MEM_HEAD_DIM)
    kv = (mem_n @ w_kv).reshape(B_, M, 2, MEM_HEADS, MEM_HEAD_DIM)
    s = jnp.einsum('bshd,bmhd->bhsm', q, kv[:, :, 0]).astype(jnp.float32) * MEM_HEAD_DIM ** -0.5
    p = jax.nn.softmax(s, axis=-1).astype(h.dtype)
    o = jnp.einsum('bhsm,bmhd->bshd', p, kv[:, :, 1]).reshape(B_, S_, D_MODEL)
    return o @ w_o

def squared_relu_mlp(h, w1, w2):
    a = jax.nn.relu(h @ w1)
    return (a * a) @ w2

def first_inputs(seed: int = 0) -> dict:
    key = jax.random.key(seed)
    ks = jax.random.split(key, 20)
    f32 = jnp.float32

    def dense(k, shape):
        return jax.random.normal(k, shape, f32) * shape[-2] ** -0.5

    return {
        'x': jax.random.normal(ks[0], (BATCH, SEQ, D_MODEL), f32),
        'mem': jax.random.normal(ks[1], (BATCH, N_MEM, D_MODEL), f32),
        'norm_gains': 1.0 + 0.05 * jax.random.normal(ks[2], (DEPTH, 6, D_MODEL), f32),
        'mem_norm_gain': 1.0 + 0.05 * jax.random.normal(ks[3], (D_MODEL,), f32),
        'w_in_ab': dense(ks[4], (N_EVEN, D_MODEL, POOL_WIDTH + 4 * REC_WIDTH)),
        'pool_w': dense(ks[5], (N_EVEN, POOL_GROUPS, POOL_GROUP_DIM, POOL_GROUP_DIM)),
        'pool_scale': 1.0 + 0.1 * jax.random.normal(ks[6], (N_EVEN, POOL_WIDTH), f32),
        'rec_lb_logits': 0.1 * jax.random.normal(ks[7], (N_EVEN, REC_WIDTH), f32),
        'rec_out_gain': 1.0 + 0.05 * jax.random.normal(ks[8], (N_EVEN, REC_HEAD_DIM), f32),
        'w_out_ab': dense(ks[9], (N_EVEN, MIX_WIDTH, D_MODEL)),
        'w_qkv': dense(ks[10], (N_ODD, D_MODEL, 3 * MIX_WIDTH)),
        'rel_bias': 0.1 * jax.random.normal(ks[11], (N_ODD, ATT_HEADS, 2 * REL_CLIP + 1), f32),
        'w_o_att': dense(ks[12], (N_ODD, MIX_WIDTH, D_MODEL)),
        'w_mem_q': dense(ks[13], (DEPTH, D_MODEL, D_MODEL)),
        'w_mem_kv': dense(ks[14], (DEPTH, D_MODEL, 2 * D_MODEL)),
        'w_mem_o': dense(ks[15], (DEPTH, D_MODEL, D_MODEL)),
        'w_ff1': dense(ks[16], (DEPTH, D_MODEL, FF_DIM)),
        'w_ff2': dense(ks[17], (DEPTH, FF_DIM, D_MODEL)),
    }

def first_block(x, mem, norm_gains, mem_norm_gain, w_in_ab, pool_w, pool_scale, rec_lb_logits,
              rec_out_gain, w_out_ab, w_qkv, rel_bias, w_o_att, w_mem_q, w_mem_kv, w_mem_o,
              w_ff1, w_ff2):
    lb_p = jax.nn.softmax(rec_lb_logits.astype(jnp.float32), axis=0)
    lbs = jnp.clip(jnp.cumsum(lb_p, axis=0) - lb_p[0], 0.0, 1.0)
    mem_n = rmsnorm(mem, mem_norm_gain)
    for l in range(DEPTH):
        g = norm_gains[l]
        h = rmsnorm(x, g[0])
        if l % 2 == 0:
            e = l // 2
            y = even_mixer(h, w_in_ab[e], pool_w[e], pool_scale[e], lbs[e], rec_out_gain[e],
                           w_out_ab[e])
        else:
            o = l // 2
            y = odd_mixer(h, w_qkv[o], rel_bias[o], w_o_att[o])
        x = x + rmsnorm(y, g[1])
        h = rmsnorm(x, g[2])
        x = x + rmsnorm(memory_cross_attention(h, mem_n, w_mem_q[l], w_mem_kv[l], w_mem_o[l]), g[3])
        h = rmsnorm(x, g[4])
        x = x + rmsnorm(squared_relu_mlp(h, w_ff1[l], w_ff2[l]), g[5])
    return x


DEPTH_2 = 1

MIX_WIDTH_2 = D_MODEL
CONV_WIDTH = MIX_WIDTH_2 // 2
CONV_KSIZE = 31
RW_WIDTH = MIX_WIDTH_2 - CONV_WIDTH
RW_HEAD_DIM = 64
RW_HEADS = RW_WIDTH // RW_HEAD_DIM
LORA_W = 64
LORA_A = 64
LORA_G = 128
RW_PROJ = 3 * RW_WIDTH + LORA_W + LORA_A + LORA_G
IN_PROJ = 2 * CONV_WIDTH + RW_PROJ
PEER_HEADS = 8
PEER_NKEYS = 128
PEER_TOPK = 16
PEER_QDIM = 256
PEER_N_EXPERTS = PEER_NKEYS * PEER_NKEYS
PEER_TOKEN_BLOCK = 128
ALPHA = (2.0 * DEPTH_2) ** 0.25
BETA = (8.0 * DEPTH_2) ** -0.25
LN_EPS = 1e-5
GN_EPS = 64e-5


def layer_norm(x, g=None, b=None, eps=LN_EPS):
    xf = x.astype(jnp.float32)
    mu = jnp.mean(xf, axis=-1, keepdims=True)
    var = jnp.mean(jnp.square(xf - mu), axis=-1, keepdims=True)
    y = (xf - mu) * lax.rsqrt(var + eps)
    if g is not None:
        y = y * g + b
    return y

def adaln(x, shift, scale):
    return layer_norm(x) * (1.0 + scale[:, None, :]) + shift[:, None, :]

def rwkv7_scan(r, decay, k, v, kk, a):
    bsz, _, nh, nd = r.shape
    xs = tuple(jnp.moveaxis(t.astype(jnp.float32), 1, 0) for t in (r, decay, k, v, kk, a))

    def step(state, inp):
        r_t, w_t, k_t, v_t, kk_t, a_t = inp
        sa = jnp.einsum('bhvk,bhk->bhv', state, -kk_t)
        state = (state * w_t[:, :, None, :]
                 + sa[..., None] * (kk_t * a_t)[:, :, None, :]
                 + v_t[..., None] * k_t[:, :, None, :])
        y_t = jnp.einsum('bhvk,bhk->bhv', state, r_t)
        return state, y_t

    state0 = jnp.zeros((bsz, nh, nd, nd), jnp.float32)
    _, ys = lax.scan(step, state0, xs)
    return jnp.moveaxis(ys, 0, 1)

def second_inputs(seed: int = 0) -> dict:
    key = jax.random.key(seed)
    ks = jax.random.split(key, 40)
    f32 = jnp.float32

    def nrm(k, shape, scale):
        return jax.random.normal(k, shape, f32) * scale

    s_in = D_MODEL ** -0.5
    col_scale = s_in * jnp.concatenate([
        jnp.full((CONV_WIDTH,), BETA, f32),
        jnp.ones((CONV_WIDTH,), f32),
        jnp.ones((2 * RW_WIDTH,), f32),
        jnp.full((RW_WIDTH,), BETA, f32),
        jnp.ones((LORA_W + LORA_A + LORA_G,), f32),
    ])
    return {
        "x": nrm(ks[0], (BATCH, SEQ, D_MODEL), 1.0),
        "c": nrm(ks[1], (BATCH, D_MODEL), 1.0),
        "cond_w": nrm(ks[2], (D_MODEL, 6 * D_MODEL), 0.5 * D_MODEL ** -0.5),
        "cond_b": nrm(ks[3], (6 * D_MODEL,), 0.02),
        "w_in": jax.random.normal(ks[4], (D_MODEL, IN_PROJ), f32) * col_scale,
        "mu_shift": jax.random.uniform(ks[5], (RW_PROJ,), f32),
        "conv_w": nrm(ks[6], (CONV_KSIZE, CONV_WIDTH), CONV_KSIZE ** -0.5),
        "conv_b": nrm(ks[7], (CONV_WIDTH,), 0.02),
        "conv_ln_g": 1.0 + nrm(ks[8], (CONV_WIDTH,), 0.05),
        "conv_ln_b": nrm(ks[9], (CONV_WIDTH,), 0.02),
        "rw_w0": jnp.linspace(-7.0, -2.0, RW_WIDTH, dtype=f32) + nrm(ks[10], (RW_WIDTH,), 0.1),
        "rw_w2": nrm(ks[11], (LORA_W, RW_WIDTH), 0.1 * LORA_W ** -0.5),
        "rw_a0": nrm(ks[12], (RW_WIDTH,), 0.1),
        "rw_a2": nrm(ks[13], (LORA_A, RW_WIDTH), LORA_A ** -0.5),
        "rw_g2": nrm(ks[14], (LORA_G, RW_WIDTH), LORA_G ** -0.5),
        "rw_kk": 0.85 + nrm(ks[15], (RW_WIDTH,), 0.05),
        "rw_ka": 1.0 + nrm(ks[16], (RW_WIDTH,), 0.05),
        "rw_rk": nrm(ks[17], (RW_HEADS, RW_HEAD_DIM), 0.1),
        "rw_lnx_g": 1.0 + nrm(ks[18], (RW_WIDTH,), 0.05),
        "rw_lnx_b": nrm(ks[19], (RW_WIDTH,), 0.02),
        "w_out": nrm(ks[20], (MIX_WIDTH_2, D_MODEL), BETA * MIX_WIDTH_2 ** -0.5),
        "ln1_g": 1.0 + nrm(ks[21], (D_MODEL,), 0.05),
        "ln1_b": nrm(ks[22], (D_MODEL,), 0.02),
        "peer_wq": nrm(ks[23], (D_MODEL, PEER_HEADS * PEER_QDIM), s_in),
        "peer_k1": nrm(ks[24], (PEER_HEADS, PEER_NKEYS, PEER_QDIM // 2), (PEER_QDIM // 2) ** -0.5),
        "peer_k2": nrm(ks[25], (PEER_HEADS, PEER_NKEYS, PEER_QDIM // 2), (PEER_QDIM // 2) ** -0.5),
        "peer_u": nrm(ks[26], (PEER_N_EXPERTS, D_MODEL), BETA * s_in),
        "peer_v": nrm(ks[27], (PEER_N_EXPERTS, D_MODEL), BETA),
        "ln2_g": 1.0 + nrm(ks[28], (D_MODEL,), 0.05),
        "ln2_b": nrm(ks[29], (D_MODEL,), 0.02),
    }

def second_block(x, c, cond_w, cond_b, w_in, mu_shift, conv_w, conv_b, conv_ln_g, conv_ln_b,
              rw_w0, rw_w2, rw_a0, rw_a2, rw_g2, rw_kk, rw_ka, rw_rk, rw_lnx_g, rw_lnx_b,
              w_out, ln1_g, ln1_b, peer_wq, peer_k1, peer_k2, peer_u, peer_v, ln2_g, ln2_b):
    bsz, seq, dm = x.shape

    mod = jax.nn.silu(c) @ cond_w + cond_b
    shift1, scale1, gate1, shift2, scale2, gate2 = jnp.split(mod, 6, axis=-1)

    for _ in range(DEPTH_2):
        h = adaln(x, shift1, scale1)
        p = h @ w_in
        p_conv = p[..., :2 * CONV_WIDTH]
        p_rw = p[..., 2 * CONV_WIDTH:]

        u = p_conv[..., :CONV_WIDTH] * jax.nn.sigmoid(p_conv[..., CONV_WIDTH:])
        u = lax.conv_general_dilated(
            u, conv_w.astype(u.dtype)[:, None, :], window_strides=(1,),
            padding=[(CONV_KSIZE - 1, 0)], dimension_numbers=('NWC', 'WIO', 'NWC'),
            feature_group_count=CONV_WIDTH) + conv_b
        y_conv = jax.nn.silu(layer_norm(u, conv_ln_g, conv_ln_b))

        p_prev = jnp.pad(p_rw[:, :-1], ((0, 0), (1, 0), (0, 0)))
        xm = p_rw + (p_prev - p_rw) * mu_shift
        o = 0
        r = xm[..., o:o + RW_WIDTH]; o += RW_WIDTH
        k = xm[..., o:o + RW_WIDTH]; o += RW_WIDTH
        v = xm[..., o:o + RW_WIDTH]; o += RW_WIDTH
        wd = xm[..., o:o + LORA_W]; o += LORA_W
        ad = xm[..., o:o + LORA_A]; o += LORA_A
        gd = xm[..., o:o + LORA_G]
        w_log = -jax.nn.softplus(-(rw_w0 + jnp.tanh(wd) @ rw_w2)) - 0.5
        decay = jnp.exp(-jnp.exp(w_log.astype(jnp.float32)))
        a = jax.nn.sigmoid(rw_a0 + ad @ rw_a2)
        g = jax.nn.sigmoid(gd) @ rw_g2
        heads = lambda t: t.reshape(bsz, seq, RW_HEADS, RW_HEAD_DIM)
        kk = heads(k * rw_kk).astype(jnp.float32)
        kk = kk / jnp.maximum(jnp.linalg.norm(kk, axis=-1, keepdims=True), 1e-12)
        k = k * (1.0 + (a - 1.0) * rw_ka)
        rh, kh, vh, ah = heads(r), heads(k), heads(v), heads(a)
        y_rw = rwkv7_scan(rh, heads(decay), kh, vh, kk, ah)
        y_rw = layer_norm(y_rw, eps=GN_EPS).reshape(bsz, seq, RW_WIDTH) * rw_lnx_g + rw_lnx_b
        bonus = jnp.sum(rh * kh * rw_rk, axis=-1, keepdims=True) * vh
        y_rw = (y_rw + bonus.reshape(bsz, seq, RW_WIDTH)) * g

        y1 = jnp.concatenate([y_conv, y_rw], axis=-1) @ w_out
        x = layer_norm(ALPHA * x + gate1[:, None, :] * y1, ln1_g, ln1_b)

        h2 = adaln(x, shift2, scale2)
        q = (h2 @ peer_wq).reshape(bsz, seq, PEER_HEADS, PEER_QDIM).astype(jnp.float32)
        half = PEER_QDIM // 2
        s1 = jnp.einsum('bshd,hnd->bshn', q[..., :half], peer_k1.astype(jnp.float32))
        s2 = jnp.einsum('bshd,hnd->bshn', q[..., half:], peer_k2.astype(jnp.float32))
        v1, i1 = lax.top_k(s1, PEER_TOPK)
        v2, i2 = lax.top_k(s2, PEER_TOPK)
        cand = (v1[..., :, None] + v2[..., None, :]).reshape(bsz, seq, PEER_HEADS, PEER_TOPK * PEER_TOPK)
        sc, ci = lax.top_k(cand, PEER_TOPK)
        experts = (jnp.take_along_axis(i1, ci // PEER_TOPK, axis=-1) * PEER_NKEYS
                   + jnp.take_along_axis(i2, ci % PEER_TOPK, axis=-1))
        gates = jax.nn.softmax(sc, axis=-1)

        n_tok = bsz * seq
        nblk = n_tok // PEER_TOKEN_BLOCK
        hk = PEER_HEADS * PEER_TOPK
        h_blk = h2.reshape(nblk, PEER_TOKEN_BLOCK, dm)
        e_blk = experts.reshape(nblk, PEER_TOKEN_BLOCK, hk)
        g_blk = gates.reshape(nblk, PEER_TOKEN_BLOCK, hk)

        def peer_block(args):
            hb, eb, gb = args
            u_sel = jnp.take(peer_u, eb, axis=0)
            z = jnp.einsum('td,tkd->tk', hb, u_sel)
            act = jax.nn.gelu(z, approximate=False) * gb
            return jnp.einsum('tk,tkd->td', act, jnp.take(peer_v, eb, axis=0))

        y2 = lax.map(peer_block, (h_blk, e_blk, g_blk)).reshape(bsz, seq, dm)
        x = layer_norm(ALPHA * x + gate2[:, None, :] * y2, ln2_g, ln2_b)

    return x


def setup_inputs(seed=0):
    out = dict(first_inputs(seed))
    for name, value in second_inputs(seed + 1).items():
        if name != "x":
            out[name + "_2"] = value
    return out


def reference(
    x, mem, norm_gains, mem_norm_gain, w_in_ab, pool_w, pool_scale, rec_lb_logits, rec_out_gain,
    w_out_ab, w_qkv, rel_bias, w_o_att, w_mem_q, w_mem_kv, w_mem_o, w_ff1, w_ff2, c_2, cond_w_2,
    cond_b_2, w_in_2, mu_shift_2, conv_w_2, conv_b_2, conv_ln_g_2, conv_ln_b_2, rw_w0_2,
    rw_w2_2, rw_a0_2, rw_a2_2, rw_g2_2, rw_kk_2, rw_ka_2, rw_rk_2, rw_lnx_g_2, rw_lnx_b_2,
    w_out_2, ln1_g_2, ln1_b_2, peer_wq_2, peer_k1_2, peer_k2_2, peer_u_2, peer_v_2, ln2_g_2,
    ln2_b_2,
):
    x = first_block(
        x, mem, norm_gains, mem_norm_gain, w_in_ab, pool_w, pool_scale, rec_lb_logits,
        rec_out_gain, w_out_ab, w_qkv, rel_bias, w_o_att, w_mem_q, w_mem_kv, w_mem_o, w_ff1,
        w_ff2,
    )
    return second_block(
        x, c_2, cond_w_2, cond_b_2, w_in_2, mu_shift_2, conv_w_2, conv_b_2, conv_ln_g_2,
        conv_ln_b_2, rw_w0_2, rw_w2_2, rw_a0_2, rw_a2_2, rw_g2_2, rw_kk_2, rw_ka_2, rw_rk_2,
        rw_lnx_g_2, rw_lnx_b_2, w_out_2, ln1_g_2, ln1_b_2, peer_wq_2, peer_k1_2, peer_k2_2,
        peer_u_2, peer_v_2, ln2_g_2, ln2_b_2,
    )


_drawn_inputs = setup_inputs


def setup_inputs(seed=0):
    import zlib

    import numpy as np

    out = dict(_drawn_inputs(seed))
    spreads = {}
    factors = {'rel_bias': 4.647,
     'cond_b_2': 6.261,
     'mu_shift_2': 3.869,
     'conv_b_2': 8.0,
     'conv_ln_g_2': 185.244,
     'conv_ln_b_2': 200.0,
     'rw_w0_2': 44.312,
     'rw_w2_2': 64.0,
     'rw_a0_2': 8.0,
     'rw_a2_2': 5.615,
     'rw_kk_2': 64.0,
     'rw_ka_2': 6.669,
     'rw_rk_2': 8.0,
     'rw_lnx_g_2': 200.0,
     'rw_lnx_b_2': 200.0,
     'ln1_b_2': 2.817,
     'ln2_b_2': 2.786}
    for name, (base, spread) in spreads.items():
        noise = np.random.default_rng([zlib.crc32(name.encode()), seed]).standard_normal(out[name].shape)
        drawn = base * np.exp(spread * noise) if base else spread * noise
        out[name] = __import__('jax').numpy.asarray(drawn.astype(out[name].dtype))
    for name, factor in factors.items():
        out[name] = (out[name] * factor).astype(out[name].dtype)
    return out
```

```python
from contextlib import ExitStack
import math

import numpy as np
import concourse.bass as bass
import concourse.mybir as mybir
from concourse.alu_op_type import AluOpType as ALU

ACT = mybir.ActivationFunctionType
F32 = mybir.dt.float32
U32 = mybir.dt.uint32
AX = mybir.AxisListType

P = 128
T = 512
D = 1024
CT = D // P
TT = T // P
M = 256
FF = 4 * D
NORM_EPS = 1e-6
LN_EPS = 1e-5
GN_EPS = 64e-5
GATE_CLIP = 60.0
POOL_WINDOWS = (2, 4, 8, 16)
POOL_PAD = max(POOL_WINDOWS)
REC_HEADS = 4
ATT_HEADS = 16
ATT_DIM = D // ATT_HEADS
CHUNK = 64
REL_CLIP = 256
MEM_HEADS = 4
MEM_TILES = CT // MEM_HEADS
CONV_K = 31
RW_CHUNK = 64
RW_HEADS = 8
RW_TILES = 4
RW_LEVELS = (1, 2, 4, 8, 16, 32)
REC_LEVELS = (1, 2, 4, 8, 16, 32, 64)
PEER_HEADS = 8
NKEYS = 128
TOPK = 16
EXPERTS = NKEYS * NKEYS
KEYS_PER_GROUP = 8
ALPHA = 2.0 ** 0.25
MASK_VALUE = -1e30
LOWEST = -3.0e38
WCH = 512
STAGE_TOKENS = 64

COLUMNS = [
    ("norm_gains", 96), ("mem_norm_gain", 8), ("pool_scale", 4), ("rec_lb_logits", 4), ("rec_out_gain", 1),
    ("c_2", 8), ("cond_b_2", 48), ("mu_shift_2", 14), ("conv_w_2", 4 * CONV_K), ("conv_b_2", 4),
    ("conv_ln_g_2", 4), ("conv_ln_b_2", 4), ("rw_w0_2", 4), ("rw_a0_2", 4), ("rw_kk_2", 4), ("rw_ka_2", 4),
    ("rw_rk_2", 4), ("rw_lnx_g_2", 4), ("rw_lnx_b_2", 4), ("ln1_g_2", 8), ("ln1_b_2", 8), ("ln2_g_2", 8),
    ("ln2_b_2", 8),
]
COLUMN_AT = {}
for _name, _n in COLUMNS:
    COLUMN_AT[_name] = sum(n for _, n in COLUMNS[:len(COLUMN_AT)])
N_COLUMNS = sum(n for _, n in COLUMNS)


def shape_constants():
    i = np.arange(P)
    out = {"identity": np.eye(P), "ones": np.ones((P, P)), "head_ones": (i[:, None] // 64 == i[None, :] // 64)}

    def level(s, t, m):
        return (s // (2 * m) == t // (2 * m)) & (s % (2 * m) < m) & (t % (2 * m) >= m)

    s, t = i[:, None], i[None, :]
    out["rec_masks"] = np.concatenate([s == t] + [level(s, t, m) for m in REC_LEVELS], axis=1)
    s, t = (i % 64)[:, None], np.arange(64)[None, :]
    out["rw_masks"] = np.concatenate(
        [s < t, s <= t, s == t] + [level(s, t, m) for m in RW_LEVELS] + [level(t, s, m) for m in RW_LEVELS], axis=1)
    pos = np.arange(T)[None, :]
    out["keep_tile"] = np.repeat(pos % P != 0, P, axis=0)
    out["keep_chunk"] = np.repeat(pos % RW_CHUNK != 0, P, axis=0)
    out["counter"] = np.repeat(np.arange(P)[None, :], P, axis=0)
    out["pool_edge"] = np.repeat(np.concatenate(
        [w / np.minimum(np.arange(1, POOL_PAD + 1), w) for w in POOL_WINDOWS])[None, :], P, axis=0)
    return {k: np.ascontiguousarray(v.astype(np.float32)) for k, v in out.items()}


CONSTANT_WIDTHS = {k: v.shape[1] for k, v in shape_constants().items()}


def flat(marks):
    for m in marks:
        if isinstance(m, tuple) and len(m) == 2 and isinstance(m[1], int):
            yield m
        elif m is not None:
            yield from flat(m)


class Lane:

    def __init__(self, eng, sem):
        self.eng, self.sem, self.count, self.waited = eng, sem, 0, {}

    def wait(self, *marks):
        for sem, value in flat(marks):
            if self.waited.get(sem.name, 0) < value:
                self.eng.wait_ge(sem, value)
                self.waited[sem.name] = value

    def mark(self, ins):
        ins.then_inc(self.sem, 1)
        self.count += 1
        return (self.sem, self.count)

    def last(self):
        return (self.sem, self.count) if self.count else None


class Queue:

    def __init__(self, eng, lane):
        self.eng, self.lane = eng, lane

    def move(self, out, in_, port, after=()):
        self.lane.wait(*after)
        self.eng.dma_start(out, in_).then_inc(port.sem, 16)
        port.count += 16
        return (port.sem, port.count)


class Port:

    def __init__(self, sem):
        self.sem, self.count = sem, 0


class Slot:
    def __init__(self, tile, port=None):
        self.tile, self.port, self.free, self.held = tile, port, [], False

    def release(self, *marks):
        self.free, self.held = list(marks), False


class Ring:

    def __init__(self, slots):
        self.slots, self.n = slots, 0

    def take(self):
        s = self.slots[self.n % len(self.slots)]
        assert not s.held, "a ring's buffer is taken before it was released"
        self.n += 1
        s.held = True
        return s


def build(nc, dram, out, gate_table):
    ctx = ExitStack()
    with ctx:
        def sb(name, cols, dt=F32):
            return ctx.enter_context(nc.sbuf_tensor(name, [P, cols], dt))

        def sem(name):
            return ctx.enter_context(nc.semaphore(name))

        pe = Lane(nc.tensor, sem("pe_done"))
        dve = Lane(nc.vector, sem("dve_done"))
        act = Lane(nc.scalar, sem("act_done"))
        pool = Lane(nc.gpsimd, sem("pool_done"))
        sp = Lane(nc.sync, sem("sp_done"))
        weight_queue = Queue(nc.sync, sp)
        side_queue = Queue(nc.gpsimd, pool)

        x = sb("residual", CT * T)[:, :].rearrange("p (c t) -> p c t", c=CT)
        h_buf = sb("normed_or_mixed", CT * T)[:, :]
        h = h_buf.rearrange("p (c t) -> p c t", c=CT)
        y_buf = sb("branch", CT * T)[:, :]
        y = y_buf.rearrange("p (c t) -> p c t", c=CT)
        ARENA = 20480
        arena = sb("arena", ARENA)[:, :]
        columns = sb("columns", N_COLUMNS)
        const = {k: sb("const_" + k, n) for k, n in CONSTANT_WIDTHS.items()}
        tmp = Ring([Slot(sb(f"tmp{i}", T)[:, :]) for i in range(6)])
        small = Ring([Slot(sb(f"small{i}", 4)[:, :]) for i in range(8)])
        scalars = sb("scalars", 8)
        weights = Ring([Slot(sb(f"weights{i}", CT * WCH)[:, :], Port(sem(f"weights_landed{i}"))) for i in range(3)])
        psum = Ring([Slot(ctx.enter_context(nc.psum_tensor(f"bank{i}", [P, 512], F32))[:, :]) for i in range(8)])
        side_ports = [Port(sem(f"side{i}")) for i in range(12)]
        out_port = Port(sem("out_written"))

        def carve(at, n):
            assert at + n <= ARENA
            return arena[:, at:at + n]

        def col(name, i=0):
            j = COLUMN_AT[name] + i
            return columns[:, j:j + 1]

        def tt(o, a, b, op, *after):
            dve.wait(*after)
            return dve.mark(nc.vector.tensor_tensor(o, a, b, op))

        def ts(o, a, s1, s2, op0, op1, *after):
            dve.wait(*after)
            if op1 is None:
                return dve.mark(nc.vector.tensor_scalar(o, a, s1, None, op0))
            return dve.mark(nc.vector.tensor_scalar(o, a, s1, s2, op0, op1))

        def stt(o, a, s, b, op0, op1, *after):
            dve.wait(*after)
            return dve.mark(nc.vector.scalar_tensor_tensor(out=o, in0=a, scalar=s, in1=b, op0=op0, op1=op1))

        def vcopy(o, a, *after):
            dve.wait(*after)
            return dve.mark(nc.vector.tensor_copy(o, a))

        def recip(o, a, *after):
            dve.wait(*after)
            return dve.mark(nc.vector.reciprocal(o, a))

        def memset(o, value, *after):
            dve.wait(*after)
            return dve.mark(nc.vector.memset(o, value))

        def reduce(o, a, op, *after):
            dve.wait(*after)
            return dve.mark(nc.vector.tensor_reduce(o, a, AX.X, op))

        def fn(o, a, func, *after, **kw):
            act.wait(*after)
            return act.mark(nc.scalar.activation(o, a, func, **kw))

        def acopy(o, a, *after):
            act.wait(*after)
            return act.mark(nc.scalar.copy(o, a))

        def ptt(o, a, b, op, *after):
            pool.wait(*after)
            return pool.mark(nc.gpsimd.tensor_tensor(o, a, b, op))

        def mm(o, lhsT, rhs, start=True, stop=True, after=(), marked=False):
            pe.wait(*after)
            ins = nc.tensor.matmul(o, lhsT, rhs, start=start, stop=stop)
            return pe.mark(ins) if marked else None

        def turn(o, a, after=(), marked=False):
            pe.wait(*after)
            n = a.shape[0]
            ins = nc.tensor.transpose(o, a, const["identity"][0:n, 0:n])
            return pe.mark(ins) if marked else None

        def join():
            marks = [lane.last() for lane in (pe, dve, act, pool)]
            for lane in (pe, dve, act, pool):
                lane.wait(*marks)

        const_mark = []
        port = side_ports[0]
        const_mark = [side_queue.move(columns[:, :], dram["columns"], port)]
        for k in const:
            const_mark = [side_queue.move(const[k][:, :], dram[k], port)]
        x_in = side_queue.move(x, dram["x"].rearrange("(c p) t -> p c t", p=P), side_ports[1])
        for lane in (pe, dve, act, pool):
            lane.wait(const_mark)
        ones, head_ones = const["ones"][:, :], const["head_ones"][:, :]
        eps_of = {}
        for i, value in enumerate((NORM_EPS, LN_EPS, GN_EPS, 1.0)):
            m = memset(scalars[:, i:i + 1], value)
            eps_of[value] = scalars[:, i:i + 1]
        act.wait(m)
        one = eps_of[1.0]

        def load(w, k0, n0, width):
            s = weights.take()
            view = s.tile[:, 0:CT * width].rearrange("p (a n) -> p a n", a=CT)
            s.ready = weight_queue.move(view, w[k0:k0 + D, n0:n0 + width].rearrange("(a p) n -> p a n", p=P),
                                        s.port, after=s.free)
            return s, view

        def gemm(w, rhs, ready, evacuate, n_first=0, n_cols=None, n_rows=D, width_out=T):
            n_cols = w.shape[1] if n_cols is None else n_cols
            for n0 in range(n_first, n_first + n_cols, WCH):
                width = min(WCH, n_first + n_cols - n0)
                banks = [psum.take() for _ in range(width // P)]
                for kb in range(n_rows // D):
                    s, wt = load(w, kb * D, n0, width)
                    for c, bank in enumerate(banks):
                        pe.wait(s.ready, bank.free)
                        for a in range(CT):
                            k = kb * CT + a
                            pe.wait(ready[k])
                            last = k == n_rows // P - 1
                            m = mm(bank.tile[:, 0:width_out], wt[:, a, c * P:(c + 1) * P], rhs(k),
                                   start=(k == 0), stop=last, marked=(a == CT - 1))
                        bank.done = m
                    s.release(m)
                for c, bank in enumerate(banks):
                    bank.release(*evacuate((n0 - n_first) // P + c, bank.tile[:, 0:width_out], bank.done))

        def gemm_tokens(w, lhs, ready, evacuate, n_first, n_cols, n_token_tiles):
            for n0 in range(n_first, n_first + n_cols, WCH):
                s, wt = load(w, 0, n0, WCH)
                for tk in range(n_token_tiles):
                    bank = psum.take()
                    pe.wait(s.ready, bank.free)
                    for a in range(CT):
                        pe.wait(ready[a])
                        m = mm(bank.tile, lhs(a)[:, tk * P:(tk + 1) * P], wt[:, a, :],
                               start=(a == 0), stop=(a == CT - 1), marked=(a == CT - 1))
                    bank.release(*evacuate(tk, n0 - n_first, bank.tile, m))
                s.release(m)

        def into(dst, by=None):
            marks = {}

            def evacuate(c, ps, m):
                marks[c] = acopy(dst(c), ps, m) if c % 2 else vcopy(dst(c), ps, m)
                return [marks[c]]
            return evacuate, marks

        def channel_sum(tiles, ready, matrix, n):
            bank = psum.take()
            pe.wait(bank.free)
            for i, tile in enumerate(tiles):
                m = mm(bank.tile[:, 0:n], matrix, tile, start=(i == 0), stop=(i == len(tiles) - 1),
                       after=[ready[i]], marked=True)
            return bank, m

        def square_sum(tiles, ready, matrix, n):
            bank = psum.take()
            pe.wait(bank.free)
            for i, tile in enumerate(tiles):
                s = tmp.take()
                q = fn(s.tile[:, 0:n], tile, ACT.Square, s.free, ready[i])
                m = mm(bank.tile[:, 0:n], matrix, s.tile[:, 0:n], start=(i == 0), stop=(i == len(tiles) - 1),
                       after=[q], marked=True)
                s.release(m)
            return bank, m

        def inverse_root(bank, mark, count, eps, n):
            s = tmp.take()
            m = fn(s.tile[:, 0:n], bank.tile[:, 0:n], ACT.Ln, s.free, mark, scale=1.0 / count, bias=eps_of[eps])
            bank.release(m)
            m = fn(s.tile[:, 0:n], s.tile[:, 0:n], ACT.Exp, m, scale=-0.5)
            return s, m

        def rms_scale(tiles, ready, gain, outs, n=T, after=()):
            bank, m = square_sum(tiles, ready, ones, n)
            r, m = inverse_root(bank, m, len(tiles) * P, NORM_EPS, n)
            marks = [stt(o, t, gain(i), r.tile[:, 0:n], ALU.mult, ALU.mult, m, after)
                     for i, (t, o) in enumerate(zip(tiles, outs))]
            r.release(marks[-1])
            return marks

        def center(tiles, ready, matrix, count, outs):
            bank, m = channel_sum(tiles, ready, matrix, T)
            marks = [stt(o, bank.tile, -1.0 / count, t, ALU.mult, ALU.add, m) for t, o in zip(tiles, outs)]
            bank.release(marks[-1])
            return marks

        def add_branch(l, n, y_marks, x_marks):
            tiles = [y[:, c, :] for c in range(CT)]
            normed = rms_scale(tiles, y_marks, lambda i: col("norm_gains", (6 * l + n) * CT + i), tiles)
            return [tt(x[:, c, :], x[:, c, :], tiles[c], ALU.add, normed[c], x_marks[c]) for c in range(CT)]

        def pre_norm(l, n, x_marks):
            return rms_scale([x[:, c, :] for c in range(CT)], x_marks,
                             lambda i: col("norm_gains", (6 * l + n) * CT + i), [h[:, c, :] for c in range(CT)])

        def h_tile(k):
            return h[:, k, :]

        def softmax(src, out_ap, scale, *after):
            s = small.take()
            mx, total = s.tile[:, 0:1], s.tile[:, 1:2]
            m = reduce(mx, src, ALU.max, s.free, after)
            m = ts(mx, mx, -scale, None, ALU.mult, None, m)
            m = fn(out_ap, src, ACT.Exp, m, after, scale=scale, bias=mx, accum_out=total)
            exp_mark = m
            m = recip(total, total, m)
            m = ts(out_ap, out_ap, total, None, ALU.mult, None, m)
            s.release(m)
            return m, exp_mark

        MEM_AT = 18432
        mem_n = carve(MEM_AT, CT * M).rearrange("p (c t) -> p c t", c=CT)

        def memory_attention(l, x_marks):
            h_marks = pre_norm(l, 2, x_marks)
            join()
            q = carve(0, CT * T).rearrange("p (c t) -> p c t", c=CT)
            k = carve(4096, CT * M).rearrange("p (c t) -> p c t", c=CT)
            v = carve(6144, 2 * D).rearrange("p (m c) -> p m c", m=2)
            probs = Ring([Slot(carve(8192 + i * M, M)) for i in range(4)])
            turned = Ring([Slot(carve(9216 + i * 2 * T, 2 * T).rearrange("p (m t) -> p m t", m=2)) for i in range(2)])
            put_k, k_marks = into(lambda c: k[:, c, :])
            gemm(dram["w_mem_kv"][l], lambda a: mem_n[:, a, :], [None] * CT, put_k, 0, D, width_out=M)
            v_marks = []

            def put_v(tk, n0, ps, m):
                v_marks.append(acopy(v[:, tk, n0:n0 + WCH], ps, m))
                return [v_marks[-1]]
            gemm_tokens(dram["w_mem_kv"][l], lambda a: mem_n[:, a, :], [None] * CT, put_v, D, D, M // P)
            put_q, q_marks = into(lambda c: q[:, c, :])
            gemm(dram["w_mem_q"][l], h_tile, h_marks, put_q)
            q_read = pe.last()
            mixed = {}
            for hd in range(MEM_HEADS):
                pt = turned.take()
                banks = [psum.take() for _ in range(2)]
                turned_marks = []
                for tq in range(TT):
                    sc = psum.take()
                    pe.wait(sc.free)
                    for j in range(MEM_TILES):
                        c = hd * MEM_TILES + j
                        m = mm(sc.tile[:, 0:M], q[:, c, tq * P:(tq + 1) * P], k[:, c, :], start=(j == 0),
                               stop=(j == MEM_TILES - 1), after=[q_marks[c], k_marks[c]], marked=True)
                    pr = probs.take()
                    m, read = softmax(sc.tile[:, 0:M], pr.tile, (D // MEM_HEADS) ** -0.5, m, pr.free)
                    sc.release(read)
                    for mt in range(2):
                        t_mark = turn(banks[mt].tile[:, tq * P:(tq + 1) * P], pr.tile[:, mt * P:(mt + 1) * P],
                                      after=[m, banks[mt].free], marked=True)
                    pr.release(t_mark)
                for mt in range(2):
                    cp = acopy(pt.tile[:, mt, :], banks[mt].tile, t_mark, pt.free)
                    banks[mt].release(cp)
                    turned_marks.append(cp)
                for j in range(MEM_TILES):
                    c = hd * MEM_TILES + j
                    o = psum.take()
                    pe.wait(o.free, turned_marks, v_marks)
                    for mt in range(2):
                        m = mm(o.tile, v[:, mt, c * P:(c + 1) * P], pt.tile[:, mt, :], start=(mt == 0),
                               stop=(mt == 1), marked=True)
                    mixed[c] = vcopy(h[:, c, :], o.tile, m, q_read)
                    o.release(mixed[c])
                pt.release(m)
            put_y, y_marks = into(lambda c: y[:, c, :])
            gemm(dram["w_mem_o"][l], h_tile, mixed, put_y)
            return add_branch(l, 3, y_marks, x_marks)

        def mlp(l, x_marks):
            h_marks = pre_norm(l, 4, x_marks)
            join()
            hidden = carve(0, FF // P * T).rearrange("p (c t) -> p c t", c=FF // P)
            hid = {}

            def put(c, ps, m):
                s = tmp.take()
                m = fn(s.tile, ps, ACT.Relu, m, s.free)
                hid[c] = tt(hidden[:, c, :], s.tile, s.tile, ALU.mult, m)
                s.release(hid[c])
                return [m]
            gemm(dram["w_ff1"][l], h_tile, h_marks, put)
            put_y, y_marks = into(lambda c: y[:, c, :])
            gemm(dram["w_ff2"][l], lambda k: hidden[:, k, :], hid, put_y, n_rows=FF)
            return add_branch(l, 5, y_marks, x_marks)

        def even_mixer(x_marks):
            h_marks = pre_norm(0, 0, x_marks)
            join()
            upad = carve(0, 4 * (POOL_PAD + T)).rearrange("p (g t) -> p g t", g=4)
            at = 4 * (POOL_PAD + T)
            q, k, b, v, gate = [carve(at + i * 4 * T, 4 * T).rearrange("p (g t) -> p g t", g=4) for i in range(5)]
            at += 5 * 4 * T
            win = [carve(at + i * (POOL_PAD + T), POOL_PAD + T) for i in range(2)]
            lb = carve(at + 4 * T, 8)
            u_marks = {}
            pad = memset(upad[:, :, 0:POOL_PAD], 0.0)
            w = dram["w_in_ab"]

            def put_u(c, ps, m):
                u_marks[c] = vcopy(upad[:, c, POOL_PAD:], ps, m)
                return [u_marks[c]]
            gemm(w, h_tile, h_marks, put_u, 0, 512)
            put_q, q_marks = into(lambda c: q[:, c, :])
            gemm(w, h_tile, h_marks, put_q, 512, 512)
            logit = columns[:, COLUMN_AT["rec_lb_logits"]:COLUMN_AT["rec_lb_logits"] + 4]
            m = tt(lb[:, 0:4], logit, logit, ALU.subtract)
            m = fn(lb[:, 0:4], lb[:, 0:4], ACT.Exp, m)
            m2 = recip(lb[:, 4:8], lb[:, 0:4], m)
            m = tt(lb[:, 0:4], lb[:, 0:4], lb[:, 4:8], ALU.mult, m2)
            m = tt(lb[:, 0:4], lb[:, 0:4], lb[:, 0:4], ALU.subtract, m)
            m = ts(lb[:, 0:4], lb[:, 0:4], 0.0, 1.0, ALU.max, ALU.min, m)
            lb_mark = ts(lb[:, 4:8], lb[:, 0:4], -1.0, 1.0, ALU.mult, ALU.add, m)
            b_marks, k_marks = {}, {}

            def put_f(c, ps, m):
                f, e, g = tmp.take(), tmp.take(), tmp.take()
                fm = ts(f.tile, ps, GATE_CLIP, -GATE_CLIP, ALU.min, ALU.max, m, f.free)
                km = fn(k[:, c, :], f.tile, ACT.Sigmoid, fm, scale=-1.0)
                k_marks[c] = ts(k[:, c, :], k[:, c, :], lb[:, 4 + c:5 + c], None, ALU.mult, None, km, lb_mark)
                em = fn(e.tile, f.tile, ACT.Abs, e.free, fm)
                em = fn(e.tile, e.tile, ACT.Exp, em, scale=-1.0)
                em = fn(e.tile, e.tile, ACT.Ln, em, bias=one)
                gm = fn(g.tile, f.tile, ACT.Exp, g.free, fm, scale=-1.0)
                gm = fn(g.tile, g.tile, ACT.Ln, gm, lb_mark, scale=lb[:, c:c + 1], bias=one)
                em = stt(e.tile, f.tile, 0.0, e.tile, ALU.min, ALU.subtract, em)
                em = tt(e.tile, e.tile, g.tile, ALU.add, em, gm)
                dve.wait(em)
                b_marks[c] = dve.mark(nc.vector.tensor_tensor_scan(
                    out=b[:, c, :], data0=const["keep_tile"][:, :], data1=e.tile, initial=0.0,
                    op0=ALU.mult, op1=ALU.add))
                f.release(em, km, gm)
                e.release(b_marks[c])
                g.release(em)
                return [fm]
            gemm(w, h_tile, h_marks, put_f, 1024, 512)
            v_marks = {}

            def put_v(tk, n0, ps, m):
                v_marks[tk] = acopy(v[:, tk, :], ps, m)
                return [v_marks[tk]]
            gemm_tokens(w, h_tile, h_marks, put_v, 1536, 512, TT)
            gate_marks = {}

            def put_g(c, ps, m):
                s = tmp.take()
                sm = fn(s.tile, ps, ACT.Sigmoid, m, s.free)
                gate_marks[c] = tt(gate[:, c, :], s.tile, ps, ALU.mult, sm)
                s.release(gate_marks[c])
                return [gate_marks[c]]
            gemm(w, h_tile, h_marks, put_g, 2048, 512)
            h_read = pe.last()
            mixed = {}
            pool_w = tmp.take()
            pw_mark = side_queue.move(pool_w.tile.rearrange("p (g d) -> p g d", g=4),
                                      dram["pool_w"].rearrange("g c d -> c g d"), side_ports[2], after=pool_w.free)
            for g, wdw in enumerate(POOL_WINDOWS):
                src, m = upad[:, g, :], [u_marks[g], pad]
                shift, n = 1, 0
                while shift < wdw:
                    dst = win[n % 2]
                    m1 = vcopy(dst[:, 0:shift], src[:, 0:shift], m)
                    m = tt(dst[:, shift:], src[:, shift:], src[:, 0:POOL_PAD + T - shift], ALU.add, m)
                    m = [m, m1]
                    src, shift, n = dst, 2 * shift, n + 1
                s = tmp.take()
                m = ts(s.tile, src[:, POOL_PAD:], 1.0 / wdw, None, ALU.mult, None, m, s.free)
                m = tt(s.tile[:, 0:POOL_PAD], s.tile[:, 0:POOL_PAD],
                       const["pool_edge"][:, g * POOL_PAD:(g + 1) * POOL_PAD], ALU.mult, m)
                m = tt(s.tile, s.tile, upad[:, g, POOL_PAD:], ALU.subtract, m)
                o = psum.take()
                m = mm(o.tile, pool_w.tile[:, g * P:(g + 1) * P], s.tile, after=[m, o.free, pw_mark], marked=True)
                s.release(m)
                mixed[g] = fn(h[:, g, :], o.tile, ACT.Identity, m, h_read, scale=col("pool_scale", g))
                o.release(mixed[g])
            pool_w.release(m)
            join()
            at2 = at
            qd, sT, acc0, acc1 = [carve(at2 + i * T, T) for i in range(4)]
            state = [carve(0 + i * P, P) for i in range(2)]
            kT = carve(2 * P, T)
            kd = carve(2 * P + T, T)
            lead = carve(2 * P + 2 * T, T)
            head_read = []
            for hd in range(REC_HEADS):
                bh, qh, kh = b[:, hd, :], q[:, hd, :], k[:, hd, :]
                e_mark = fn(lead, bh, ACT.Exp, head_read)
                qd_mark = tt(qd, qh, lead, ALU.mult, e_mark, head_read)
                s = tmp.take()
                b3 = bh.rearrange("p (n t) -> p n t", t=P)
                m = tt(s.tile.rearrange("p (n t) -> p n t", t=P), b3[:, :, P - 1:P].to_broadcast([P, TT, P]), b3,
                       ALU.subtract, s.free)
                m = fn(s.tile, s.tile, ACT.Exp, m)
                kd_mark = tt(kd, kh, s.tile, ALU.mult, m, head_read)
                s.release(kd_mark)
                bank = psum.take()
                for tk in range(TT):
                    m = turn(bank.tile[:, tk * P:(tk + 1) * P], kd[:, tk * P:(tk + 1) * P],
                             after=[kd_mark, bank.free], marked=True)
                kT_mark = acopy(kT, bank.tile, m, head_read)
                bank.release(kT_mark)
                acc_mark = None
                for lv, half in enumerate((0,) + REC_LEVELS):
                    bank = psum.take()
                    if half:
                        s, s2 = tmp.take(), tmp.take()
                        n = T // (2 * half)
                        bl = bh.rearrange("p (n t) -> p n t", t=2 * half)
                        m = tt(s.tile.rearrange("p (n t) -> p n t", t=2 * half), bl,
                               bl[:, :, half - 1:half].to_broadcast([P, n, 2 * half]), ALU.subtract, s.free)
                        m = fn(s.tile, s.tile, ACT.Abs, m)
                        m = fn(s.tile, s.tile, ACT.Exp, m, scale=-1.0)
                        qm = ptt(s2.tile, qh, s.tile, ALU.mult, m, s2.free)
                        km = tt(s.tile, kh, s.tile, ALU.mult, m, qm)
                        ql, kl, marks = s2.tile, s.tile, [qm, km]
                    else:
                        ql, kl, marks = qh, kh, []
                    for tk in range(TT):
                        m = mm(bank.tile[:, tk * P:(tk + 1) * P], kl[:, tk * P:(tk + 1) * P],
                               ql[:, tk * P:(tk + 1) * P], after=[marks, bank.free], marked=True)
                    if half:
                        s.release(m)
                        s2.release(m)
                    mask = const["rec_masks"][:, lv * P:(lv + 1) * P]
                    mask = mask.rearrange("p (o t) -> p o t", o=1).to_broadcast([P, TT, P])
                    ps3 = bank.tile.rearrange("p (n t) -> p n t", t=P)
                    dst = sT if lv == 0 else acc0
                    m = tt(dst.rearrange("p (n t) -> p n t", t=P), ps3, mask, ALU.mult, m, head_read, acc_mark)
                    bank.release(m)
                    acc_mark = m if lv == 0 else tt(sT, sT, acc0, ALU.add, m)
                o = psum.take()
                st_mark = None
                for tk in range(TT):
                    cur = slice(tk * P, (tk + 1) * P)
                    vh = v[:, tk, hd * P:(hd + 1) * P]
                    m = mm(o.tile[:, cur], vh, sT[:, cur], start=True, stop=(tk == 0),
                           after=[acc_mark, o.free], marked=True)
                    if tk:
                        m = mm(o.tile[:, cur], state[(tk - 1) % 2], qd[:, cur], start=False, stop=True,
                               after=[st_mark, qd_mark], marked=True)
                    o_read = m
                    if tk < TT - 1:
                        u = psum.take()
                        m = mm(u.tile[:, 0:P], kT[:, cur], vh, after=[kT_mark, u.free], marked=True)
                        if tk == 0:
                            st_mark = vcopy(state[0], u.tile[:, 0:P], m)
                        else:
                            st_mark = stt(state[tk % 2], state[(tk - 1) % 2], lead[:, (tk + 1) * P - 1:(tk + 1) * P],
                                          u.tile[:, 0:P], ALU.mult, ALU.add, m, st_mark, o_read)
                        u.release(st_mark)
                s = tmp.take()
                cp = vcopy(s.tile, o.tile, o_read, s.free)
                o.release(cp)
                head_read = [o_read, st_mark]
                bank, m = square_sum([s.tile], [cp], ones, T)
                r, m = inverse_root(bank, m, P, NORM_EPS, T)
                m = stt(s.tile, s.tile, col("rec_out_gain"), r.tile, ALU.mult, ALU.mult, m)
                r.release(m)
                mixed[4 + hd] = tt(h[:, 4 + hd, :], s.tile, gate[:, hd, :], ALU.mult, m)
                s.release(mixed[4 + hd])
            put_y, y_marks = into(lambda c: y[:, c, :])
            gemm(dram["w_out_ab"], h_tile, mixed, put_y)
            return add_branch(0, 1, y_marks, x_marks)

        def odd_mixer(x_marks):
            h_marks = pre_norm(1, 0, x_marks)
            join()
            q, k = [carve(i * 4096, 4096).rearrange("p (c t) -> p c t", c=CT) for i in range(2)]
            v = carve(8192, 4096).rearrange("p (n c) -> p n c", n=TT)
            bias = Ring([Slot(carve(12288 + i * T, T), side_ports[3 + i]) for i in range(2)])
            turned = Ring([Slot(carve(13312 + i * 4 * T, 4 * T).rearrange("p (j t) -> p j t", j=TT)) for i in range(2)])
            probs = Ring([Slot(carve(17408 + i * T, T)) for i in range(2)])
            w = dram["w_qkv"]
            put_q, q_marks = into(lambda c: q[:, c, :])
            gemm(w, h_tile, h_marks, put_q, 0, D)
            put_k, k_marks = into(lambda c: k[:, c, :])
            gemm(w, h_tile, h_marks, put_k, D, D)
            v_marks = []

            def put_v(tk, n0, ps, m):
                v_marks.append(acopy(v[:, tk, n0:n0 + WCH], ps, m))
                return [v_marks[-1]]
            gemm_tokens(w, h_tile, h_marks, put_v, 2 * D, D, TT)
            h_read = pe.last()
            mixed = {}
            for hd in range(ATT_HEADS):
                c, half = hd // 2, slice(64 * (hd % 2), 64 * (hd % 2) + 64)
                bs = bias.take()
                bm = side_queue.move(bs.tile, dram["rel_bias"][hd], bs.port, after=bs.free)
                bm = [bm, memset(bs.tile[0:CHUNK, T - CHUNK:T], MASK_VALUE, bm)]
                pt = turned.take()
                tbanks = [psum.take() for _ in range(TT)]
                for tq in range(TT):
                    n = (tq + 1) * P
                    sc = psum.take()
                    m = mm(sc.tile[:, 0:n], q[half, c, tq * P:(tq + 1) * P], k[half, c, 0:n],
                           after=[q_marks[c], k_marks[c], sc.free], marked=True)
                    pr = probs.take()
                    m = stt(pr.tile[:, 0:n], sc.tile[:, 0:n], ATT_DIM ** -0.5, bs.tile[:, T - n:T],
                            ALU.mult, ALU.add, m, bm, pr.free)
                    sc.release(m)
                    m, _ = softmax(pr.tile[:, 0:n], pr.tile[:, 0:n], 1.0, m)
                    for j in range(tq + 1):
                        t_mark = turn(tbanks[j].tile[:, tq * P:(tq + 1) * P], pr.tile[:, j * P:(j + 1) * P],
                                      after=[m, tbanks[j].free], marked=True)
                    pr.release(t_mark)
                bs.release(dve.last())
                cps = []
                for j in range(TT):
                    lane_copy = acopy if j % 2 else vcopy
                    cps.append(lane_copy(pt.tile[:, j, j * P:T], tbanks[j].tile[:, j * P:T], t_mark, pt.free))
                    tbanks[j].release(cps[-1])
                o = psum.take()
                for j in range(TT):
                    m = mm(o.tile[0:64, j * P:T], v[:, j, hd * 64:(hd + 1) * 64], pt.tile[:, j, j * P:T],
                           start=(j == 0), stop=(j == TT - 1), after=[cps[j], o.free, v_marks], marked=True)
                mixed[hd] = acopy(h[half, c, :], o.tile[0:64, :], m, h_read)
                o.release(mixed[hd])
                pt.release(m)
            put_y, y_marks = into(lambda c: y[:, c, :])
            gemm(dram["w_o_att"], h_tile, [[mixed[2 * c], mixed[2 * c + 1]] for c in range(CT)], put_y)
            return add_branch(1, 1, y_marks, x_marks)

        mod = sb("modulation", 48)
        scale_1 = sb("one_plus_scale", 16)

        def modulation():
            s, g = tmp.take(), tmp.take()
            c_in = columns[:, COLUMN_AT["c_2"]:COLUMN_AT["c_2"] + CT]
            m = fn(s.tile[:, 0:CT], c_in, ACT.Sigmoid, s.free)
            m = tt(g.tile[:, 0:CT], s.tile[:, 0:CT], c_in, ALU.mult, m, g.free)
            s.release(m)
            bank = psum.take()
            pe.wait(m, bank.free)
            for n0 in range(0, 6 * D, WCH):
                ws, wt = load(dram["cond_w"], 0, n0, WCH)
                pe.wait(ws.ready)
                for c in range(4):
                    j = n0 // P + c
                    for a in range(CT):
                        last = mm(bank.tile[:, j:j + 1], wt[:, a, c * P:(c + 1) * P], g.tile[:, a:a + 1],
                                  start=(a == 0), stop=(a == CT - 1), marked=(c == 3 and a == CT - 1))
                ws.release(last)
            g.release(last)
            m = tt(mod[:, :], bank.tile[:, 0:48], columns[:, COLUMN_AT["cond_b_2"]:COLUMN_AT["cond_b_2"] + 48],
                   ALU.add, last)
            bank.release(m)
            ts(scale_1[:, 0:8], mod[:, 8:16], 1.0, None, ALU.add, None, m)
            return ts(scale_1[:, 8:16], mod[:, 32:40], 1.0, None, ALU.add, None, m)

        def ada_norm(x_marks, which, mod_mark):
            xs, hs = [x[:, c, :] for c in range(CT)], [h[:, c, :] for c in range(CT)]
            cm = center(xs, x_marks, ones, D, hs)
            bank, m = square_sum(hs, cm, ones, T)
            r, m = inverse_root(bank, m, D, LN_EPS, T)
            marks = []
            for c in range(CT):
                m2 = stt(hs[c], hs[c], scale_1[:, 8 * which + c:8 * which + c + 1], r.tile, ALU.mult, ALU.mult,
                         m, mod_mark)
                marks.append(fn(hs[c], hs[c], ACT.Identity, m2, bias=mod[:, 24 * which + c:24 * which + c + 1]))
            r.release(m2)
            return marks

        def close_block(x_marks, y_marks, which, gain, shift, mod_mark):
            xs, ys = [x[:, c, :] for c in range(CT)], [y[:, c, :] for c in range(CT)]
            marks = []
            for c in range(CT):
                g = mod[:, 24 * which + 16 + c:24 * which + 17 + c]
                m = ts(ys[c], ys[c], g, None, ALU.mult, None, y_marks[c], mod_mark)
                marks.append(stt(xs[c], xs[c], ALPHA, ys[c], ALU.mult, ALU.add, m, x_marks[c]))
            cm = center(xs, marks, ones, D, xs)
            bank, m = square_sum(xs, cm, ones, T)
            r, m = inverse_root(bank, m, D, LN_EPS, T)
            out_marks = []
            for c in range(CT):
                m2 = stt(xs[c], xs[c], col(gain, c), r.tile, ALU.mult, ALU.mult, m)
                out_marks.append(fn(xs[c], xs[c], ACT.Identity, m2, bias=col(shift, c)))
            r.release(m2)
            return out_marks

        def rw_mixer(h_marks):
            join()
            NPT = 14
            p = carve(0, NPT * (T + 1)).rearrange("p (c t) -> p c t", c=NPT)
            at = NPT * (T + 1)
            CP = CONV_K - 1
            upad = carve(at, 4 * (CP + T)).rearrange("p (c t) -> p c t", c=4)
            conv = carve(at + 4 * (CP + T), 4 * T).rearrange("p (c t) -> p c t", c=4)
            pad = [memset(upad[:, :, 0:CP], 0.0), memset(p[:, :, 0:1], 0.0)]
            w = dram["w_in"]
            a_marks, u_marks = {}, {}

            def put_a(c, ps, m):
                a_marks[c] = vcopy(upad[:, c, CP:], ps, m)
                return [a_marks[c]]
            gemm(w, h_tile, h_marks, put_a, 0, 512)

            def put_b(c, ps, m):
                s = tmp.take()
                m = fn(s.tile, ps, ACT.Sigmoid, m, s.free)
                u_marks[c] = tt(upad[:, c, CP:], upad[:, c, CP:], s.tile, ALU.mult, m, a_marks[c])
                s.release(u_marks[c])
                return [m]
            gemm(w, h_tile, h_marks, put_b, 512, 512)
            p_marks = {}

            def put_p(c, ps, m):
                p_marks[c] = acopy(p[:, c, 1:], ps, m)
                return [p_marks[c]]
            gemm(w, h_tile, h_marks, put_p, 1024, 1792)
            h_read = pe.last()
            mixed = {}
            mixed_p = {}
            for c in range(NPT):
                s = tmp.take()
                m = tt(s.tile, p[:, c, 0:T], p[:, c, 1:], ALU.subtract, p_marks[c], pad, s.free)
                mixed_p[c] = stt(p[:, c, 1:], s.tile, col("mu_shift_2", c), p[:, c, 1:], ALU.mult, ALU.add, m)
                s.release(mixed_p[c])
            cv = [None] * 4
            for tap_i in range(CONV_K):
                for c in range(4):
                    src = upad[:, c, tap_i:tap_i + T]
                    wc = col("conv_w_2", tap_i * 4 + c)
                    if tap_i == 0:
                        cv[c] = ts(conv[:, c, :], src, wc, col("conv_b_2", c), ALU.mult, ALU.add, u_marks[c], pad)
                    else:
                        cv[c] = stt(conv[:, c, :], src, wc, conv[:, c, :], ALU.mult, ALU.add, cv[c])
            cs = [conv[:, c, :] for c in range(4)]
            cv = center(cs, cv, ones, 512, cs)
            bank, m = square_sum(cs, cv, ones, T)
            r, m = inverse_root(bank, m, 512, LN_EPS, T)
            for c in range(4):
                m2 = stt(cs[c], cs[c], col("conv_ln_g_2", c), r.tile, ALU.mult, ALU.mult, m)
                m2 = ts(cs[c], cs[c], col("conv_ln_b_2", c), None, ALU.add, None, m2)
                s = tmp.take()
                m3 = fn(s.tile, cs[c], ACT.Sigmoid, m2, s.free)
                mixed[c] = tt(h[:, c, :], cs[c], s.tile, ALU.mult, m3, h_read)
                s.release(mixed[c])
            r.release(m2)
            join()

            lora, g2 = carve(18500, T), carve(18500 + T, T)
            lm = [side_queue.move(lora, dram["lora"], side_ports[5]), side_queue.move(g2, dram["rw_g2"], side_ports[6])]
            r_t, k_t, v_t = [[p[:, 4 * i + c, 1:] for c in range(4)] for i in range(3)]
            wd, ad, gd = p[0:64, 12, 1:], p[64:128, 12, 1:], p[:, 13, 1:]
            wm = fn(wd, wd, ACT.Tanh, mixed_p[12])
            gm = fn(gd, gd, ACT.Sigmoid, mixed_p[13])
            a_hat = carve(at, 4 * T).rearrange("p (c t) -> p c t", c=4)
            tok = carve(at + 4 * T, 3 * 4 * T).rearrange("p (k n c) -> p k n c", k=3, n=TT)
            v_tok, k_tok, b_tok = tok[:, 0], tok[:, 1], tok[:, 2]
            inv_at = at + 4 * 4 * T
            slot_a, slot_b = weights.take(), weights.take()
            for lane in (dve, act):
                lane.wait(slot_a.free, slot_b.free)
            kinds = [s.tile[:, i * 4 * T:(i + 1) * 4 * T].rearrange("p (c n) -> p c n", c=4)
                     for s in (slot_a, slot_b) for i in range(2)]
            M_T, RK_T, RB_T, Y = kinds
            gate = y_buf[:, 0:4 * T].rearrange("p (c t) -> p c t", c=4)
            bonus = y_buf[:, 4 * T:8 * T].rearrange("p (c t) -> p c t", c=4)
            end_decay = sb("chunk_decay", 4 * T // RW_CHUNK)
            n_ch = T // RW_CHUNK
            ready = {}
            for c in range(4):
                cs_ = slice(c * P, (c + 1) * P)
                lw, kk, aa = [tmp.take() for _ in range(3)]
                bank = psum.take()
                m = mm(bank.tile, lora[0:64, cs_], wd, after=[lm, wm, bank.free], marked=True)
                m = fn(lw.tile, bank.tile, ACT.Sigmoid, m, lw.free, bias=col("rw_w0_2", c))
                bank.release(m)
                lw_mark = ts(lw.tile, lw.tile, -math.exp(-0.5), None, ALU.mult, None, m)
                bank = psum.take()
                m = mm(bank.tile, lora[64:128, cs_], ad, after=[lm, mixed_p[12], bank.free], marked=True)
                a_mark = fn(aa.tile, bank.tile, ACT.Sigmoid, m, aa.free, bias=col("rw_a0_2", c))
                bank.release(a_mark)
                bank = psum.take()
                m = mm(bank.tile, g2[:, cs_], gd, after=[lm, gm, bank.free], marked=True)
                g_mark = acopy(gate[:, c, :], bank.tile, m)
                bank.release(g_mark)
                m = ts(kk.tile, k_t[c], col("rw_kk_2", c), None, ALU.mult, None, mixed_p[4 + c], kk.free)
                bank, sm = square_sum([kk.tile], [m], head_ones, T)
                nrm = tmp.take()
                m = fn(nrm.tile, bank.tile, ACT.Sqrt, sm, nrm.free)
                bank.release(m)
                m = ts(nrm.tile, nrm.tile, 1e-12, None, ALU.max, None, m)
                m = recip(nrm.tile, nrm.tile, m)
                kk_mark = tt(kk.tile, kk.tile, nrm.tile, ALU.mult, m)
                m = ts(nrm.tile, aa.tile, 1.0, col("rw_ka_2", c), ALU.subtract, ALU.mult, kk_mark, a_mark)
                k_mark = stt(k_t[c], nrm.tile, 1.0, k_t[c], ALU.add, ALU.mult, m)
                m = stt(nrm.tile, r_t[c], col("rw_rk_2", c), k_t[c], ALU.mult, ALU.mult, k_mark, mixed_p[c])
                bank, m = channel_sum([nrm.tile], [m], head_ones, T)
                bonus_mark = tt(bonus[:, c, :], bank.tile, v_t[c], ALU.mult, m, mixed_p[8 + c])
                bank.release(bonus_mark)
                bank = psum.take()
                for tk in range(TT):
                    m = turn(bank.tile[:, tk * P:(tk + 1) * P], v_t[c][:, tk * P:(tk + 1) * P],
                             after=[mixed_p[8 + c], bank.free], marked=True)
                v_read = m
                v_mark = acopy(v_tok[:, :, cs_], bank.tile.rearrange("p (n c) -> p n c", n=TT), m)
                bank.release(v_mark)
                total = tmp.take()
                dve.wait(lw_mark, total.free)
                m = dve.mark(nc.vector.tensor_tensor_scan(
                    out=total.tile, data0=const["keep_chunk"][:, :], data1=lw.tile, initial=0.0,
                    op0=ALU.mult, op1=ALU.add))
                m1 = tt(lw.tile, total.tile, lw.tile, ALU.subtract, m)
                before = fn(lw.tile, lw.tile, ACT.Exp, m1)
                pm = fn(nrm.tile, total.tile, ACT.Exp, m, bonus_mark)
                ahat_mark = tt(a_hat[:, c, :], kk.tile, lw.tile, ALU.mult, before, kk_mark)
                r_mark = tt(r_t[c], r_t[c], nrm.tile, ALU.mult, pm, bonus_mark)
                ed_mark = vcopy(end_decay[:, c * n_ch:(c + 1) * n_ch],
                                nrm.tile.rearrange("p (n t) -> p n t", t=RW_CHUNK)[:, :, RW_CHUNK - 1], pm)
                im = fn(total.tile, total.tile, ACT.Exp, m1, pm, scale=-1.0)
                khat_mark = tt(k_t[c], k_t[c], total.tile, ALU.mult, im)
                m = stt(aa.tile, kk.tile, -1.0, aa.tile, ALU.mult, ALU.mult, a_mark, kk_mark)
                b_mark = tt(v_t[c], aa.tile, total.tile, ALU.mult, m, im, v_read, bonus_mark)
                lw.release(ahat_mark)
                kk.release(m)
                aa.release(b_mark)
                total.release(b_mark)
                nrm.release(ed_mark)
                for src, dst, mk in ((k_t[c], k_tok, khat_mark), (v_t[c], b_tok, b_mark)):
                    bank = psum.take()
                    for tk in range(TT):
                        m = turn(bank.tile[:, tk * P:(tk + 1) * P], src[:, tk * P:(tk + 1) * P],
                                 after=[mk, bank.free], marked=True)
                    m = acopy(dst[:, :, cs_], bank.tile.rearrange("p (n c) -> p n c", n=TT), m)
                    bank.release(m)
                ready[c] = [ahat_mark, khat_mark, b_mark, r_mark]
            b_hat = v_t
            rm = const["rw_masks"][:, :].rearrange("p (k t) -> p k t", t=64)

            def wide(mask):
                return rm[:, mask:mask + 1, :].to_broadcast([P, 8, 64])

            def blocks(ap):
                return ap.rearrange("p (n t) -> p n t", t=64)

            def each():
                for hh in range(2):
                    for ch in range(n_ch):
                        yield hh, ch, slice(64 * (ch % 2), 64 * (ch % 2) + 64), \
                            slice((hh * TT + ch // 2) * 64, (hh * TT + ch // 2) * 64 + 64)

            def gram(rows, cols_, c, evacuate):
                marks = []
                for hh in range(2):
                    bank = psum.take()
                    pe.wait(bank.free, ready[c])
                    hs_ = slice(64 * hh, 64 * hh + 64)
                    for ch in range(n_ch):
                        part, cc = slice(64 * (ch % 2), 64 * (ch % 2) + 64), slice(ch // 2 * 64, ch // 2 * 64 + 64)
                        tsl = slice(ch * 64, ch * 64 + 64)
                        m = mm(bank.tile[part, cc], rows[hs_, tsl], cols_[hs_, tsl], marked=(ch == n_ch - 1))
                    marks.append(evacuate(slice(hh * 4 * 64, (hh + 1) * 4 * 64), bank.tile[:, 0:256], m))
                    bank.release(marks[-1])
                return marks

            def small_products(lhs, rhs, *after):
                bank = psum.take()
                pe.wait(bank.free, *after)
                for hh, ch, part, cc in each():
                    m = mm(bank.tile[part, cc], lhs[part, cc], rhs(part, cc, hh, ch // 2),
                           marked=(hh == 1 and ch == n_ch - 1))
                return bank, m

            def plain(ap):
                return lambda part, cc, hh, tk: ap[part, cc]

            y_inv = {}
            kept = {}
            for c in range(4):
                for rows, cols_, mask, dst in ((k_t[c], a_hat[:, c, :], 0, M_T), (k_t[c], r_t[c], 1, RK_T),
                                               (b_hat[c], r_t[c], 1, RB_T)):
                    tri = rm[:, mask:mask + 1, :].to_broadcast([P, 4, 64])
                    gram(rows, cols_, c, lambda cc, ps, m: tt(blocks(dst[:, c, cc]), blocks(ps), tri, ALU.mult, m))
            for pair in range(2):
                n_, l_, x_ = [[carve(inv_at + (k3 * 2 + i) * T, T) for i in range(2)] for k3 in range(3)]
                xm, nm, lm_, ym = {}, {}, {}, {}
                for i in range(2):
                    c = 2 * pair + i
                    nm[i] = gram(b_hat[c], a_hat[:, c, :], c,
                                 lambda cc, ps, m: acopy(n_[i][:, cc], ps, m, kept.get(i)))
                    lm_[i] = gram(a_hat[:, c, :], b_hat[c], c,
                                  lambda cc, ps, m: acopy(l_[i][:, cc], ps, m, kept.get(i)))
                    m = tt(blocks(Y[:, c, :]), blocks(n_[i]), wide(3), ALU.mult, nm[i])
                    ym[i] = tt(blocks(Y[:, c, :]), blocks(Y[:, c, :]), wide(2), ALU.add, m)
                    m = tt(blocks(x_[i]), blocks(l_[i]), wide(3 + len(RW_LEVELS)), ALU.mult, lm_[i])
                    xm[i] = tt(blocks(x_[i]), blocks(x_[i]), wide(2), ALU.add, m)
                for lv in range(1, len(RW_LEVELS)):
                    for i in range(2):
                        c = 2 * pair + i
                        s1, s2 = tmp.take(), tmp.take()
                        m1 = tt(blocks(s1.tile), blocks(l_[i]), wide(3 + len(RW_LEVELS) + lv), ALU.mult, s1.free)
                        m2 = tt(blocks(s2.tile), blocks(n_[i]), wide(3 + lv), ALU.mult, s2.free)
                        b1, p1 = small_products(s1.tile, plain(Y[:, c, :]), m1, ym[i])
                        b2, p2 = small_products(s2.tile, plain(x_[i]), m2, xm[i])
                        e1 = acopy(s1.tile, b1.tile, p1)
                        b1.release(e1)
                        e2 = acopy(s2.tile, b2.tile, p2)
                        b2.release(e2)
                        b1, p1 = small_products(x_[i], plain(s1.tile), e1)
                        b2, p2 = small_products(Y[:, c, :], plain(s2.tile), e2)
                        s1.release(p1)
                        s2.release(p2)
                        ym[i] = tt(Y[:, c, :], Y[:, c, :], b1.tile, ALU.add, p1, p2)
                        b1.release(ym[i])
                        xm[i] = tt(x_[i], x_[i], b2.tile, ALU.add, p2, p1)
                        b2.release(xm[i])
                for i in range(2):
                    c = 2 * pair + i
                    kept[i] = [ym[i], xm[i]]
                    s1, s2 = tmp.take(), tmp.take()
                    bank, m = small_products(M_T[:, c, :], lambda part, cc, hh, tk:
                                             v_tok[part, tk, c * P + hh * 64:c * P + hh * 64 + 64])
                    e = acopy(s1.tile, bank.tile, m, s1.free)
                    bank.release(e)
                    bank, m = small_products(Y[:, c, :], plain(s1.tile), e, ym[i])
                    e = acopy(M_T[:, c, :], bank.tile, m)
                    bank.release(e)
                    s1.release(m)
                    bank = psum.take()
                    for tk in range(TT):
                        m = turn(bank.tile[:, tk * P:(tk + 1) * P], a_hat[:, c, tk * P:(tk + 1) * P],
                                 after=[bank.free], marked=True)
                    e = acopy(s2.tile, bank.tile, m, s2.free)
                    bank.release(e)
                    for odd in range(2):
                        bank = psum.take()
                        part = slice(64 * odd, 64 * odd + 64)
                        pe.wait(bank.free, e)
                        for hh in range(2):
                            for tk in range(TT):
                                o = slice(64 * hh, 64 * hh + 64)
                                m = mm(bank.tile[o, tk * 64:(tk + 1) * 64],
                                       s2.tile[part, tk * P + hh * 64:tk * P + hh * 64 + 64],
                                       Y[part, c, (hh * TT + tk) * 64:(hh * TT + tk) * 64 + 64],
                                       marked=(hh == 1 and tk == TT - 1))
                        w2 = a_hat[:, c, :].rearrange("p (n o t) -> p n o t", o=2, t=64)[:, :, odd, :]
                        e2 = acopy(w2, bank.tile[:, 0:256].rearrange("p (n t) -> p n t", t=64), m)
                        bank.release(e2)
                    s2.release(m)
            join()
            st = [carve(inv_at + i * 256, 256).rearrange("p (c v) -> p c v", c=4) for i in range(2)]
            uus = [carve(inv_at + 512 + i * T, T) for i in range(2)]
            out_rw = a_hat
            st_mark = memset(st[0], 0.0)
            u_read = [None, None]
            for ch in range(n_ch):
                part, tk = slice(64 * (ch % 2), 64 * (ch % 2) + 64), ch // 2
                tsl = slice(ch * 64, ch * 64 + 64)
                old, new = st[ch % 2], st[(ch + 1) % 2]
                uu = uus[ch % 2]

                def heads():
                    for hd in range(RW_HEADS):
                        c, hh = hd // 2, hd % 2
                        yield hd, c, slice(64 * hh, 64 * hh + 64), slice(hd * 64, hd * 64 + 64), \
                            slice((hh * TT + tk) * 64, (hh * TT + tk) * 64 + 64)
                um = []
                for hh in range(2):
                    bank = psum.take()
                    pe.wait(bank.free, st_mark)
                    hp = slice(64 * hh, 64 * hh + 64)
                    for c in range(4):
                        m = mm(bank.tile[part, c * 64:(c + 1) * 64], a_hat[hp, c, tsl], old[hp, c, :], marked=(c == 3))
                    u4 = uu[part, :].rearrange("p (c o v) -> p c o v", c=4, o=2)[:, :, hh, :]
                    um.append(tt(u4, bank.tile[part, 0:256].rearrange("p (c v) -> p c v", c=4),
                                 M_T[part, :, (hh * TT + tk) * 64:(hh * TT + tk) * 64 + 64], ALU.add, m,
                                 u_read[ch % 2]))
                    bank.release(um[-1])
                bank = psum.take()
                pe.wait(bank.free, um)
                for hd, c, hp, hv, cc in heads():
                    o = bank.tile[hp, c * 64:(c + 1) * 64]
                    mm(o, k_tok[part, tk, hv], v_tok[part, tk, hv], start=True, stop=False)
                    m = mm(o, b_tok[part, tk, hv], uu[part, hv], start=False, stop=True, marked=(hd == RW_HEADS - 1))
                b3 = bank.tile[:, 0:256].rearrange("p (c v) -> p c v", c=4)
                hm = tt(new, old, b3, ALU.add, m, st_mark)
                bank.release(hm)
                ed = end_decay[:, :].rearrange("p (c n) -> p c n", c=4)[:, :, ch:ch + 1].to_broadcast([P, 4, 64])
                st_new = tt(new, new, ed, ALU.mult, hm)
                bank, bank2 = psum.take(), psum.take()
                pe.wait(bank.free, bank2.free)
                for hd, c, hp, hv, cc in heads():
                    m1 = mm(bank.tile[hp, c * 64:(c + 1) * 64], old[hp, c, :], r_t[c][hp, tsl],
                            marked=(hd == RW_HEADS - 1))
                for hd, c, hp, hv, cc in heads():
                    o = bank2.tile[hp, c * 64:(c + 1) * 64]
                    mm(o, v_tok[part, tk, hv], RK_T[part, c, cc], start=True, stop=False)
                    m = mm(o, uu[part, hv], RB_T[part, c, cc], start=False, stop=True, marked=(hd == RW_HEADS - 1))
                u_read[ch % 2] = m
                yc_ = out_rw[:, :, tsl]
                ym_ = acopy(yc_, bank.tile[:, 0:256].rearrange("p (c v) -> p c v", c=4), m1)
                bank.release(ym_)
                ym_ = tt(yc_, yc_, bank2.tile[:, 0:256].rearrange("p (c v) -> p c v", c=4), ALU.add, m, ym_)
                bank2.release(ym_)
                st_mark = [st_new, m]
            slot_a.release(m)
            slot_b.release(m)
            for c in range(4):
                yc = [out_rw[:, c, :]]
                cm = center(yc, [ym_], head_ones, 64, yc)
                bank, m = square_sum(yc, cm, head_ones, T)
                r, m = inverse_root(bank, m, 64, GN_EPS, T)
                m = stt(yc[0], yc[0], col("rw_lnx_g_2", c), r.tile, ALU.mult, ALU.mult, m)
                r.release(m)
                m = stt(yc[0], yc[0], col("rw_lnx_b_2", c), bonus[:, c, :], ALU.add, ALU.add, m)
                mixed[4 + c] = tt(h[:, 4 + c, :], yc[0], gate[:, c, :], ALU.mult, m, h_read)
            join()
            put_y, y_marks = into(lambda c: y[:, c, :])
            gemm(dram["w_out"], h_tile, mixed, put_y)
            return y_marks

        def peer(h_marks):
            join()
            NQ = 2 * PEER_HEADS
            q = carve(0, NQ * T).rearrange("p (c t) -> p c t", c=NQ)
            sc = carve(8192, NQ * NKEYS).rearrange("p (g n) -> p g n", g=NQ)
            cand = carve(10240, PEER_HEADS * TOPK * TOPK).rearrange("p (h n) -> p h n", h=PEER_HEADS)
            pick = carve(12288, 2048)
            KAT = 14336
            keys = [carve(KAT + i * 1024, 1024) for i in range(2)]
            HK = PEER_HEADS * TOPK
            at = KAT + 2048
            top_v = carve(at, NQ * TOPK).rearrange("p (g k) -> p g k", g=NQ)
            top_i = carve(at + 256, NQ * TOPK).rearrange("p (g k) -> p g k", g=NQ)
            idx = carve(at + 512, 256).bitcast(U32)
            best_v = carve(at + 768, HK)
            parts = carve(at + 896, HK * 3)
            half_f = carve(at + 1280, 2 * HK)
            total = carve(at + 1536, 8)
            turned = carve(18432, 3 * T).rearrange("p (k t) -> p k t", k=3)
            km = [side_queue.move(keys[i], dram[f"peer_k{i + 1}"], side_ports[7 + i]) for i in range(2)]
            put_q, q_marks = into(lambda c: q[:, c, :])
            gemm(dram["peer_wq"], h_tile, h_marks, put_q)
            counter = const["counter"]
            prev = []
            for tk in range(TT):
                s_marks = []
                for g4 in range(NQ // 4):
                    bank = psum.take()
                    pe.wait(bank.free, km)
                    for j in range(4):
                        g = g4 * 4 + j
                        m = mm(bank.tile[:, j * P:(j + 1) * P], q[:, g, tk * P:(tk + 1) * P],
                               keys[g % 2][:, (g // 2) * P:(g // 2 + 1) * P], after=[q_marks[g]], marked=(j == 3))
                    cp = acopy(sc[:, g4 * 4:g4 * 4 + 4, :], bank.tile.rearrange("p (g n) -> p g n", g=4), m, prev)
                    bank.release(cp)
                    s_marks.append(cp)

                def top16(src, vals, inds, *after):
                    dve.wait(*after)
                    m = dve.mark(nc.vector.max(vals[:, 0:8], src))
                    dve.wait(m)
                    m = dve.mark(nc.vector.max_index(inds[:, 0:8], vals[:, 0:8], src))
                    dve.wait(m)
                    m = dve.mark(nc.vector.match_replace(src, vals[:, 0:8], src, LOWEST))
                    dve.wait(m)
                    m = dve.mark(nc.vector.max(vals[:, 8:16], src))
                    dve.wait(m)
                    return dve.mark(nc.vector.max_index(inds[:, 8:16], vals[:, 8:16], src))
                m = prev
                for g in range(NQ):
                    m1 = top16(sc[:, g, :], top_v[:, g, :], idx[:, g * TOPK:(g + 1) * TOPK], s_marks[g // 4], m)
                sc_read = m1
                m = vcopy(top_i.rearrange("p g k -> p (g k)"), idx, m1)
                tv = top_v.rearrange("p (h s) k -> p h s k", s=2)
                c4 = cand.rearrange("p h (i j) -> p h i j", i=TOPK)
                shape = [P, PEER_HEADS, TOPK, TOPK]
                for hd in range(PEER_HEADS):
                    m2 = tt(c4[:, hd], tv[:, hd, 0, :].unsqueeze(2).to_broadcast([P, TOPK, TOPK]),
                            tv[:, hd, 1, :].unsqueeze(1).to_broadcast([P, TOPK, TOPK]), ALU.add, m)
                for hd in range(PEER_HEADS):
                    m3 = top16(cand[:, hd, :], best_v[:, hd * TOPK:(hd + 1) * TOPK],
                               idx[:, hd * TOPK:(hd + 1) * TOPK], m2)
                ci = idx[:, 0:HK]
                m_hi = ts(idx[:, HK:2 * HK], ci, 4, None, ALU.logical_shift_right, None, m3)
                m_a = vcopy(half_f[:, 0:HK], idx[:, HK:2 * HK], m_hi)
                m_lo = ts(idx[:, HK:2 * HK], ci, 15, None, ALU.bitwise_and, None, m_a)
                m_b = vcopy(half_f[:, HK:2 * HK], idx[:, HK:2 * HK], m_lo)
                pk = pick.rearrange("p (n i) -> p n i", i=TOPK)
                ti = top_i.rearrange("p (h s) k -> p h s k", s=2)
                m = m_b
                for side in range(2):
                    place = half_f[:, side * HK:(side + 1) * HK].unsqueeze(2).to_broadcast([P, HK, TOPK])
                    count = counter[:, 0:TOPK].unsqueeze(1).to_broadcast([P, HK, TOPK])
                    m = tt(pk, place, count, ALU.is_equal, m, prev)
                    for hd in range(PEER_HEADS):
                        pv = pk[:, hd * TOPK:(hd + 1) * TOPK, :]
                        m4 = tt(pv, pv, ti[:, hd, side, :].unsqueeze(1).to_broadcast([P, TOPK, TOPK]), ALU.mult, m)
                    m = reduce(parts[:, side * HK:(side + 1) * HK], pk, ALU.add, m4)
                b3 = best_v.rearrange("p (h k) -> p h k", h=PEER_HEADS)
                g3 = parts[:, 2 * HK:3 * HK].rearrange("p (h k) -> p h k", h=PEER_HEADS)
                m = tt(g3, b3, b3[:, :, 0:1].to_broadcast([P, PEER_HEADS, TOPK]), ALU.subtract, m)
                m = fn(g3, g3, ACT.Exp, m)
                m = reduce(total, g3, ALU.add, m)
                m = recip(total, total, m)
                m = tt(g3, g3, total.unsqueeze(2).to_broadcast([P, PEER_HEADS, TOPK]), ALU.mult, m)
                bank = psum.take()
                for j in range(3):
                    mt = turn(bank.tile[:, j * P:(j + 1) * P], parts[:, j * HK:(j + 1) * HK],
                              after=[m, bank.free], marked=True)
                cp = acopy(turned[:, :, tk * P:(tk + 1) * P],
                           bank.tile[:, 0:3 * P].rearrange("p (k t) -> p k t", k=3), mt)
                bank.release(cp)
                prev = [cp, sc_read]
            join()
            stages = Ring([Slot(carve(i * 8192, 8192).rearrange("p (a t) -> p a t", t=STAGE_TOKENS), side_ports[9 + i])
                           for i in range(2)])
            hots = Ring([Slot(carve(16384 + i * 256, 256)) for i in range(8)])
            table_marks = []
            for t0 in range(0, T, STAGE_TOKENS):
                sg = stages.take()
                for t4 in range(t0, t0 + STAGE_TOKENS, 4):
                    bank = psum.take()
                    pe.wait(bank.free)
                    for j in range(4):
                        t = t4 + j
                        hot = hots.take()
                        key2, key1 = hot.tile[:, 0:P], hot.tile[:, P:2 * P]
                        m = ts(key2, counter[:, :], turned[:, 1, t:t + 1], None, ALU.is_equal, None, hot.free)
                        m = ts(key1, counter[:, :], turned[:, 0, t:t + 1], turned[:, 2, t:t + 1],
                               ALU.is_equal, ALU.mult, hot.free)
                        m = mm(bank.tile[:, j * P:(j + 1) * P], key2, key1, after=[m], marked=True)
                        hot.release(m)
                    cp = acopy(sg.tile[:, :, t4 - t0:t4 - t0 + 4],
                               bank.tile.rearrange("p (t a) -> p a t", t=4), m, sg.free)
                    bank.release(cp)
                wr = weight_queue.move(gate_table[:, :, t0:t0 + STAGE_TOKENS].rearrange("a p t -> p a t"), sg.tile,
                                     sg.port, after=[cp])
                sg.release(wr)
                table_marks.append(wr)
            join()
            n_groups = NKEYS // KEYS_PER_GROUP
            acts = Ring([Slot(carve(i * 4096, 4096).rearrange("p (a t) -> p a t", t=T)) for i in range(2)])
            gates = Ring([Slot(carve(8192 + i * 4096, 4096).rearrange("p (a t) -> p a t", t=T), side_ports[7 + i])
                          for i in range(2)])
            GE = KEYS_PER_GROUP * NKEYS
            for s in acts.slots + gates.slots:
                s.free = table_marks[:]
            y_marks = [None] * CT
            act_marks = {}

            def experts_in(g):
                gt, ab = gates.take(), acts.take()
                gm = side_queue.move(gt.tile, gate_table[g * KEYS_PER_GROUP:(g + 1) * KEYS_PER_GROUP]
                                     .rearrange("a p t -> p a t"), gt.port, after=[gt.free, table_marks])
                marks = {}

                def put(c, ps, m):
                    s = tmp.take()
                    m = fn(s.tile, ps, ACT.Gelu, m, s.free)
                    marks[c] = tt(ab.tile[:, c, :], s.tile, gt.tile[:, c, :], ALU.mult, m, gm, ab.free)
                    s.release(marks[c])
                    return [m]
                gemm(dram["peer_u"], h_tile, h_marks, put, g * GE, GE)
                gt.release(marks[CT - 1])
                act_marks[g] = (ab, marks)

            def experts_out(g):
                ab, marks = act_marks.pop(g)

                def put(c, ps, m):
                    if g == 0:
                        y_marks[c] = vcopy(y[:, c, :], ps, m)
                    else:
                        y_marks[c] = tt(y[:, c, :], y[:, c, :], ps, ALU.add, m, y_marks[c])
                    return [y_marks[c]]
                gemm(dram["peer_v"][g * GE:(g + 1) * GE, :], lambda k: ab.tile[:, k, :], marks, put)
                ab.release(pe.last())
            for g in range(n_groups):
                experts_in(g)
                if g:
                    experts_out(g - 1)
            experts_out(n_groups - 1)
            return y_marks

        mem_raw = h_buf[:, 0:CT * M].rearrange("p (c t) -> p c t", c=CT)
        mm_in = side_queue.move(mem_raw, dram["mem"].rearrange("(c p) t -> p c t", p=P), side_ports[11])
        rms_scale([mem_raw[:, c, :] for c in range(CT)], [mm_in] * CT, lambda i: col("mem_norm_gain", i),
                  [mem_n[:, c, :] for c in range(CT)], n=M)
        join()
        xm = [x_in] * CT
        xm = even_mixer(xm)
        xm = memory_attention(0, xm)
        xm = mlp(0, xm)
        xm = odd_mixer(xm)
        xm = memory_attention(1, xm)
        xm = mlp(1, xm)
        mod_mark = modulation()
        hm = ada_norm(xm, 0, mod_mark)
        ym = rw_mixer(hm)
        xm = close_block(xm, ym, 0, "ln1_g_2", "ln1_b_2", mod_mark)
        hm = ada_norm(xm, 1, mod_mark)
        ym = peer(hm)
        xm = close_block(xm, ym, 1, "ln2_g_2", "ln2_b_2", mod_mark)
        done = weight_queue.move(out.rearrange("(c p) t -> p c t", p=P), x, out_port, after=[xm])
        sp.wait(done)
        for prt in side_ports:
            if prt.count:
                sp.wait((prt.sem, prt.count))


def layouts(i):
    a = {k: np.asarray(v) for k, v in i.items()}
    cols = [a[n].reshape(-1, P).T for n, _ in COLUMNS]
    p_, u_ = np.arange(P)[:, None], np.arange(T)[None, :]
    dist = np.clip(p_ + T - P - u_, -REL_CLIP, REL_CLIP) + REL_CLIP
    out = {
        "columns": np.concatenate(cols, axis=1),
        "x": a["x"][0].T, "mem": a["mem"][0].T,
        "w_in_ab": a["w_in_ab"][0], "pool_w": a["pool_w"][0], "w_out_ab": a["w_out_ab"][0],
        "w_qkv": a["w_qkv"][0], "rel_bias": a["rel_bias"][0][:, dist], "w_o_att": a["w_o_att"][0],
        "w_mem_q": a["w_mem_q"], "w_mem_kv": a["w_mem_kv"], "w_mem_o": a["w_mem_o"],
        "w_ff1": a["w_ff1"], "w_ff2": a["w_ff2"],
        "cond_w": a["cond_w_2"], "w_in": a["w_in_2"], "w_out": a["w_out_2"],
        "lora": np.concatenate([a["rw_w2_2"], a["rw_a2_2"]], axis=0), "rw_g2": a["rw_g2_2"],
        "peer_wq": a["peer_wq_2"],
        "peer_k1": a["peer_k1_2"].transpose(2, 0, 1).reshape(P, -1),
        "peer_k2": a["peer_k2_2"].transpose(2, 0, 1).reshape(P, -1),
        "peer_u": a["peer_u_2"].T, "peer_v": a["peer_v_2"],
    }
    out.update(shape_constants())
    return {k: np.ascontiguousarray(v) for k, v in out.items()}


def kernel(**inputs):
    import concourse.bacc as bacc
    from concourse.bass_utils import run_bass_kernel_spmd
    arrays = layouts(inputs)
    nc = bacc.Bacc("TRN2", target_bir_lowering=False, num_devices=1)
    dram = {k: nc.dram_tensor(f"in_{k}", v.shape, F32, kind="ExternalInput").ap() for k, v in arrays.items()}
    gate_table = nc.dram_tensor("gate_table", (NKEYS, NKEYS, T), F32, kind="Internal").ap()
    out = nc.dram_tensor("out", (D, T), F32, kind="ExternalOutput").ap()
    build(nc, dram, out, gate_table)
    r = run_bass_kernel_spmd(nc, [{f"in_{k}": v for k, v in arrays.items()}], core_ids=[0])
    return np.ascontiguousarray(r.results[0]["out"].T)[None]
```

```python
from contextlib import ExitStack
import math

import numpy as np
import concourse.bass as bass
import concourse.mybir as mybir
from concourse.alu_op_type import AluOpType as ALU

ACT = mybir.ActivationFunctionType
F32 = mybir.dt.float32
F32R = mybir.dt.float32r
U32 = mybir.dt.uint32
AX = mybir.AxisListType

P = 128
T = 512
D = 1024
CT = D // P
TT = T // P
M = 256
FF = 4 * D
NORM_EPS = 1e-6
LN_EPS = 1e-5
GN_EPS = 64e-5
GATE_CLIP = 60.0
POOL_WINDOWS = (2, 4, 8, 16)
POOL_PAD = max(POOL_WINDOWS)
REC_HEADS = 4
ATT_HEADS = 16
ATT_DIM = D // ATT_HEADS
CHUNK = 64
REL_CLIP = 256
MEM_HEADS = 4
MEM_TILES = CT // MEM_HEADS
CONV_K = 31
RW_CHUNK = 64
RW_HEADS = 8
RW_TILES = 4
RW_LEVELS = (1, 2, 4, 8, 16, 32)
REC_LEVELS = (1, 2, 4, 8, 16, 32, 64)
PEER_HEADS = 8
NKEYS = 128
TOPK = 16
EXPERTS = NKEYS * NKEYS
ALPHA = 2.0 ** 0.25
MASK_VALUE = -1e30
ARENA = 18176
LOWEST = -3.0e38
CHUNK_WORDS = 2048
GROUP = 4
STAGE_TOKENS = 32
EARLY_GROUPS = 20

COLUMNS = [
    ("norm_gains", 96), ("mem_norm_gain", 8), ("pool_scale", 4), ("rec_lb_logits", 4), ("rec_out_gain", 1),
    ("c_2", 8), ("cond_b_2", 48), ("mu_shift_2", 14), ("conv_w_2", 4 * CONV_K), ("conv_b_2", 4),
    ("conv_ln_g_2", 4), ("conv_ln_b_2", 4), ("rw_w0_2", 4), ("rw_a0_2", 4), ("rw_kk_2", 4), ("rw_ka_2", 4),
    ("rw_rk_2", 4), ("rw_lnx_g_2", 4), ("rw_lnx_b_2", 4), ("ln1_g_2", 8), ("ln1_b_2", 8), ("ln2_g_2", 8),
    ("ln2_b_2", 8),
]
COLUMN_AT = {}
for _name, _n in COLUMNS:
    COLUMN_AT[_name] = sum(n for _, n in COLUMNS[:len(COLUMN_AT)])
N_COLUMNS = sum(n for _, n in COLUMNS)


SCRATCH = {
    "gate_table": (T // STAGE_TOKENS, NKEYS, NKEYS * STAGE_TOKENS),
    "early_table": (EARLY_GROUPS * GROUP, P, T),
    "memory_k": (2, CT, P, M),
    "memory_v": (2, M // P, P, D),
}


def shape_constants():
    i = np.arange(P)
    out = {"identity": np.eye(P), "ones": np.ones((P, P)), "head_ones": (i[:, None] // 64 == i[None, :] // 64)}

    def level(s, t, m):
        return (s // (2 * m) == t // (2 * m)) & (s % (2 * m) < m) & (t % (2 * m) >= m)

    s, t = i[:, None], i[None, :]
    out["rec_masks"] = np.concatenate([s == t] + [level(s, t, m) for m in REC_LEVELS], axis=1)
    s, t = (i % 64)[:, None], np.arange(64)[None, :]
    out["rw_masks"] = np.concatenate(
        [s < t, s <= t, s == t] + [level(s, t, m) for m in RW_LEVELS] + [level(t, s, m) for m in RW_LEVELS], axis=1)
    pos = np.arange(T)[None, :]
    out["keep_tile"] = np.repeat(pos % P != 0, P, axis=0)
    out["keep_chunk"] = np.repeat(pos % RW_CHUNK != 0, P, axis=0)
    out["counter"] = np.repeat(np.arange(P)[None, :], P, axis=0)
    out["pool_edge"] = np.repeat(np.concatenate(
        [w / np.minimum(np.arange(1, POOL_PAD + 1), w) for w in POOL_WINDOWS])[None, :], P, axis=0)
    return {k: np.ascontiguousarray(v.astype(np.float32)) for k, v in out.items()}


STAGE_CONSTANTS = ("rec_masks", "rw_masks", "keep_tile", "keep_chunk")
CONSTANT_WIDTHS = {k: v.shape[1] for k, v in shape_constants().items()}


def flat(marks):
    for m in marks:
        if isinstance(m, tuple) and len(m) == 2 and isinstance(m[1], int):
            yield m
        elif m is not None:
            yield from flat(m)


class Lane:

    def __init__(self, eng, sem):
        self.eng, self.sem, self.count, self.waited = eng, sem, 0, {}

    def wait(self, *marks):
        for sem, value in flat(marks):
            if self.waited.get(sem.name, 0) < value:
                self.eng.wait_ge(sem, value)
                self.waited[sem.name] = value

    def mark(self, ins):
        ins.then_inc(self.sem, 1)
        self.count += 1
        return (self.sem, self.count)

    def last(self):
        return (self.sem, self.count) if self.count else None


class Queue:

    def __init__(self, eng, lane):
        self.eng, self.lane = eng, lane

    def move(self, out, in_, port, after=()):
        self.lane.wait(*after)
        self.eng.dma_start(out, in_).then_inc(port.sem, 16)
        port.count += 16
        return (port.sem, port.count)


class Port:

    def __init__(self, sem):
        self.sem, self.count = sem, 0


class Slot:
    def __init__(self, tile, port=None):
        self.tile, self.port, self.free, self.held = tile, port, [], False

    def release(self, *marks):
        self.free, self.held = list(marks), False


class Ring:

    def __init__(self, slots):
        self.slots, self.n = slots, 0

    def take(self):
        assert not all(s.held for s in self.slots), "a ring's buffer is taken before one was released"
        while self.slots[self.n % len(self.slots)].held:
            self.n += 1
        s = self.slots[self.n % len(self.slots)]
        self.n += 1
        s.held = True
        return s


def build(nc, dram, out, gate_table, early_table, memory_k, memory_v):
    ctx = ExitStack()
    with ctx:
        def sb(name, cols, dt=F32):
            return ctx.enter_context(nc.sbuf_tensor(name, [P, cols], dt))

        def sem(name):
            return ctx.enter_context(nc.semaphore(name))

        pe = Lane(nc.tensor, sem("pe_done"))
        dve = Lane(nc.vector, sem("dve_done"))
        act = Lane(nc.scalar, sem("act_done"))
        pool = Lane(nc.gpsimd, sem("pool_done"))
        sp = Lane(nc.sync, sem("sp_done"))
        weight_queue = Queue(nc.sync, sp)
        side_queue = Queue(nc.gpsimd, pool)

        x = sb("residual", CT * T)[:, :].rearrange("p (c t) -> p c t", c=CT)
        h_hi = sb("normed_high", CT * T, F32R)[:, :].rearrange("p (c t) -> p c t", c=CT)
        h_lo = sb("normed_low", CT * T, F32R)[:, :].rearrange("p (c t) -> p c t", c=CT)
        y_buf = sb("branch", CT * T)[:, :]
        y = y_buf.rearrange("p (c t) -> p c t", c=CT)
        columns = sb("columns", N_COLUMNS)
        const = {k: sb("const_" + k, n) for k, n in CONSTANT_WIDTHS.items() if k not in STAGE_CONSTANTS}
        tmp = Ring([Slot(sb(f"tmp{i}", T)[:, :]) for i in range(6)])
        small = Ring([Slot(sb(f"small{i}", 4)[:, :]) for i in range(8)])
        scalars = sb("scalars", 4 + 2 * CT)
        mod = sb("modulation", 48)
        scale_1 = sb("one_plus_scale", 16)
        end_decay = sb("chunk_decay", 4 * T // RW_CHUNK)
        raw = Ring([Slot(sb(f"weights{i}", CHUNK_WORDS)[:, :], Port(sem(f"weights_landed{i}"))) for i in range(3)])
        space = {}

        def open_split(name):
            ctx_ = space["split_ctx"] = ExitStack()
            space["split"] = Ring([Slot([ctx_.enter_context(nc.sbuf_tensor(f"{name}_{part}{i}", [P, CHUNK_WORDS], F32R))
                                         [:, :] for part in ("high", "low")]) for i in range(2)])

        def open_arena(name, width=ARENA):
            ctx_ = space["arena_ctx"] = ExitStack()
            space["arena"] = ctx_.enter_context(nc.sbuf_tensor(name, [P, width], F32))[:, :]
            space["width"] = width

        ctx.callback(lambda: space["split_ctx"].close())
        ctx.callback(lambda: space["arena_ctx"].close())
        open_split("split")
        open_arena("arena")
        psum = Ring([Slot(ctx.enter_context(nc.psum_tensor(f"bank{i}", [P, 512], F32))[:, :]) for i in range(8)])
        side_ports = [Port(sem(f"side{i}")) for i in range(12)]
        early_ports = [Port(sem(f"early_written{i}")) for i in range(CT)]
        out_port = Port(sem("out_written"))

        def carve(at, n):
            assert at + n <= space["width"]
            return space["arena"][:, at:at + n]

        def col(name, i=0):
            j = COLUMN_AT[name] + i
            return columns[:, j:j + 1]

        def tt(o, a, b, op, *after):
            dve.wait(*after)
            return dve.mark(nc.vector.tensor_tensor(o, a, b, op))

        def ts(o, a, s1, s2, op0, op1, *after):
            dve.wait(*after)
            if op1 is None:
                return dve.mark(nc.vector.tensor_scalar(o, a, s1, None, op0))
            return dve.mark(nc.vector.tensor_scalar(o, a, s1, s2, op0, op1))

        def stt(o, a, s, b, op0, op1, *after):
            dve.wait(*after)
            return dve.mark(nc.vector.scalar_tensor_tensor(out=o, in0=a, scalar=s, in1=b, op0=op0, op1=op1))

        def vcopy(o, a, *after):
            dve.wait(*after)
            return dve.mark(nc.vector.tensor_copy(o, a))

        def recip(o, a, *after):
            dve.wait(*after)
            return dve.mark(nc.vector.reciprocal(o, a))

        def memset(o, value, *after):
            dve.wait(*after)
            return dve.mark(nc.vector.memset(o, value))

        def reduce(o, a, op, *after):
            dve.wait(*after)
            return dve.mark(nc.vector.tensor_reduce(o, a, AX.X, op))

        def fn(o, a, func, *after, **kw):
            act.wait(*after)
            return act.mark(nc.scalar.activation(o, a, func, **kw))

        def acopy(o, a, *after):
            act.wait(*after)
            return act.mark(nc.scalar.copy(o, a))

        def ptt(o, a, b, op, *after):
            pool.wait(*after)
            return pool.mark(nc.gpsimd.tensor_tensor(o, a, b, op))

        def mm(o, lhsT, rhs, start=True, stop=True, after=(), marked=False):
            pe.wait(*after)
            ins = nc.tensor.matmul(o, lhsT, rhs, start=start, stop=stop)
            return pe.mark(ins) if marked else None

        def turn(o, a, after=(), marked=False):
            pe.wait(*after)
            n = a.shape[0]
            ins = nc.tensor.transpose(o, a, const["identity"][0:n, 0:n])
            return pe.mark(ins) if marked else None

        def join():
            marks = [lane.last() for lane in (pe, dve, act, pool)]
            for lane in (pe, dve, act, pool):
                lane.wait(*marks)

        port = side_ports[0]
        const_mark = [side_queue.move(columns[:, :], dram["columns"], port)]
        for k in const:
            const_mark = [side_queue.move(const[k][:, :], dram[k], port)]
        x_in = side_queue.move(x, dram["x"].rearrange("(c p) t -> p c t", p=P), side_ports[1])
        for lane in (pe, dve, act, pool):
            lane.wait(const_mark)
        ones, head_ones = const["ones"][:, :], const["head_ones"][:, :]
        eps_of = {}
        for i, value in enumerate((NORM_EPS, LN_EPS, GN_EPS, 1.0)):
            m = memset(scalars[:, i:i + 1], value)
            eps_of[value] = scalars[:, i:i + 1]
        act.wait(m)
        one = eps_of[1.0]

        def fetch(w, k0, n0, width):
            s = raw.take()
            n_k = CHUNK_WORDS // width
            s.ready = weight_queue.move(s.tile.rearrange("p (a n) -> p a n", a=n_k),
                                        w[k0:k0 + n_k * P, n0:n0 + width].rearrange("(a p) n -> p a n", p=P),
                                        s.port, after=s.free)
            return s

        low_on = {"pool": 1}

        def split_chunk(w, k0, n0, width):
            s = fetch(w, k0, n0, width)
            d = space["split"].take()
            hi, lo = d.tile
            half = CHUNK_WORDS // 2
            marks = []
            for i in range(2):
                cut_ = slice(i * half, (i + 1) * half)
                mh = acopy(hi[:, cut_], s.tile[:, cut_], s.ready, d.free)
                op = ptt if i < low_on["pool"] else tt
                marks += [mh, op(lo[:, cut_], s.tile[:, cut_], hi[:, cut_].bitcast(F32), ALU.subtract, mh, d.free)]
            s.release(*marks)
            d.ready = [marks[0:2], marks[2:4]]
            d.parts = [part.rearrange("p (a n) -> p a n", n=width) for part in (hi, lo)]
            return d

        class Stream:

            def __init__(self, w, k0=0, n0=0, n_cols=None, width=256):
                n_cols = w.shape[1] if n_cols is None else n_cols
                self.specs = [(w, k0, n, width) for n in range(n0, n0 + n_cols, width)]
                self.split = []

            def ahead(self, i, following):
                if i < len(self.specs):
                    if i == len(self.split):
                        self.split.append(split_chunk(*self.specs[i]))
                elif following is not None and not following.split:
                    following.ahead(0, None)

        def triple(o, a_parts, b_parts, first, last, marked):
            (ah, al), (bh, bl) = a_parts, b_parts
            mm(o, ah, bh, start=first, stop=False)
            mm(o, ah, bl, start=False, stop=False)
            return mm(o, al, bh, start=False, stop=last, marked=marked)

        def product_steps(stream, rhs, ready, evacuate, width_out=T, following=None):
            stream.ahead(0, None)
            c_all = 0
            for i, (_, _, _, width) in enumerate(stream.specs):
                d = stream.split[i]
                n_k = CHUNK_WORDS // width
                stream.ahead(i + 1, following)
                for c in range(width // P):
                    bank = psum.take()
                    pe.wait(d.ready, bank.free)
                    for a in range(n_k):
                        pe.wait(ready[a])
                        m = triple(bank.tile[:, 0:width_out], [w_[:, a, c * P:(c + 1) * P] for w_ in d.parts], rhs(a),
                                   a == 0, a == n_k - 1, a == n_k - 1)
                    if c == width // P - 1:
                        d.release(m)
                    bank.release(*evacuate(c_all, bank.tile[:, 0:width_out], m))
                    c_all += 1
                    yield

        def token_steps(stream, lhs, ready, evacuate, n_token_tiles, following=None):
            stream.ahead(0, None)
            for i, (_, _, n0, width) in enumerate(stream.specs):
                d = stream.split[i]
                stream.ahead(i + 1, following)
                for tk in range(n_token_tiles):
                    bank = psum.take()
                    pe.wait(d.ready, bank.free)
                    for a in range(CT):
                        pe.wait(ready[a])
                        m = triple(bank.tile[:, 0:width], [l_[:, tk * P:(tk + 1) * P] for l_ in lhs(a)],
                                   [w_[:, a, :] for w_ in d.parts], a == 0, a == CT - 1, a == CT - 1)
                    if tk == n_token_tiles - 1:
                        d.release(m)
                    bank.release(*evacuate(tk, n0 - stream.specs[0][2], bank.tile[:, 0:width], m))
                    yield

        def run(steps):
            for _ in steps:
                pass

        def product(*args, **kw):
            run(product_steps(*args, **kw))

        def into(dst):
            marks = {}

            def evacuate(c, ps, m):
                marks[c] = acopy(dst(c), ps, m) if c % 2 else vcopy(dst(c), ps, m)
                return [marks[c]]
            return evacuate, marks

        def split_to(hi, lo, src, *after):
            m = acopy(hi, src, *after)
            return [m, tt(lo, src, hi.bitcast(F32), ALU.subtract, m, *after)]

        def channel_sum(tiles, ready, matrix, n):
            bank = psum.take()
            pe.wait(bank.free)
            for i, tile in enumerate(tiles):
                m = mm(bank.tile[:, 0:n], matrix, tile, start=(i == 0), stop=(i == len(tiles) - 1),
                       after=[ready[i]], marked=True)
            return bank, m

        def square_sum(tiles, ready, matrix, n):
            bank = psum.take()
            pe.wait(bank.free)
            for i, tile in enumerate(tiles):
                s = tmp.take()
                q = fn(s.tile[:, 0:n], tile, ACT.Square, s.free, ready[i])
                m = mm(bank.tile[:, 0:n], matrix, s.tile[:, 0:n], start=(i == 0), stop=(i == len(tiles) - 1),
                       after=[q], marked=True)
                s.release(m)
            return bank, m

        def inverse_root(bank, mark, count, eps, n):
            s = tmp.take()
            m = fn(s.tile[:, 0:n], bank.tile[:, 0:n], ACT.Ln, s.free, mark, scale=1.0 / count, bias=eps_of[eps])
            bank.release(m)
            m = fn(s.tile[:, 0:n], s.tile[:, 0:n], ACT.Exp, m, scale=-0.5)
            return s, m

        def rms_scale(tiles, ready, gain, outs, n=T, after=()):
            bank, m = square_sum(tiles, ready, ones, n)
            r, m = inverse_root(bank, m, len(tiles) * P, NORM_EPS, n)
            marks = [stt(o, t, gain(i), r.tile[:, 0:n], ALU.mult, ALU.mult, m, after)
                     for i, (t, o) in enumerate(zip(tiles, outs))]
            r.release(marks[-1])
            return marks

        def center(tiles, ready, matrix, count, outs):
            bank, m = channel_sum(tiles, ready, matrix, T)
            marks = [stt(o, bank.tile, -1.0 / count, t, ALU.mult, ALU.add, m) for t, o in zip(tiles, outs)]
            bank.release(marks[-1])
            return marks

        def add_branch(l, n, y_marks, x_marks):
            tiles = [y[:, c, :] for c in range(CT)]
            normed = rms_scale(tiles, y_marks, lambda i: col("norm_gains", (6 * l + n) * CT + i), tiles)
            return [tt(x[:, c, :], x[:, c, :], tiles[c], ALU.add, normed[c], x_marks[c]) for c in range(CT)]

        def rms_split(tiles, ready, gain, n=T):
            normed = rms_scale(tiles, ready, gain, [y[:, i, 0:n] for i in range(len(tiles))], n)
            return [split_to(h_hi[:, i, 0:n], h_lo[:, i, 0:n], y[:, i, 0:n], normed[i]) for i in range(len(tiles))]

        def pre_norm(l, n, x_marks):
            return rms_split([x[:, c, :] for c in range(CT)], x_marks,
                             lambda i: col("norm_gains", (6 * l + n) * CT + i))

        def h_tile(k):
            return h_hi[:, k, :], h_lo[:, k, :]

        def softmax(src, out_ap, scale, *after):
            s = small.take()
            mx, total = s.tile[:, 0:1], s.tile[:, 1:2]
            m = reduce(mx, src, ALU.max, s.free, after)
            m = ts(mx, mx, -scale, None, ALU.mult, None, m)
            m = fn(out_ap, src, ACT.Exp, m, after, scale=scale, bias=mx, accum_out=total)
            exp_mark = m
            m = recip(total, total, m)
            m = ts(out_ap, out_ap, total, None, ALU.mult, None, m)
            s.release(m)
            return m, exp_mark

        memory_marks = {}

        def memory_keys_steps(l, mem_marks, following):
            marks = memory_marks[l] = []

            def mem_tile(a):
                return h_hi[:, a, 0:M], h_lo[:, a, 0:M]

            def keep(dst, ps, m, width):
                s = mem_out.take()
                cp = acopy(s.tile[:, 0:width], ps, m, s.free)
                s.release(side_queue.move(dst, s.tile[:, 0:width], s.port, after=[cp]))
                marks.append(s.free[0])
                return [cp]
            values = Stream(dram["w_mem_kv"][l], n0=D, n_cols=D)
            yield from product_steps(Stream(dram["w_mem_kv"][l], n_cols=D), mem_tile, mem_marks,
                                     lambda c, ps, m: keep(memory_k[l, c], ps, m, M), width_out=M, following=values)
            yield from token_steps(values, mem_tile, mem_marks,
                                   lambda tk, n0, ps, m: keep(memory_v[l, tk][:, n0:n0 + 256], ps, m, 256), M // P,
                                   following=following)

        def memory_attention(l, x_marks, following):
            w_o = Stream(dram["w_mem_o"][l])
            w_q = Stream(dram["w_mem_q"][l])
            w_q.ahead(0, None)
            h_marks = pre_norm(l, 2, x_marks)
            join()
            q = carve(0, CT * T).rearrange("p (c t) -> p c t", c=CT)
            k = carve(4096, CT * M).rearrange("p (c t) -> p c t", c=CT)
            v = carve(6144, 2 * D).rearrange("p (m c) -> p m c", m=2)
            probs = Ring([Slot(carve(8192 + i * M, M)) for i in range(4)])
            turned = Ring([Slot(carve(9216 + i * 2 * T, 2 * T).rearrange("p (m t) -> p m t", m=2)) for i in range(2)])
            kv_mark = [side_queue.move(k, memory_k[l].rearrange("c p t -> p c t"), side_ports[1], after=memory_marks[l]),
                       side_queue.move(v, memory_v[l].rearrange("m p c -> p m c"), side_ports[11],
                                       after=memory_marks[l])]
            put_q, q_marks = into(lambda c: q[:, c, :])
            product(w_q, h_tile, h_marks, put_q, following=w_o)
            q_read = pe.last()
            mixed = {}
            head = {}

            def score(hd, tq):
                sc = psum.take()
                pe.wait(sc.free, kv_mark)
                for j in range(MEM_TILES):
                    c = hd * MEM_TILES + j
                    m = mm(sc.tile[:, 0:M], q[:, c, tq * P:(tq + 1) * P], k[:, c, :], start=(j == 0),
                           stop=(j == MEM_TILES - 1), after=[q_marks[c]], marked=True)
                pr = probs.take()
                m, read = softmax(sc.tile[:, 0:M], pr.tile, (D // MEM_HEADS) ** -0.5, m, pr.free)
                sc.release(read)
                return pr, m

            def spread(hd, tq, pr, m):
                if tq == 0:
                    head["banks"] = [psum.take() for _ in range(2)]
                banks = head["banks"]
                for mt in range(2):
                    t_mark = turn(banks[mt].tile[:, tq * P:(tq + 1) * P], pr.tile[:, mt * P:(mt + 1) * P],
                                  after=[m, banks[mt].free], marked=True)
                pr.release(t_mark)
                if tq < TT - 1:
                    return
                pt = turned.take()
                turned_marks = []
                for mt in range(2):
                    cp = acopy(pt.tile[:, mt, :], banks[mt].tile, t_mark, pt.free)
                    banks[mt].release(cp)
                    turned_marks.append(cp)
                for j in range(MEM_TILES):
                    c = hd * MEM_TILES + j
                    o = psum.take()
                    pe.wait(o.free, turned_marks)
                    for mt in range(2):
                        m = mm(o.tile, v[:, mt, c * P:(c + 1) * P], pt.tile[:, mt, :], start=(mt == 0),
                               stop=(mt == 1), marked=True)
                    mixed[c] = split_to(h_hi[:, c, :], h_lo[:, c, :], o.tile, m, q_read)
                    o.release(mixed[c])
                pt.release(m)
            items = [(hd, tq) for hd in range(MEM_HEADS) for tq in range(TT)]
            flying = []
            for item in items:
                flying.append((*item, *score(*item)))
                if len(flying) > 2:
                    spread(*flying.pop(0))
            for f in flying:
                spread(*f)
            put_y, y_marks = into(lambda c: y[:, c, :])
            product(w_o, h_tile, mixed, put_y, following=following)
            return add_branch(l, 3, y_marks, x_marks)

        def grouped_product(n_groups, first, second, make, following):
            parts = Ring([Slot([space["hidden"][i][j] for j in range(2)]) for i in range(2)])
            y_marks, flying = [None] * CT, {}

            def one(g):
                slot, marks = parts.take(), {}
                hi, lo = slot.tile
                st, nxt = first(g)
                if st is None:
                    for c in range(GROUP):
                        marks[c], _ = make(g, c, None, None, hi[:, c, :], lo[:, c, :], slot.free)
                else:
                    def put(c, ps, m):
                        marks[c], read = make(g, c, ps, m, hi[:, c, :], lo[:, c, :], slot.free)
                        return read
                    product(st, h_tile, space["h_marks"], put, following=nxt)
                flying[g] = (slot, marks)

            def two(g, nxt):
                slot, marks = flying.pop(g)
                hi, lo = slot.tile

                def put(c, ps, m):
                    if g == 0:
                        y_marks[c] = vcopy(y[:, c, :], ps, m, space["y_free"])
                    else:
                        y_marks[c] = tt(y[:, c, :], y[:, c, :], ps, ALU.add, m, y_marks[c])
                    return [y_marks[c]]
                product(second(g), lambda k: (hi[:, k, :], lo[:, k, :]), marks, put, following=nxt)
                slot.release(pe.last())
            for g in range(n_groups):
                one(g)
                if g:
                    two(g - 1, first(g + 1)[0] if g + 1 < n_groups and first(g + 1)[0] else second(g))
            two(n_groups - 1, following)
            return y_marks

        def open_hidden(name, rest):
            space["arena_ctx"].close()
            c_ = ExitStack()
            space["hidden"] = [[c_.enter_context(nc.sbuf_tensor(f"{name}_{part}{i}", [P, GROUP * T], F32R))[:, :]
                                .rearrange("p (c t) -> p c t", c=GROUP) for part in ("high", "low")] for i in range(2)]
            space["arena"] = c_.enter_context(nc.sbuf_tensor(f"{name}_arena", [P, rest], F32))[:, :] if rest else None
            space["width"] = rest
            space["arena_ctx"] = c_

        def mlp(l, x_marks, following):
            w1 = [Stream(dram["w_ff1"][l], n0=g * GROUP * P, n_cols=GROUP * P) for g in range(FF // P // GROUP)]
            w2 = [Stream(dram["w_ff2"][l], k0=g * GROUP * P, width=512) for g in range(FF // P // GROUP)]
            w1[0].ahead(0, None)
            h_marks = pre_norm(l, 4, x_marks)
            join()
            open_hidden(f"hidden{l}", 0)
            space["h_marks"], space["y_free"] = h_marks, None

            def make(g, c, ps, m, hi, lo, free):
                s = tmp.take()
                m = fn(s.tile, ps, ACT.Relu, m, s.free)
                q = tt(s.tile, s.tile, s.tile, ALU.mult, m)
                marks = split_to(hi, lo, s.tile, q, free)
                s.release(marks)
                return marks, [m]
            n = len(w1)
            y_marks = grouped_product(n, lambda g: (w1[g], w2[g - 1] if g else w1[1]), lambda g: w2[g], make, following)
            x_marks = add_branch(l, 5, y_marks, x_marks)
            join()
            space["arena_ctx"].close()
            if l == 0:
                open_arena("arena_1")
            else:
                space["split_ctx"].close()
                open_arena("arena_2")
                open_split("split_2")
            return x_marks

        def even_mixer(x_marks, following):
            w = dram["w_in_ab"]
            w_u, w_q, w_f, w_i, w_g = [Stream(w, n0=i * 512, n_cols=512) for i in range(5)]
            w_o = Stream(dram["w_out_ab"])
            w_u.ahead(0, None)
            h_marks = pre_norm(0, 0, x_marks)
            join()
            masks_at = ARENA - 8 * P
            rec_masks, keep_tile = carve(masks_at, 8 * P), carve(masks_at - T, T)
            mask_mark = [side_queue.move(rec_masks, dram["rec_masks"], side_ports[3]),
                         side_queue.move(keep_tile, dram["keep_tile"], side_ports[4])]
            upad = carve(0, 4 * (POOL_PAD + T)).rearrange("p (g t) -> p g t", g=4)
            at = 4 * (POOL_PAD + T)
            q, k, b, v, gate = [carve(at + i * 4 * T, 4 * T).rearrange("p (g t) -> p g t", g=4) for i in range(5)]
            at += 5 * 4 * T
            win = [carve(at + i * (POOL_PAD + T), POOL_PAD + T) for i in range(2)]
            lb = carve(at + 2 * (POOL_PAD + T), 8)
            u_marks = {}
            pad = memset(upad[:, :, 0:POOL_PAD], 0.0)

            def put_u(c, ps, m):
                u_marks[c] = vcopy(upad[:, c, POOL_PAD:], ps, m)
                return [u_marks[c]]
            product(w_u, h_tile, h_marks, put_u, following=w_q)
            put_q, q_marks = into(lambda c: q[:, c, :])
            product(w_q, h_tile, h_marks, put_q, following=w_f)
            logit = columns[:, COLUMN_AT["rec_lb_logits"]:COLUMN_AT["rec_lb_logits"] + 4]
            m = tt(lb[:, 0:4], logit, logit, ALU.subtract)
            m = fn(lb[:, 0:4], lb[:, 0:4], ACT.Exp, m)
            m2 = recip(lb[:, 4:8], lb[:, 0:4], m)
            m = tt(lb[:, 0:4], lb[:, 0:4], lb[:, 4:8], ALU.mult, m2)
            m = tt(lb[:, 0:4], lb[:, 0:4], lb[:, 0:4], ALU.subtract, m)
            m = ts(lb[:, 0:4], lb[:, 0:4], 0.0, 1.0, ALU.max, ALU.min, m)
            lb_mark = ts(lb[:, 4:8], lb[:, 0:4], -1.0, 1.0, ALU.mult, ALU.add, m)
            b_marks, k_marks = {}, {}

            def put_f(c, ps, m):
                f, e, g = tmp.take(), tmp.take(), tmp.take()
                fm = ts(f.tile, ps, GATE_CLIP, -GATE_CLIP, ALU.min, ALU.max, m, f.free)
                km = fn(k[:, c, :], f.tile, ACT.Sigmoid, fm, scale=-1.0)
                k_marks[c] = ts(k[:, c, :], k[:, c, :], lb[:, 4 + c:5 + c], None, ALU.mult, None, km, lb_mark)
                em = fn(e.tile, f.tile, ACT.Abs, e.free, fm)
                em = fn(e.tile, e.tile, ACT.Exp, em, scale=-1.0)
                em = fn(e.tile, e.tile, ACT.Ln, em, bias=one)
                gm = fn(g.tile, f.tile, ACT.Exp, g.free, fm, scale=-1.0)
                gm = fn(g.tile, g.tile, ACT.Ln, gm, lb_mark, scale=lb[:, c:c + 1], bias=one)
                em = stt(e.tile, f.tile, 0.0, e.tile, ALU.min, ALU.subtract, em)
                em = tt(e.tile, e.tile, g.tile, ALU.add, em, gm)
                dve.wait(em, mask_mark)
                b_marks[c] = dve.mark(nc.vector.tensor_tensor_scan(
                    out=b[:, c, :], data0=keep_tile, data1=e.tile, initial=0.0,
                    op0=ALU.mult, op1=ALU.add))
                f.release(em, km, gm)
                e.release(b_marks[c])
                g.release(em)
                return [fm]
            product(w_f, h_tile, h_marks, put_f, following=w_i)
            v_marks = {}

            def put_v(tk, n0, ps, m):
                v_marks[tk] = acopy(v[:, tk, n0:n0 + 256], ps, m)
                return [v_marks[tk]]
            run(token_steps(w_i, h_tile, h_marks, put_v, TT, following=w_g))
            gate_marks = {}

            def put_g(c, ps, m):
                s = tmp.take()
                sm = fn(s.tile, ps, ACT.Sigmoid, m, s.free)
                gate_marks[c] = tt(gate[:, c, :], s.tile, ps, ALU.mult, sm)
                s.release(gate_marks[c])
                return [gate_marks[c]]
            product(w_g, h_tile, h_marks, put_g, following=w_o)
            h_read = pe.last()
            mixed = {}
            pool_w = tmp.take()
            pw_mark = side_queue.move(pool_w.tile.rearrange("p (g d) -> p g d", g=4),
                                      dram["pool_w"].rearrange("g c d -> c g d"), side_ports[2], after=pool_w.free)
            for g, wdw in enumerate(POOL_WINDOWS):
                src, m = upad[:, g, :], [u_marks[g], pad]
                shift, n = 1, 0
                while shift < wdw:
                    dst = win[n % 2]
                    m1 = vcopy(dst[:, 0:shift], src[:, 0:shift], m)
                    m = tt(dst[:, shift:], src[:, shift:], src[:, 0:POOL_PAD + T - shift], ALU.add, m)
                    m = [m, m1]
                    src, shift, n = dst, 2 * shift, n + 1
                s = tmp.take()
                m = ts(s.tile, src[:, POOL_PAD:], 1.0 / wdw, None, ALU.mult, None, m, s.free)
                m = tt(s.tile[:, 0:POOL_PAD], s.tile[:, 0:POOL_PAD],
                       const["pool_edge"][:, g * POOL_PAD:(g + 1) * POOL_PAD], ALU.mult, m)
                m = tt(s.tile, s.tile, upad[:, g, POOL_PAD:], ALU.subtract, m)
                o = psum.take()
                m = mm(o.tile, pool_w.tile[:, g * P:(g + 1) * P], s.tile, after=[m, o.free, pw_mark], marked=True)
                s.release(m)
                mh = fn(h_hi[:, g, :], o.tile, ACT.Identity, m, h_read, scale=col("pool_scale", g))
                mixed[g] = [mh, stt(h_lo[:, g, :], o.tile, col("pool_scale", g), h_hi[:, g, :].bitcast(F32),
                                    ALU.mult, ALU.subtract, mh, h_read)]
                o.release(mixed[g])
            pool_w.release(m)
            join()
            at += 8
            qd, sT, kT = [[carve(at + (2 * i + j) * T, T) for j in range(2)] for i in range(3)]
            lead = [carve(0 + j * T, T) for j in range(2)]
            state = [carve(2 * T + i * P, P) for i in range(2)]
            factor = Ring([Slot(y[:, i, :]) for i in range(CT)])
            head, head_read = {}, {}

            def factors(hd, lv):
                if lv == 0:
                    return None
                half = REC_LEVELS[lv - 1]
                s, s2 = factor.take(), factor.take()
                n = T // (2 * half)
                bl = b[:, hd, :].rearrange("p (n t) -> p n t", t=2 * half)
                m = tt(s.tile.rearrange("p (n t) -> p n t", t=2 * half), bl,
                       bl[:, :, half - 1:half].to_broadcast([P, n, 2 * half]), ALU.subtract, s.free)
                m = fn(s.tile, s.tile, ACT.Abs, m)
                m = fn(s.tile, s.tile, ACT.Exp, m, scale=-1.0)
                qm = ptt(s2.tile, q[:, hd, :], s.tile, ALU.mult, m, s2.free)
                return s, s2, tt(s.tile, k[:, hd, :], s.tile, ALU.mult, m, qm), qm

            def whole_tile(hd):
                j = hd % 2
                bh = b[:, hd, :]
                e_mark = fn(lead[j], bh, ACT.Exp, head_read.get(hd - 2))
                head["qd", hd] = tt(qd[j], q[:, hd, :], lead[j], ALU.mult, e_mark, head_read.get(hd - 2))
                s = tmp.take()
                b3 = bh.rearrange("p (n t) -> p n t", t=P)
                m = tt(s.tile.rearrange("p (n t) -> p n t", t=P), b3[:, :, P - 1:P].to_broadcast([P, TT, P]), b3,
                       ALU.subtract, s.free)
                m = fn(s.tile, s.tile, ACT.Exp, m)
                m = tt(s.tile, k[:, hd, :], s.tile, ALU.mult, m)
                bank = psum.take()
                for tk in range(TT):
                    t_mark = turn(bank.tile[:, tk * P:(tk + 1) * P], s.tile[:, tk * P:(tk + 1) * P],
                                  after=[m, bank.free], marked=True)
                s.release(t_mark)
                head["kT", hd] = acopy(kT[j], bank.tile, t_mark, head_read.get(hd - 2))
                bank.release(head["kT", hd])

            def pairs(hd, lv, got):
                j = hd % 2
                bank = psum.take()
                ql, kl, marks = (q[:, hd, :], k[:, hd, :], []) if lv == 0 else (got[1].tile, got[0].tile, got[2:])
                for tk in range(TT):
                    m = mm(bank.tile[:, tk * P:(tk + 1) * P], kl[:, tk * P:(tk + 1) * P],
                           ql[:, tk * P:(tk + 1) * P], after=[list(marks), bank.free], marked=True)
                mask = rec_masks[:, lv * P:(lv + 1) * P]
                mask = mask.rearrange("p (o t) -> p o t", o=1).to_broadcast([P, TT, P])
                ps3 = bank.tile.rearrange("p (n t) -> p n t", t=P)
                if lv == 0:
                    m = tt(sT[j].rearrange("p (n t) -> p n t", t=P), ps3, mask, ALU.mult, m, head_read.get(hd - 2))
                    bank.release(m)
                else:
                    mk = tt(got[0].tile.rearrange("p (n t) -> p n t", t=P), ps3, mask, ALU.mult, m)
                    bank.release(mk)
                    m2 = ptt(sT[j], sT[j], got[0].tile, ALU.add, mk, head["acc", hd])
                    got[0].release(m2)
                    got[1].release(m)
                    m = m2
                head["acc", hd] = m

            def outputs(hd):
                j = hd % 2
                o = psum.take()
                st_mark = head_read.get(hd - 1)
                for tk in range(TT):
                    cur = slice(tk * P, (tk + 1) * P)
                    vh = v[:, tk, hd * P:(hd + 1) * P]
                    m = mm(o.tile[:, cur], vh, sT[j][:, cur], start=True, stop=(tk == 0),
                           after=[head["acc", hd], o.free], marked=True)
                    if tk:
                        m = mm(o.tile[:, cur], state[(tk - 1) % 2], qd[j][:, cur], start=False, stop=True,
                               after=[st_mark, head["qd", hd]], marked=True)
                    o_read = m
                    if tk < TT - 1:
                        u = psum.take()
                        m = mm(u.tile[:, 0:P], kT[j][:, cur], vh, after=[head["kT", hd], u.free], marked=True)
                        if tk == 0:
                            st_mark = vcopy(state[0], u.tile[:, 0:P], m, st_mark)
                        else:
                            st_mark = stt(state[tk % 2], state[(tk - 1) % 2], lead[j][:, (tk + 1) * P - 1:(tk + 1) * P],
                                          u.tile[:, 0:P], ALU.mult, ALU.add, m, st_mark, o_read)
                        u.release(st_mark)
                s = tmp.take()
                cp = vcopy(s.tile, o.tile, o_read, s.free)
                o.release(cp)
                head_read[hd] = [o_read, st_mark, cp]
                bank, m = square_sum([s.tile], [cp], ones, T)
                rs, m = inverse_root(bank, m, P, NORM_EPS, T)
                m = stt(s.tile, s.tile, col("rec_out_gain"), rs.tile, ALU.mult, ALU.mult, m)
                rs.release(m)
                m = tt(s.tile, s.tile, gate[:, hd, :], ALU.mult, m)
                mixed[4 + hd] = split_to(h_hi[:, 4 + hd, :], h_lo[:, 4 + hd, :], s.tile, m)
                s.release(mixed[4 + hd])

            flying = []

            def land():
                hd, lv, got = flying.pop(0)
                pairs(hd, lv, got)
                if lv == len(REC_LEVELS):
                    outputs(hd)
            for hd in range(REC_HEADS):
                for lv in range(len(REC_LEVELS) + 1):
                    flying.append((hd, lv, factors(hd, lv)))
                    if len(flying) > 2:
                        land()
                    if lv == 1:
                        whole_tile(hd)
            while flying:
                land()
            put_y, y_marks = into(lambda c: y[:, c, :])
            product(w_o, h_tile, mixed, put_y, following=following)
            return add_branch(0, 1, y_marks, x_marks)

        def odd_mixer(x_marks, following):
            w = dram["w_qkv"]
            w_q, w_k, w_v = [Stream(w, n0=i * D, n_cols=D) for i in range(3)]
            w_o = Stream(dram["w_o_att"])
            w_q.ahead(0, None)
            h_marks = pre_norm(1, 0, x_marks)
            join()
            q, k = [carve(i * 4096, 4096).rearrange("p (c t) -> p c t", c=CT) for i in range(2)]
            v = y_buf.rearrange("p (n c) -> p n c", n=TT)
            bias = Ring([Slot(carve(8192 + i * T, T), side_ports[3 + i]) for i in range(2)])
            turned = Ring([Slot(carve(9216 + i * 4 * T, 4 * T).rearrange("p (j t) -> p j t", j=TT)) for i in range(2)])
            probs = Ring([Slot(carve(13312 + i * T, T)) for i in range(4)])
            put_q, q_marks = into(lambda c: q[:, c, :])
            product(w_q, h_tile, h_marks, put_q, following=w_k)
            put_k, k_marks = into(lambda c: k[:, c, :])
            product(w_k, h_tile, h_marks, put_k, following=w_v)
            v_marks = []

            def put_v(tk, n0, ps, m):
                v_marks.append(acopy(v[:, tk, n0:n0 + 256], ps, m))
                return [v_marks[-1]]
            run(token_steps(w_v, h_tile, h_marks, put_v, TT, following=w_o))
            h_read = pe.last()
            mixed, head = {}, {}

            def score(hd, tq):
                c, half = hd // 2, slice(64 * (hd % 2), 64 * (hd % 2) + 64)
                if tq == 0:
                    bs = head["bias", hd] = bias.take()
                    bm = side_queue.move(bs.tile, dram["rel_bias"][hd], bs.port, after=bs.free)
                    bs.ready = [bm, memset(bs.tile[0:CHUNK, T - CHUNK:T], MASK_VALUE, bm)]
                bs = head["bias", hd]
                n = (tq + 1) * P
                sc = psum.take()
                m = mm(sc.tile[:, 0:n], q[half, c, tq * P:(tq + 1) * P], k[half, c, 0:n],
                       after=[q_marks[c], k_marks[c], sc.free], marked=True)
                pr = probs.take()
                m = stt(pr.tile[:, 0:n], sc.tile[:, 0:n], ATT_DIM ** -0.5, bs.tile[:, T - n:T],
                        ALU.mult, ALU.add, m, bs.ready, pr.free)
                sc.release(m)
                if tq == TT - 1:
                    bs.release(m)
                return pr, softmax(pr.tile[:, 0:n], pr.tile[:, 0:n], 1.0, m)[0]

            def spread(hd, tq, pr, m):
                c, half = hd // 2, slice(64 * (hd % 2), 64 * (hd % 2) + 64)
                if tq == 0:
                    head["banks"] = [psum.take() for _ in range(TT)]
                banks = head["banks"]
                for j in range(tq + 1):
                    t_mark = turn(banks[j].tile[:, tq * P:(tq + 1) * P], pr.tile[:, j * P:(j + 1) * P],
                                  after=[m, banks[j].free], marked=True)
                pr.release(t_mark)
                if tq < TT - 1:
                    return
                pt = turned.take()
                cps = []
                for j in range(TT):
                    lane_copy = acopy if j % 2 else vcopy
                    cps.append(lane_copy(pt.tile[:, j, j * P:T], banks[j].tile[:, j * P:T], t_mark, pt.free))
                    banks[j].release(cps[-1])
                o = psum.take()
                for j in range(TT):
                    m = mm(o.tile[0:64, j * P:T], v[:, j, hd * 64:(hd + 1) * 64], pt.tile[:, j, j * P:T],
                           start=(j == 0), stop=(j == TT - 1), after=[cps[j], o.free, v_marks], marked=True)
                mixed[hd] = split_to(h_hi[half, c, :], h_lo[half, c, :], o.tile[0:64, :], m, h_read)
                o.release(mixed[hd])
                pt.release(m)
            flying = []
            for hd in range(ATT_HEADS):
                for tq in range(TT):
                    flying.append((hd, tq, *score(hd, tq)))
                    if len(flying) > 2:
                        spread(*flying.pop(0))
                for _ in range(2):
                    next(modulation_steps, None)
            for f in flying:
                spread(*f)
            put_y, y_marks = into(lambda c: y[:, c, :])
            product(w_o, h_tile, [[mixed[2 * c], mixed[2 * c + 1]] for c in range(CT)], put_y, following=following)
            return add_branch(1, 1, y_marks, x_marks)

        modulation_mark = []

        def modulate():
            g = scalars[:, 4:4 + 2 * CT]
            c_in = columns[:, COLUMN_AT["c_2"]:COLUMN_AT["c_2"] + CT]
            m = fn(g[:, 0:CT], c_in, ACT.Sigmoid)
            m = tt(g[:, CT:2 * CT], g[:, 0:CT], c_in, ALU.mult, m)
            pe.wait(m)
            for n0 in range(0, 6 * D, 256):
                s = fetch(dram["cond_w"], 0, n0, 256)
                wt = s.tile.rearrange("p (a n) -> p a n", a=CT)
                bank = psum.take()
                pe.wait(s.ready, bank.free)
                for c in range(2):
                    for a in range(CT):
                        last = mm(bank.tile[:, c:c + 1], wt[:, a, c * P:(c + 1) * P], g[:, CT + a:CT + a + 1],
                                  start=(a == 0), stop=(a == CT - 1), marked=(c == 1 and a == CT - 1))
                s.release(last)
                j = n0 // P
                b0 = COLUMN_AT["cond_b_2"] + j
                m = tt(mod[:, j:j + 2], bank.tile[:, 0:2], columns[:, b0:b0 + 2], ALU.add, last)
                bank.release(m)
                yield
            ts(scale_1[:, 0:8], mod[:, 8:16], 1.0, None, ALU.add, None, m)
            modulation_mark.append(ts(scale_1[:, 8:16], mod[:, 32:40], 1.0, None, ALU.add, None, m))

        def ada_norm(x_marks, which, mod_mark):
            xs, hs = [x[:, c, :] for c in range(CT)], [y[:, c, :] for c in range(CT)]
            cm = center(xs, x_marks, ones, D, hs)
            bank, m = square_sum(hs, cm, ones, T)
            r, m = inverse_root(bank, m, D, LN_EPS, T)
            marks = []
            for c in range(CT):
                m2 = stt(hs[c], hs[c], scale_1[:, 8 * which + c:8 * which + c + 1], r.tile, ALU.mult, ALU.mult,
                         m, mod_mark)
                m3 = fn(hs[c], hs[c], ACT.Identity, m2, bias=mod[:, 24 * which + c:24 * which + c + 1])
                marks.append(split_to(h_hi[:, c, :], h_lo[:, c, :], hs[c], m3))
            r.release(m2)
            return marks

        def close_block(x_marks, y_marks, which, gain, shift, mod_mark):
            xs, ys = [x[:, c, :] for c in range(CT)], [y[:, c, :] for c in range(CT)]
            marks = []
            for c in range(CT):
                g = mod[:, 24 * which + 16 + c:24 * which + 17 + c]
                m = ts(ys[c], ys[c], g, None, ALU.mult, None, y_marks[c], mod_mark)
                marks.append(stt(xs[c], xs[c], ALPHA, ys[c], ALU.mult, ALU.add, m, x_marks[c]))
            cm = center(xs, marks, ones, D, xs)
            bank, m = square_sum(xs, cm, ones, T)
            r, m = inverse_root(bank, m, D, LN_EPS, T)
            out_marks = []
            for c in range(CT):
                m2 = stt(xs[c], xs[c], col(gain, c), r.tile, ALU.mult, ALU.mult, m)
                out_marks.append(fn(xs[c], xs[c], ACT.Identity, m2, bias=col(shift, c)))
            r.release(m2)
            return out_marks

        def rw_mixer(h_marks, streams):
            NPT = 14
            CP = CONV_K - 1
            at = NPT * (T + 1)

            p = carve(0, NPT * (T + 1)).rearrange("p (c t) -> p c t", c=NPT)
            upad = carve(at, 4 * (CP + T)).rearrange("p (c t) -> p c t", c=4)
            conv = carve(at + 4 * (CP + T), 4 * T).rearrange("p (c t) -> p c t", c=4)
            pad = [memset(upad[:, :, 0:CP], 0.0), memset(p[:, :, 0:1], 0.0)]
            w_a, w_b, w_p = streams
            a_marks, u_marks = {}, {}

            def put_a(c, ps, m):
                a_marks[c] = vcopy(upad[:, c, CP:], ps, m)
                return [a_marks[c]]
            product(w_a, h_tile, h_marks, put_a, following=w_b)

            def put_b(c, ps, m):
                s = tmp.take()
                m = fn(s.tile, ps, ACT.Sigmoid, m, s.free)
                u_marks[c] = tt(upad[:, c, CP:], upad[:, c, CP:], s.tile, ALU.mult, m, a_marks[c])
                s.release(u_marks[c])
                return [m]
            product(w_b, h_tile, h_marks, put_b, following=w_p)
            p_marks = {}
            cv = [None] * 4

            def convolve():
                for tap in range(CONV_K):
                    for c in range(4):
                        src = upad[:, c, tap:tap + T]
                        wc = col("conv_w_2", tap * 4 + c)
                        if tap == 0:
                            cv[c] = ts(conv[:, c, :], src, wc, col("conv_b_2", c), ALU.mult, ALU.add, u_marks[c], pad)
                        else:
                            cv[c] = stt(conv[:, c, :], src, wc, conv[:, c, :], ALU.mult, ALU.add, cv[c])
                    yield
            taps = convolve()

            def put_p(c, ps, m):
                p_marks[c] = acopy(p[:, c, 1:], ps, m)
                for _ in range(2):
                    next(taps, None)
                return [p_marks[c]]
            low_on["pool"] = 2
            product(w_p, h_tile, h_marks, put_p)
            low_on["pool"] = 1
            h_read = pe.last()
            mixed = {}
            mixed_p = {}
            for c in range(NPT):
                s = tmp.take()
                m = tt(s.tile, p[:, c, 0:T], p[:, c, 1:], ALU.subtract, p_marks[c], pad, s.free)
                mixed_p[c] = stt(p[:, c, 1:], s.tile, col("mu_shift_2", c), p[:, c, 1:], ALU.mult, ALU.add, m)
                s.release(mixed_p[c])
            run(taps)
            cs = [conv[:, c, :] for c in range(4)]
            cv = center(cs, cv, ones, 512, cs)
            bank, m = square_sum(cs, cv, ones, T)
            r, m = inverse_root(bank, m, 512, LN_EPS, T)
            for c in range(4):
                m2 = stt(cs[c], cs[c], col("conv_ln_g_2", c), r.tile, ALU.mult, ALU.mult, m)
                m2 = ts(cs[c], cs[c], col("conv_ln_b_2", c), None, ALU.add, None, m2)
                s = tmp.take()
                m3 = fn(s.tile, cs[c], ACT.Sigmoid, m2, s.free)
                m3 = tt(s.tile, cs[c], s.tile, ALU.mult, m3)
                mixed[c] = split_to(h_hi[:, c, :], h_lo[:, c, :], s.tile, m3, h_read)
                s.release(mixed[c])
            r.release(m2)
            join()
            space["split_ctx"].close()
            space["split_ctx"] = ExitStack()
            extra = space["split_ctx"].enter_context(nc.sbuf_tensor("rw_extra", [P, 4 * CHUNK_WORDS], F32))[:, :]

            inv_at = at + 4 * 4 * T
            rw_masks = extra[:, 6144:6144 + 15 * 64]
            keep_chunk = extra[:, 7168:7168 + T]
            M_T, RK_T, RB_T = [extra[:, i * 4 * T:(i + 1) * 4 * T].rearrange("p (c n) -> p c n", c=4) for i in range(3)]
            lora, g2 = extra[:, 0:T], extra[:, T:2 * T]
            lm = [side_queue.move(lora, dram["lora"], side_ports[5]), side_queue.move(g2, dram["rw_g2"], side_ports[6])]
            mask_mark = [side_queue.move(rw_masks, dram["rw_masks"], side_ports[7]),
                         side_queue.move(keep_chunk, dram["keep_chunk"], side_ports[8])]
            dve.wait(mask_mark)
            r_t, k_t, v_t = [[p[:, 4 * i + c, 1:] for c in range(4)] for i in range(3)]
            wd, ad, gd = p[0:64, 12, 1:], p[64:128, 12, 1:], p[:, 13, 1:]
            wm = fn(wd, wd, ACT.Tanh, mixed_p[12])
            gm = fn(gd, gd, ACT.Sigmoid, mixed_p[13])
            a_hat = carve(at, 4 * T).rearrange("p (c t) -> p c t", c=4)
            tok = carve(at + 4 * T, 3 * 4 * T).rearrange("p (k n c) -> p k n c", k=3, n=TT)
            v_tok, k_tok, b_tok = tok[:, 0], tok[:, 1], tok[:, 2]
            Y = p[:, 4:8, 1:]
            gate = y_buf[:, 0:4 * T].rearrange("p (c t) -> p c t", c=4)
            bonus = y_buf[:, 4 * T:8 * T].rearrange("p (c t) -> p c t", c=4)
            n_ch = T // RW_CHUNK
            ready = {}
            for c in range(4):
                cs_ = slice(c * P, (c + 1) * P)
                lw, kk, aa = [tmp.take() for _ in range(3)]
                bank = psum.take()
                m = mm(bank.tile, lora[0:64, cs_], wd, after=[lm, wm, bank.free], marked=True)
                m = fn(lw.tile, bank.tile, ACT.Sigmoid, m, lw.free, bias=col("rw_w0_2", c))
                bank.release(m)
                lw_mark = ts(lw.tile, lw.tile, -math.exp(-0.5), None, ALU.mult, None, m)
                bank = psum.take()
                m = mm(bank.tile, lora[64:128, cs_], ad, after=[lm, mixed_p[12], bank.free], marked=True)
                a_mark = fn(aa.tile, bank.tile, ACT.Sigmoid, m, aa.free, bias=col("rw_a0_2", c))
                bank.release(a_mark)
                bank = psum.take()
                m = mm(bank.tile, g2[:, cs_], gd, after=[lm, gm, bank.free], marked=True)
                g_mark = acopy(gate[:, c, :], bank.tile, m)
                bank.release(g_mark)
                m = ts(kk.tile, k_t[c], col("rw_kk_2", c), None, ALU.mult, None, mixed_p[4 + c], kk.free)
                bank, sm = square_sum([kk.tile], [m], head_ones, T)
                nrm = tmp.take()
                m = fn(nrm.tile, bank.tile, ACT.Sqrt, sm, nrm.free)
                bank.release(m)
                m = ts(nrm.tile, nrm.tile, 1e-12, None, ALU.max, None, m)
                m = recip(nrm.tile, nrm.tile, m)
                kk_mark = tt(kk.tile, kk.tile, nrm.tile, ALU.mult, m)
                m = ts(nrm.tile, aa.tile, 1.0, col("rw_ka_2", c), ALU.subtract, ALU.mult, kk_mark, a_mark)
                k_mark = stt(k_t[c], nrm.tile, 1.0, k_t[c], ALU.add, ALU.mult, m)
                m = stt(nrm.tile, r_t[c], col("rw_rk_2", c), k_t[c], ALU.mult, ALU.mult, k_mark, mixed_p[c])
                bank, m = channel_sum([nrm.tile], [m], head_ones, T)
                bonus_mark = tt(bonus[:, c, :], bank.tile, v_t[c], ALU.mult, m, mixed_p[8 + c])
                bank.release(bonus_mark)
                bank = psum.take()
                for tk in range(TT):
                    m = turn(bank.tile[:, tk * P:(tk + 1) * P], v_t[c][:, tk * P:(tk + 1) * P],
                             after=[mixed_p[8 + c], bank.free], marked=True)
                v_read = m
                v_mark = acopy(v_tok[:, :, cs_], bank.tile.rearrange("p (n c) -> p n c", n=TT), m)
                bank.release(v_mark)
                total = tmp.take()
                dve.wait(lw_mark, total.free)
                m = dve.mark(nc.vector.tensor_tensor_scan(
                    out=total.tile, data0=keep_chunk, data1=lw.tile, initial=0.0,
                    op0=ALU.mult, op1=ALU.add))
                m1 = tt(lw.tile, total.tile, lw.tile, ALU.subtract, m)
                before = fn(lw.tile, lw.tile, ACT.Exp, m1)
                pm = fn(nrm.tile, total.tile, ACT.Exp, m, bonus_mark)
                ahat_mark = tt(a_hat[:, c, :], kk.tile, lw.tile, ALU.mult, before, kk_mark)
                r_mark = tt(r_t[c], r_t[c], nrm.tile, ALU.mult, pm, bonus_mark)
                ed_mark = vcopy(end_decay[:, c * n_ch:(c + 1) * n_ch],
                                nrm.tile.rearrange("p (n t) -> p n t", t=RW_CHUNK)[:, :, RW_CHUNK - 1], pm)
                im = fn(total.tile, total.tile, ACT.Exp, m1, pm, scale=-1.0)
                khat_mark = tt(k_t[c], k_t[c], total.tile, ALU.mult, im)
                m = stt(aa.tile, kk.tile, -1.0, aa.tile, ALU.mult, ALU.mult, a_mark, kk_mark)
                b_mark = tt(v_t[c], aa.tile, total.tile, ALU.mult, m, im, v_read, bonus_mark)
                lw.release(ahat_mark)
                kk.release(m)
                aa.release(b_mark)
                total.release(b_mark)
                nrm.release(ed_mark)
                for src, dst, mk in ((k_t[c], k_tok, khat_mark), (v_t[c], b_tok, b_mark)):
                    bank = psum.take()
                    for tk in range(TT):
                        m = turn(bank.tile[:, tk * P:(tk + 1) * P], src[:, tk * P:(tk + 1) * P],
                                 after=[mk, bank.free], marked=True)
                    m = acopy(dst[:, :, cs_], bank.tile.rearrange("p (n c) -> p n c", n=TT), m)
                    bank.release(m)
                ready[c] = [ahat_mark, khat_mark, b_mark, r_mark]
            b_hat = v_t
            rm = rw_masks.rearrange("p (k t) -> p k t", t=64)

            def wide(mask):
                return rm[:, mask:mask + 1, :].to_broadcast([P, 8, 64])

            def blocks(ap):
                return ap.rearrange("p (n t) -> p n t", t=64)

            def each():
                for hh in range(2):
                    for ch in range(n_ch):
                        yield hh, ch, slice(64 * (ch % 2), 64 * (ch % 2) + 64), \
                            slice((hh * TT + ch // 2) * 64, (hh * TT + ch // 2) * 64 + 64)

            def gram(rows, cols_, c, evacuate):
                marks = []
                for hh in range(2):
                    bank = psum.take()
                    pe.wait(bank.free, ready[c])
                    hs_ = slice(64 * hh, 64 * hh + 64)
                    for ch in range(n_ch):
                        part, cc = slice(64 * (ch % 2), 64 * (ch % 2) + 64), slice(ch // 2 * 64, ch // 2 * 64 + 64)
                        tsl = slice(ch * 64, ch * 64 + 64)
                        m = mm(bank.tile[part, cc], rows[hs_, tsl], cols_[hs_, tsl], marked=(ch == n_ch - 1))
                    marks.append(evacuate(slice(hh * 4 * 64, (hh + 1) * 4 * 64), bank.tile[:, 0:256], m))
                    bank.release(marks[-1])
                return marks

            def small_products(lhs, rhs, *after):
                bank = psum.take()
                pe.wait(bank.free, *after)
                for hh, ch, part, cc in each():
                    m = mm(bank.tile[part, cc], lhs[part, cc], rhs(part, cc, hh, ch // 2),
                           marked=(hh == 1 and ch == n_ch - 1))
                return bank, m

            def plain(ap):
                return lambda part, cc, hh, tk: ap[part, cc]

            y_inv = {}
            kept = {}
            for c in range(4):
                for rows, cols_, mask, dst in ((k_t[c], a_hat[:, c, :], 0, M_T), (k_t[c], r_t[c], 1, RK_T),
                                               (b_hat[c], r_t[c], 1, RB_T)):
                    tri = rm[:, mask:mask + 1, :].to_broadcast([P, 4, 64])
                    gram(rows, cols_, c, lambda cc, ps, m: tt(blocks(dst[:, c, cc]), blocks(ps), tri, ALU.mult, m))
            gram_read = pe.last()
            for pair in range(2):
                n_, l_ = [[carve(inv_at + (k3 * 2 + i) * T, T) for i in range(2)] for k3 in range(2)]
                x_ = [b_hat[2 * pair + i] for i in range(2)]
                xm, nm, lm_, ym = {}, {}, {}, {}
                for i in range(2):
                    c = 2 * pair + i
                    nm[i] = gram(b_hat[c], a_hat[:, c, :], c,
                                 lambda cc, ps, m: acopy(n_[i][:, cc], ps, m, kept.get(i)))
                    lm_[i] = gram(a_hat[:, c, :], b_hat[c], c,
                                  lambda cc, ps, m: acopy(l_[i][:, cc], ps, m, kept.get(i)))
                    m = tt(blocks(Y[:, c, :]), blocks(n_[i]), wide(3), ALU.mult, nm[i], gram_read)
                    ym[i] = tt(blocks(Y[:, c, :]), blocks(Y[:, c, :]), wide(2), ALU.add, m)
                    m = tt(blocks(x_[i]), blocks(l_[i]), wide(3 + len(RW_LEVELS)), ALU.mult, lm_[i], nm[i])
                    xm[i] = tt(blocks(x_[i]), blocks(x_[i]), wide(2), ALU.add, m)
                for lv in range(1, len(RW_LEVELS)):
                    for i in range(2):
                        c = 2 * pair + i
                        s1, s2 = tmp.take(), tmp.take()
                        m1 = tt(blocks(s1.tile), blocks(l_[i]), wide(3 + len(RW_LEVELS) + lv), ALU.mult, s1.free)
                        m2 = tt(blocks(s2.tile), blocks(n_[i]), wide(3 + lv), ALU.mult, s2.free)
                        b1, p1 = small_products(s1.tile, plain(Y[:, c, :]), m1, ym[i])
                        b2, p2 = small_products(s2.tile, plain(x_[i]), m2, xm[i])
                        e1 = acopy(s1.tile, b1.tile, p1)
                        b1.release(e1)
                        e2 = acopy(s2.tile, b2.tile, p2)
                        b2.release(e2)
                        b1, p1 = small_products(x_[i], plain(s1.tile), e1)
                        b2, p2 = small_products(Y[:, c, :], plain(s2.tile), e2)
                        s1.release(p1)
                        s2.release(p2)
                        ym[i] = tt(Y[:, c, :], Y[:, c, :], b1.tile, ALU.add, p1, p2)
                        b1.release(ym[i])
                        xm[i] = tt(x_[i], x_[i], b2.tile, ALU.add, p2, p1)
                        b2.release(xm[i])
                for i in range(2):
                    c = 2 * pair + i
                    kept[i] = [ym[i], xm[i]]
                    s1, s2 = tmp.take(), tmp.take()
                    bank, m = small_products(M_T[:, c, :], lambda part, cc, hh, tk:
                                             v_tok[part, tk, c * P + hh * 64:c * P + hh * 64 + 64])
                    e = acopy(s1.tile, bank.tile, m, s1.free)
                    bank.release(e)
                    bank, m = small_products(Y[:, c, :], plain(s1.tile), e, ym[i])
                    e = acopy(M_T[:, c, :], bank.tile, m)
                    bank.release(e)
                    s1.release(m)
                    bank = psum.take()
                    for tk in range(TT):
                        m = turn(bank.tile[:, tk * P:(tk + 1) * P], a_hat[:, c, tk * P:(tk + 1) * P],
                                 after=[bank.free], marked=True)
                    e = acopy(s2.tile, bank.tile, m, s2.free)
                    bank.release(e)
                    for odd in range(2):
                        bank = psum.take()
                        part = slice(64 * odd, 64 * odd + 64)
                        pe.wait(bank.free, e)
                        for hh in range(2):
                            for tk in range(TT):
                                o = slice(64 * hh, 64 * hh + 64)
                                m = mm(bank.tile[o, tk * 64:(tk + 1) * 64],
                                       s2.tile[part, tk * P + hh * 64:tk * P + hh * 64 + 64],
                                       Y[part, c, (hh * TT + tk) * 64:(hh * TT + tk) * 64 + 64],
                                       marked=(hh == 1 and tk == TT - 1))
                        w2 = a_hat[:, c, :].rearrange("p (n o t) -> p n o t", o=2, t=64)[:, :, odd, :]
                        e2 = acopy(w2, bank.tile[:, 0:256].rearrange("p (n t) -> p n t", t=64), m)
                        bank.release(e2)
                    s2.release(m)
            join()
            st = [carve(inv_at + i * 256, 256).rearrange("p (c v) -> p c v", c=4) for i in range(2)]
            uus = [carve(inv_at + 512 + i * T, T) for i in range(2)]
            out_rw = a_hat
            st_mark = memset(st[0], 0.0)
            u_read = [None, None]
            for ch in range(n_ch):
                part, tk = slice(64 * (ch % 2), 64 * (ch % 2) + 64), ch // 2
                tsl = slice(ch * 64, ch * 64 + 64)
                old, new = st[ch % 2], st[(ch + 1) % 2]
                uu = uus[ch % 2]

                def heads():
                    for hd in range(RW_HEADS):
                        c, hh = hd // 2, hd % 2
                        yield hd, c, slice(64 * hh, 64 * hh + 64), slice(hd * 64, hd * 64 + 64), \
                            slice((hh * TT + tk) * 64, (hh * TT + tk) * 64 + 64)
                um = []
                for hh in range(2):
                    bank = psum.take()
                    pe.wait(bank.free, st_mark)
                    hp = slice(64 * hh, 64 * hh + 64)
                    for c in range(4):
                        m = mm(bank.tile[part, c * 64:(c + 1) * 64], a_hat[hp, c, tsl], old[hp, c, :], marked=(c == 3))
                    u4 = uu[part, :].rearrange("p (c o v) -> p c o v", c=4, o=2)[:, :, hh, :]
                    um.append(tt(u4, bank.tile[part, 0:256].rearrange("p (c v) -> p c v", c=4),
                                 M_T[part, :, (hh * TT + tk) * 64:(hh * TT + tk) * 64 + 64], ALU.add, m,
                                 u_read[ch % 2]))
                    bank.release(um[-1])
                bank = psum.take()
                pe.wait(bank.free, um)
                for hd, c, hp, hv, cc in heads():
                    o = bank.tile[hp, c * 64:(c + 1) * 64]
                    mm(o, k_tok[part, tk, hv], v_tok[part, tk, hv], start=True, stop=False)
                    m = mm(o, b_tok[part, tk, hv], uu[part, hv], start=False, stop=True, marked=(hd == RW_HEADS - 1))
                b3 = bank.tile[:, 0:256].rearrange("p (c v) -> p c v", c=4)
                hm = tt(new, old, b3, ALU.add, m, st_mark)
                bank.release(hm)
                ed = end_decay[:, :].rearrange("p (c n) -> p c n", c=4)[:, :, ch:ch + 1].to_broadcast([P, 4, 64])
                st_new = tt(new, new, ed, ALU.mult, hm)
                bank, bank2 = psum.take(), psum.take()
                pe.wait(bank.free, bank2.free)
                for hd, c, hp, hv, cc in heads():
                    m1 = mm(bank.tile[hp, c * 64:(c + 1) * 64], old[hp, c, :], r_t[c][hp, tsl],
                            marked=(hd == RW_HEADS - 1))
                for hd, c, hp, hv, cc in heads():
                    o = bank2.tile[hp, c * 64:(c + 1) * 64]
                    mm(o, v_tok[part, tk, hv], RK_T[part, c, cc], start=True, stop=False)
                    m = mm(o, uu[part, hv], RB_T[part, c, cc], start=False, stop=True, marked=(hd == RW_HEADS - 1))
                u_read[ch % 2] = m
                yc_ = out_rw[:, :, tsl]
                ym_ = acopy(yc_, bank.tile[:, 0:256].rearrange("p (c v) -> p c v", c=4), m1)
                bank.release(ym_)
                ym_ = tt(yc_, yc_, bank2.tile[:, 0:256].rearrange("p (c v) -> p c v", c=4), ALU.add, m, ym_)
                bank2.release(ym_)
                st_mark = [st_new, m]
            for c in range(4):
                yc = [out_rw[:, c, :]]
                cm = center(yc, [ym_], head_ones, 64, yc)
                bank, m = square_sum(yc, cm, head_ones, T)
                r, m = inverse_root(bank, m, 64, GN_EPS, T)
                m = stt(yc[0], yc[0], col("rw_lnx_g_2", c), r.tile, ALU.mult, ALU.mult, m)
                r.release(m)
                m = stt(yc[0], yc[0], col("rw_lnx_b_2", c), bonus[:, c, :], ALU.add, ALU.add, m)
                m = tt(yc[0], yc[0], gate[:, c, :], ALU.mult, m)
                mixed[4 + c] = split_to(h_hi[:, 4 + c, :], h_lo[:, 4 + c, :], yc[0], m, h_read)
            join()
            space["split_ctx"].close()
            space["arena_ctx"].close()
            open_split("split_3")
            open_arena("arena_3")
            put_y, y_marks = into(lambda c: y[:, c, :])
            product(Stream(dram["w_out"]), h_tile, mixed, put_y)
            return y_marks

        def peer(h_marks, w_query):
            join()
            NQ = 2 * PEER_HEADS
            HK = PEER_HEADS * TOPK
            n_groups = NKEYS // GROUP
            q = carve(0, NQ * T).rearrange("p (c t) -> p c t", c=NQ)
            works = [carve(8192 + i * 2048, 2048) for i in range(2)]
            keys = [carve(12288 + i * 1024, 1024) for i in range(2)]
            at = 14336
            top_v = carve(at, NQ * TOPK).rearrange("p (g k) -> p g k", g=NQ)
            top_i = carve(at + 256, NQ * TOPK).rearrange("p (g k) -> p g k", g=NQ)
            idx = carve(at + 512, 256).bitcast(U32)
            best_v = carve(at + 768, HK)
            parts = carve(at + 896, HK * 3)
            half_f = carve(at + 1280, 2 * HK)
            total = carve(at + 1536, 8)
            turned = carve(at + 1544, 3 * T).rearrange("p (k t) -> p k t", k=3)
            km = [side_queue.move(keys[i], dram[f"peer_k{i + 1}"], side_ports[7 + i]) for i in range(2)]
            w_in = [Stream(dram["peer_u"], n0=g * GROUP * P, n_cols=GROUP * P) for g in range(n_groups)]
            w_outs = [Stream(dram["peer_v"], k0=g * GROUP * P, width=512) for g in range(n_groups)]
            put_q, q_marks = into(lambda c: q[:, c, :])
            product(w_query, h_tile, h_marks, put_q, following=w_in[0])
            counter = const["counter"]
            early = Ring([Slot(y[:, c, :], early_ports[c]) for c in range(CT)])
            early_marks = {}

            def early_steps():
                for g in range(EARLY_GROUPS):
                    def put(c, ps, m, g=g):
                        s = early.take()
                        m = fn(s.tile, ps, ACT.Gelu, m, s.free)
                        s.release(weight_queue.move(early_table[g * GROUP + c], s.tile, s.port, after=[m]))
                        early_marks[g, c] = s.free[0]
                        return [m]
                    yield from product_steps(w_in[g], h_tile, h_marks, put,
                                             following=w_in[g + 1] if g + 1 < EARLY_GROUPS else None)
            ahead = early_steps()
            low_on["pool"] = 2

            def fill(n):
                for _ in range(n):
                    next(ahead, None)
            prev, work_free = [], [None, None]

            def top16(src, vals, inds, *after):
                dve.wait(*after)
                m = dve.mark(nc.vector.max(vals[:, 0:8], src))
                dve.wait(m)
                m = dve.mark(nc.vector.max_index(inds[:, 0:8], vals[:, 0:8], src))
                dve.wait(m)
                m = dve.mark(nc.vector.match_replace(src, vals[:, 0:8], src, LOWEST))
                dve.wait(m)
                m = dve.mark(nc.vector.max(vals[:, 8:16], src))
                dve.wait(m)
                return dve.mark(nc.vector.max_index(inds[:, 8:16], vals[:, 8:16], src))

            def scores(tk):
                sc = works[tk % 2].rearrange("p (g n) -> p g n", g=NQ)
                s_marks = []
                for g4 in range(NQ // 4):
                    bank = psum.take()
                    pe.wait(bank.free, km)
                    for j in range(4):
                        g = g4 * 4 + j
                        m = mm(bank.tile[:, j * P:(j + 1) * P], q[:, g, tk * P:(tk + 1) * P],
                               keys[g % 2][:, (g // 2) * P:(g // 2 + 1) * P], after=[q_marks[g]], marked=(j == 3))
                    cp = acopy(sc[:, g4 * 4:g4 * 4 + 4, :], bank.tile.rearrange("p (g n) -> p g n", g=4), m,
                               work_free[tk % 2])
                    bank.release(cp)
                    s_marks.append(cp)
                return s_marks
            s_marks = scores(0)
            for tk in range(TT):
                work = works[tk % 2]
                sc = work.rearrange("p (g n) -> p g n", g=NQ)
                m = prev
                for g in range(NQ):
                    m1 = top16(sc[:, g, :], top_v[:, g, :], idx[:, g * TOPK:(g + 1) * TOPK], s_marks[g // 4], m)
                    if g % 4 == 3:
                        fill(1)
                m = vcopy(top_i.rearrange("p g k -> p (g k)"), idx, m1)
                if tk < TT - 1:
                    s_marks = scores(tk + 1)
                cand = work.rearrange("p (h n) -> p h n", h=PEER_HEADS)
                tv = top_v.rearrange("p (h s) k -> p h s k", s=2)
                c4 = cand.rearrange("p h (i j) -> p h i j", i=TOPK)
                for hd in range(PEER_HEADS):
                    m2 = tt(c4[:, hd], tv[:, hd, 0, :].unsqueeze(2).to_broadcast([P, TOPK, TOPK]),
                            tv[:, hd, 1, :].unsqueeze(1).to_broadcast([P, TOPK, TOPK]), ALU.add, m)
                for hd in range(PEER_HEADS):
                    m3 = top16(cand[:, hd, :], best_v[:, hd * TOPK:(hd + 1) * TOPK],
                               idx[:, hd * TOPK:(hd + 1) * TOPK], m2)
                    if hd % 2:
                        fill(1)
                ci = idx[:, 0:HK]
                m_hi = ts(idx[:, HK:2 * HK], ci, 4, None, ALU.logical_shift_right, None, m3)
                m_a = vcopy(half_f[:, 0:HK], idx[:, HK:2 * HK], m_hi)
                m_lo = ts(idx[:, HK:2 * HK], ci, 15, None, ALU.bitwise_and, None, m_a)
                m_b = vcopy(half_f[:, HK:2 * HK], idx[:, HK:2 * HK], m_lo)
                pk = work.rearrange("p (n i) -> p n i", i=TOPK)
                ti = top_i.rearrange("p (h s) k -> p h s k", s=2)
                m = m_b
                for side in range(2):
                    place = half_f[:, side * HK:(side + 1) * HK].unsqueeze(2).to_broadcast([P, HK, TOPK])
                    count = counter[:, 0:TOPK].unsqueeze(1).to_broadcast([P, HK, TOPK])
                    m = tt(pk, place, count, ALU.is_equal, m, prev)
                    for hd in range(PEER_HEADS):
                        pv = pk[:, hd * TOPK:(hd + 1) * TOPK, :]
                        m4 = tt(pv, pv, ti[:, hd, side, :].unsqueeze(1).to_broadcast([P, TOPK, TOPK]), ALU.mult, m)
                    m = reduce(parts[:, side * HK:(side + 1) * HK], pk, ALU.add, m4)
                    fill(1)
                work_free[tk % 2] = m
                b3 = best_v.rearrange("p (h k) -> p h k", h=PEER_HEADS)
                g3 = parts[:, 2 * HK:3 * HK].rearrange("p (h k) -> p h k", h=PEER_HEADS)
                m = tt(g3, b3, b3[:, :, 0:1].to_broadcast([P, PEER_HEADS, TOPK]), ALU.subtract, m)
                m = fn(g3, g3, ACT.Exp, m)
                m = reduce(total, g3, ALU.add, m)
                m = recip(total, total, m)
                m = tt(g3, g3, total.unsqueeze(2).to_broadcast([P, PEER_HEADS, TOPK]), ALU.mult, m)
                bank = psum.take()
                for j in range(3):
                    mt = turn(bank.tile[:, j * P:(j + 1) * P], parts[:, j * HK:(j + 1) * HK],
                              after=[m, bank.free], marked=True)
                cp = acopy(turned[:, :, tk * P:(tk + 1) * P],
                           bank.tile[:, 0:3 * P].rearrange("p (k t) -> p k t", k=3), mt)
                bank.release(cp)
                prev = [cp, m1]
            join()
            stages = Ring([Slot(carve(i * 4096, 4096).rearrange("p (a t) -> p a t", t=STAGE_TOKENS), side_ports[9 + i])
                           for i in range(2)])
            hots = Ring([Slot(carve(8192 + i * 256, 256)) for i in range(24)])
            table_marks = []
            batch = 0
            for block in range(T // STAGE_TOKENS):
                sg = stages.take()
                for t4 in range(0, STAGE_TOKENS, 4):
                    bank = psum.take()
                    pe.wait(bank.free)
                    for j in range(4):
                        t = block * STAGE_TOKENS + t4 + j
                        hot = hots.take()
                        key2, key1 = hot.tile[:, 0:P], hot.tile[:, P:2 * P]
                        m = ts(key2, counter[:, :], turned[:, 1, t:t + 1], None, ALU.is_equal, None, hot.free)
                        m = ts(key1, counter[:, :], turned[:, 0, t:t + 1], turned[:, 2, t:t + 1],
                               ALU.is_equal, ALU.mult, hot.free)
                        m = mm(bank.tile[:, j * P:(j + 1) * P], key2, key1, after=[m], marked=True)
                        hot.release(m)
                    cp = acopy(sg.tile[:, :, t4:t4 + 4], bank.tile.rearrange("p (t a) -> p a t", t=4), m, sg.free)
                    bank.release(cp)
                    batch += 1
                    if batch % 4 == 0:
                        fill(1)
                wr = weight_queue.move(gate_table[block], sg.tile.rearrange("p a t -> p (a t)"), sg.port, after=[cp])
                sg.release(wr)
                table_marks.append(wr)
            run(ahead)
            low_on["pool"] = 1
            join()
            for lane in (dve, act, pool):
                lane.wait(table_marks)
            open_hidden("experts", 2 * 4096)
            gates = Ring([Slot(carve(i * 2048, 2048).rearrange("p (b a t) -> p b a t", a=GROUP, t=STAGE_TOKENS),
                               side_ports[7 + i]) for i in range(2)])
            lates = Ring([Slot(carve(4096 + i * 2048, 2048).rearrange("p (c t) -> p c t", t=T), side_ports[1 + i])
                          for i in range(2)])
            for s in gates.slots + lates.slots:
                s.free = table_marks[:]
            space["h_marks"], space["y_free"] = h_marks, [early_marks[k_] for k_ in early_marks]
            order = list(range(EARLY_GROUPS, n_groups)) + list(range(EARLY_GROUPS))
            held = {}

            def make(n, c, ps, m, hi, lo, free):
                g = order[n]
                if c == 0:
                    gt = gates.take()
                    held["gate"] = gt
                    gt.ready = side_queue.move(gt.tile.rearrange("p b a t -> p b (a t)"),
                                               gate_table.rearrange("b p n -> p b n")
                                               [:, :, g * GROUP * STAGE_TOKENS:(g + 1) * GROUP * STAGE_TOKENS],
                                               gt.port, after=[gt.free, table_marks])
                    if ps is None:
                        lt = lates.take()
                        held["late"] = lt
                        lt.ready = side_queue.move(lt.tile, early_table[g * GROUP:(g + 1) * GROUP]
                                                   .rearrange("c p t -> p c t"), lt.port,
                                                   after=[lt.free, [early_marks[g, c_] for c_ in range(GROUP)]])
                gt = held["gate"]
                s = tmp.take()
                if ps is None:
                    src, sm = held["late"].tile[:, c, :], held["late"].ready
                else:
                    src, sm = s.tile, fn(s.tile, ps, ACT.Gelu, m, s.free)
                blocks_ = "p (b t) -> p b t"
                q_ = tt(s.tile.rearrange(blocks_, t=STAGE_TOKENS), src.rearrange(blocks_, t=STAGE_TOKENS),
                        gt.tile[:, :, c, :], ALU.mult, sm, gt.ready, s.free)
                marks = split_to(hi, lo, s.tile, q_, free)
                s.release(marks)
                if c == GROUP - 1:
                    gt.release(q_)
                    if ps is None:
                        held["late"].release(q_)
                return marks, [sm] if ps is not None else []

            def first(n):
                if n >= n_groups or order[n] < EARLY_GROUPS:
                    return None, None
                return w_in[order[n]], (w_outs[order[n - 1]] if n else first(1)[0] or w_outs[order[0]])
            return grouped_product(n_groups, first, lambda n: w_outs[order[n]], make, None)

        mem_raw = carve(2048, CT * M).rearrange("p (c t) -> p c t", c=CT)
        mem_in = side_queue.move(mem_raw, dram["mem"].rearrange("(c p) t -> p c t", p=P), side_ports[11])
        mem_out = Ring([Slot(carve(i * 256, 256), side_ports[5 + i]) for i in range(4)])
        mem_marks = rms_split([mem_raw[:, c, :] for c in range(CT)], [mem_in] * CT, lambda i: col("mem_norm_gain", i),
                              n=M)
        for l in range(2):
            run(memory_keys_steps(l, mem_marks, None))
        join()
        for lane in (dve, act, pool):
            lane.wait([s.free for s in mem_out.slots])
        modulation_steps = modulate()
        xm = [x_in] * CT
        xm = even_mixer(xm, None)
        xm = memory_attention(0, xm, None)
        xm = mlp(0, xm, None)
        xm = odd_mixer(xm, None)
        xm = memory_attention(1, xm, None)
        xm = mlp(1, xm, None)
        run(modulation_steps)
        mod_mark = modulation_mark[0]
        w_in_streams = [Stream(dram["w_in"], n0=n0, n_cols=n) for n0, n in ((0, 512), (512, 512), (1024, 1792))]
        w_in_streams[0].ahead(0, None)
        hm = ada_norm(xm, 0, mod_mark)
        join()
        ym = rw_mixer(hm, w_in_streams)
        xm = close_block(xm, ym, 0, "ln1_g_2", "ln1_b_2", mod_mark)
        w_query = Stream(dram["peer_wq"])
        w_query.ahead(0, None)
        hm = ada_norm(xm, 1, mod_mark)
        ym = peer(hm, w_query)
        xm = close_block(xm, ym, 1, "ln2_g_2", "ln2_b_2", mod_mark)
        done = weight_queue.move(out.rearrange("(c p) t -> p c t", p=P), x, out_port, after=[xm])
        sp.wait(done)
        for prt in side_ports + early_ports:
            if prt.count:
                sp.wait((prt.sem, prt.count))


def layouts(i):
    a = {k: np.asarray(v) for k, v in i.items()}
    cols = [a[n].reshape(-1, P).T for n, _ in COLUMNS]
    p_, u_ = np.arange(P)[:, None], np.arange(T)[None, :]
    dist = np.clip(p_ + T - P - u_, -REL_CLIP, REL_CLIP) + REL_CLIP
    out = {
        "columns": np.concatenate(cols, axis=1),
        "x": a["x"][0].T, "mem": a["mem"][0].T,
        "w_in_ab": a["w_in_ab"][0], "pool_w": a["pool_w"][0], "w_out_ab": a["w_out_ab"][0],
        "w_qkv": a["w_qkv"][0], "rel_bias": a["rel_bias"][0][:, dist], "w_o_att": a["w_o_att"][0],
        "w_mem_q": a["w_mem_q"], "w_mem_kv": a["w_mem_kv"], "w_mem_o": a["w_mem_o"],
        "w_ff1": a["w_ff1"], "w_ff2": a["w_ff2"],
        "cond_w": a["cond_w_2"], "w_in": a["w_in_2"], "w_out": a["w_out_2"],
        "lora": np.concatenate([a["rw_w2_2"], a["rw_a2_2"]], axis=0), "rw_g2": a["rw_g2_2"],
        "peer_wq": a["peer_wq_2"],
        "peer_k1": a["peer_k1_2"].transpose(2, 0, 1).reshape(P, -1),
        "peer_k2": a["peer_k2_2"].transpose(2, 0, 1).reshape(P, -1),
        "peer_u": a["peer_u_2"].T, "peer_v": a["peer_v_2"],
    }
    out.update(shape_constants())
    return {k: np.ascontiguousarray(v) for k, v in out.items()}


def kernel(**inputs):
    import concourse.bacc as bacc
    from concourse.bass_utils import run_bass_kernel_spmd
    arrays = layouts(inputs)
    nc = bacc.Bacc("TRN2", target_bir_lowering=False, num_devices=1)
    dram = {k: nc.dram_tensor(f"in_{k}", v.shape, F32, kind="ExternalInput").ap() for k, v in arrays.items()}
    scratch = [nc.dram_tensor(k, shape, F32, kind="Internal").ap() for k, shape in SCRATCH.items()]
    out = nc.dram_tensor("out", (D, T), F32, kind="ExternalOutput").ap()
    build(nc, dram, out, *scratch)
    r = run_bass_kernel_spmd(nc, [{f"in_{k}": v for k, v in arrays.items()}], core_ids=[0])
    return np.ascontiguousarray(r.results[0]["out"].T)[None]
```

```python
from contextlib import ExitStack
import math

import numpy as np
import concourse.bass as bass
import concourse.mybir as mybir
from concourse.alu_op_type import AluOpType as ALU

ACT = mybir.ActivationFunctionType
F32 = mybir.dt.float32
F32R = mybir.dt.float32r
U32 = mybir.dt.uint32
AX = mybir.AxisListType

P = 128
T = 512
D = 1024
CT = D // P
TT = T // P
M = 256
FF = 4 * D
NORM_EPS = 1e-6
LN_EPS = 1e-5
GN_EPS = 64e-5
GATE_CLIP = 60.0
POOL_WINDOWS = (2, 4, 8, 16)
POOL_PAD = max(POOL_WINDOWS)
REC_HEADS = 4
ATT_HEADS = 16
ATT_DIM = D // ATT_HEADS
CHUNK = 64
REL_CLIP = 256
MEM_HEADS = 4
MEM_TILES = CT // MEM_HEADS
CONV_K = 31
RW_CHUNK = 64
RW_HEADS = 8
RW_LEVELS = (1, 2, 4, 8, 16, 32)
REC_LEVELS = (1, 2, 4, 8, 16, 32, 64)
PEER_HEADS = 8
NKEYS = 128
TOPK = 16
ALPHA = 2.0 ** 0.25
MASK_VALUE = -1e30
ARENA = 18176
LOWEST = -3.0e38
CHUNK_WORDS = 2048
GROUP = 4
STAGE_TOKENS = 32
EARLY_GROUPS = 18

COLUMNS = [
    ("norm_gains", 96), ("mem_norm_gain", 8), ("pool_scale", 4), ("rec_lb_logits", 4), ("rec_out_gain", 1),
    ("c_2", 8), ("cond_b_2", 48), ("mu_shift_2", 14), ("conv_w_2", 4 * CONV_K), ("conv_b_2", 4),
    ("conv_ln_g_2", 4), ("conv_ln_b_2", 4), ("rw_w0_2", 4), ("rw_a0_2", 4), ("rw_kk_2", 4), ("rw_ka_2", 4),
    ("rw_rk_2", 4), ("rw_lnx_g_2", 4), ("rw_lnx_b_2", 4), ("ln1_g_2", 8), ("ln1_b_2", 8), ("ln2_g_2", 8),
    ("ln2_b_2", 8),
]
COLUMN_AT = {}
for _name, _n in COLUMNS:
    COLUMN_AT[_name] = sum(n for _, n in COLUMNS[:len(COLUMN_AT)])
N_COLUMNS = sum(n for _, n in COLUMNS)


SCRATCH = {
    "gate_table": (T // STAGE_TOKENS, NKEYS, NKEYS * STAGE_TOKENS),
    "early_table": (EARLY_GROUPS * GROUP, P, T),
    "memory_k": (2, CT, P, M),
    "memory_v": (2, M // P, P, D),
}


def shape_constants():
    i = np.arange(P)
    out = {"identity": np.eye(P), "ones": np.ones((P, P)), "head_ones": (i[:, None] // 64 == i[None, :] // 64)}

    def level(s, t, m):
        return (s // (2 * m) == t // (2 * m)) & (s % (2 * m) < m) & (t % (2 * m) >= m)

    s, t = i[:, None], i[None, :]
    out["rec_masks"] = np.concatenate([s == t] + [level(s, t, m) for m in REC_LEVELS], axis=1)
    s, t = (i % 64)[:, None], np.arange(64)[None, :]
    out["rw_masks"] = np.concatenate(
        [s < t, s <= t, s == t] + [level(s, t, m) for m in RW_LEVELS] + [level(t, s, m) for m in RW_LEVELS], axis=1)
    pos = np.arange(T)[None, :]
    out["keep_tile"] = np.repeat(pos % P != 0, P, axis=0)
    out["keep_chunk"] = np.repeat(pos % RW_CHUNK != 0, P, axis=0)
    out["counter"] = np.repeat(np.arange(P)[None, :], P, axis=0)
    out["pool_edge"] = np.repeat(np.concatenate(
        [w / np.minimum(np.arange(1, POOL_PAD + 1), w) for w in POOL_WINDOWS])[None, :], P, axis=0)
    return {k: np.ascontiguousarray(v.astype(np.float32)) for k, v in out.items()}


SCORES_AHEAD = 4
STAGE_CONSTANTS = ("rec_masks", "rw_masks", "keep_tile", "keep_chunk")
CONSTANT_WIDTHS = {k: v.shape[1] for k, v in shape_constants().items()}


def flat(marks):
    for m in marks:
        if isinstance(m, tuple) and len(m) == 2 and isinstance(m[1], int):
            yield m
        elif m is not None:
            yield from flat(m)


class Lane:

    def __init__(self, eng, sem):
        self.eng, self.sem, self.count, self.waited = eng, sem, 0, {}

    def wait(self, *marks):
        for sem, value in flat(marks):
            if self.waited.get(sem.name, 0) < value:
                self.eng.wait_ge(sem, value)
                self.waited[sem.name] = value

    def mark(self, ins):
        ins.then_inc(self.sem, 1)
        self.count += 1
        return (self.sem, self.count)

    def last(self):
        return (self.sem, self.count) if self.count else None


class Queue:

    def __init__(self, eng, lane):
        self.eng, self.lane = eng, lane

    def move(self, out, in_, port, after=()):
        self.lane.wait(*after)
        self.eng.dma_start(out, in_).then_inc(port.sem, 16)
        port.count += 16
        return (port.sem, port.count)


class Port:

    def __init__(self, sem):
        self.sem, self.count = sem, 0


class Slot:
    def __init__(self, tile, port=None):
        self.tile, self.port, self.free, self.held = tile, port, [], False

    def release(self, *marks):
        self.free, self.held = list(marks), False


class Ring:

    def __init__(self, slots):
        self.slots, self.n = slots, 0

    def take(self):
        assert not all(s.held for s in self.slots), "a ring's buffer is taken before one was released"
        while self.slots[self.n % len(self.slots)].held:
            self.n += 1
        s = self.slots[self.n % len(self.slots)]
        self.n += 1
        s.held = True
        return s


def build(nc, dram, out, gate_table, early_table, memory_k, memory_v):
    ctx = ExitStack()
    with ctx:
        def sb(name, cols, dt=F32):
            return ctx.enter_context(nc.sbuf_tensor(name, [P, cols], dt))

        def sem(name):
            return ctx.enter_context(nc.semaphore(name))

        pe = Lane(nc.tensor, sem("pe_done"))
        dve = Lane(nc.vector, sem("dve_done"))
        act = Lane(nc.scalar, sem("act_done"))
        pool = Lane(nc.gpsimd, sem("pool_done"))
        sp = Lane(nc.sync, sem("sp_done"))
        weight_queue = Queue(nc.sync, sp)
        side_queue = Queue(nc.gpsimd, pool)

        x = sb("residual", CT * T)[:, :].rearrange("p (c t) -> p c t", c=CT)
        h_hi = sb("normed_high", CT * T, F32R)[:, :].rearrange("p (c t) -> p c t", c=CT)
        h_lo = sb("normed_low", CT * T, F32R)[:, :].rearrange("p (c t) -> p c t", c=CT)
        y_buf = sb("branch", CT * T)[:, :]
        y = y_buf.rearrange("p (c t) -> p c t", c=CT)
        columns = sb("columns", N_COLUMNS)
        const = {k: sb("const_" + k, n) for k, n in CONSTANT_WIDTHS.items() if k not in STAGE_CONSTANTS}
        tmp = Ring([Slot(sb(f"tmp{i}", T)[:, :]) for i in range(6)])
        small = Ring([Slot(sb(f"small{i}", 4)[:, :]) for i in range(8)])
        scalars = sb("scalars", 4 + 2 * CT)
        mod = sb("modulation", 48)
        scale_1 = sb("one_plus_scale", 16)
        end_decay = sb("chunk_decay", 4 * T // RW_CHUNK)
        raw = Ring([Slot(sb(f"weights{i}", CHUNK_WORDS)[:, :], Port(sem(f"weights_landed{i}"))) for i in range(3)])
        space = {}

        def open_split(name):
            ctx_ = space["split_ctx"] = ExitStack()
            space["split"] = Ring([Slot([ctx_.enter_context(nc.sbuf_tensor(f"{name}_{part}{i}", [P, CHUNK_WORDS], F32R))
                                         [:, :] for part in ("high", "low")]) for i in range(2)])

        def open_arena(name, width=ARENA):
            ctx_ = space["arena_ctx"] = ExitStack()
            space["arena"] = ctx_.enter_context(nc.sbuf_tensor(name, [P, width], F32))[:, :]
            space["width"] = width

        ctx.callback(lambda: space["split_ctx"].close())
        ctx.callback(lambda: space["arena_ctx"].close())
        open_split("split")
        open_arena("arena")
        psum = Ring([Slot(ctx.enter_context(nc.psum_tensor(f"bank{i}", [P, 512], F32))[:, :]) for i in range(8)])
        side_ports = [Port(sem(f"side{i}")) for i in range(12)]
        early_ports = [Port(sem(f"early_written{i}")) for i in range(CT)]
        mem_port = Port(sem("memory_landed"))
        out_port = Port(sem("out_written"))

        def carve(at, n):
            assert at + n <= space["width"]
            return space["arena"][:, at:at + n]

        def col(name, i=0):
            j = COLUMN_AT[name] + i
            return columns[:, j:j + 1]

        def tt(o, a, b, op, *after):
            dve.wait(*after)
            return dve.mark(nc.vector.tensor_tensor(o, a, b, op))

        def ts(o, a, s1, s2, op0, op1, *after):
            dve.wait(*after)
            if op1 is None:
                return dve.mark(nc.vector.tensor_scalar(o, a, s1, None, op0))
            return dve.mark(nc.vector.tensor_scalar(o, a, s1, s2, op0, op1))

        def stt(o, a, s, b, op0, op1, *after):
            dve.wait(*after)
            return dve.mark(nc.vector.scalar_tensor_tensor(out=o, in0=a, scalar=s, in1=b, op0=op0, op1=op1))

        def vcopy(o, a, *after):
            dve.wait(*after)
            return dve.mark(nc.vector.tensor_copy(o, a))

        def recip(o, a, *after):
            dve.wait(*after)
            return dve.mark(nc.vector.reciprocal(o, a))

        def memset(o, value, *after):
            dve.wait(*after)
            return dve.mark(nc.vector.memset(o, value))

        def reduce(o, a, op, *after):
            dve.wait(*after)
            return dve.mark(nc.vector.tensor_reduce(o, a, AX.X, op))

        def fn(o, a, func, *after, **kw):
            act.wait(*after)
            return act.mark(nc.scalar.activation(o, a, func, **kw))

        def acopy(o, a, *after):
            act.wait(*after)
            return act.mark(nc.scalar.copy(o, a))

        def ptt(o, a, b, op, *after):
            pool.wait(*after)
            return pool.mark(nc.gpsimd.tensor_tensor(o, a, b, op))

        def mm(o, lhsT, rhs, start=True, stop=True, after=(), marked=False):
            pe.wait(*after)
            ins = nc.tensor.matmul(o, lhsT, rhs, start=start, stop=stop)
            return pe.mark(ins) if marked else None

        def turn(o, a, after=(), marked=False):
            pe.wait(*after)
            n = a.shape[0]
            ins = nc.tensor.transpose(o, a, const["identity"][0:n, 0:n])
            return pe.mark(ins) if marked else None

        def join():
            marks = [lane.last() for lane in (pe, dve, act, pool)]
            for lane in (pe, dve, act, pool):
                lane.wait(*marks)

        port = side_ports[0]
        mem_raw = carve(2048, CT * M).rearrange("p (c t) -> p c t", c=CT)
        mem_in = weight_queue.move(mem_raw, dram["mem"].rearrange("(c p) t -> p c t", p=P), mem_port)
        const_mark = [side_queue.move(columns[:, :], dram["columns"], port)]
        for k in const:
            const_mark = [side_queue.move(const[k][:, :], dram[k], port)]
        x_in = side_queue.move(x, dram["x"].rearrange("(c p) t -> p c t", p=P), side_ports[1])
        for lane in (pe, dve, act, pool):
            lane.wait(const_mark)
        ones, head_ones = const["ones"][:, :], const["head_ones"][:, :]
        eps_of = {}
        for i, value in enumerate((NORM_EPS, LN_EPS, GN_EPS, 1.0)):
            m = memset(scalars[:, i:i + 1], value)
            eps_of[value] = scalars[:, i:i + 1]
        act.wait(m)
        one = eps_of[1.0]

        def fetch(w, k0, n0, width):
            s = raw.take()
            n_k = CHUNK_WORDS // width
            s.ready = weight_queue.move(s.tile.rearrange("p (a n) -> p a n", a=n_k),
                                        w[k0:k0 + n_k * P, n0:n0 + width].rearrange("(a p) n -> p a n", p=P),
                                        s.port, after=s.free)
            return s

        low_on = {"pool": 1}

        def split_chunk(w, k0, n0, width):
            s = fetch(w, k0, n0, width)
            d = space["split"].take()
            hi, lo = d.tile
            half = CHUNK_WORDS // 2
            marks = []
            for i in range(2):
                cut_ = slice(i * half, (i + 1) * half)
                mh = acopy(hi[:, cut_], s.tile[:, cut_], s.ready, d.free)
                op = ptt if i < low_on["pool"] else tt
                marks += [mh, op(lo[:, cut_], s.tile[:, cut_], hi[:, cut_].bitcast(F32), ALU.subtract, mh, d.free)]
            s.release(*marks)
            d.ready = [marks[0:2], marks[2:4]]
            d.parts = [part.rearrange("p (a n) -> p a n", n=width) for part in (hi, lo)]
            return d

        class Stream:

            def __init__(self, w, k0=0, n0=0, n_cols=None, width=256):
                n_cols = w.shape[1] if n_cols is None else n_cols
                self.specs = [(w, k0, n, width) for n in range(n0, n0 + n_cols, width)]
                self.split = []

            def ahead(self, i, following):
                if i < len(self.specs):
                    if i == len(self.split):
                        self.split.append(split_chunk(*self.specs[i]))
                elif following is not None and not following.split:
                    following.ahead(0, None)

        def triple(o, a_parts, b_parts, first, last, marked):
            (ah, al), (bh, bl) = a_parts, b_parts
            mm(o, ah, bh, start=first, stop=False)
            mm(o, ah, bl, start=False, stop=False)
            return mm(o, al, bh, start=False, stop=last, marked=marked)

        def product_steps(stream, rhs, ready, evacuate, width_out=T, following=None):
            stream.ahead(0, None)
            c_all = 0
            for i, (_, _, _, width) in enumerate(stream.specs):
                d = stream.split[i]
                n_k = CHUNK_WORDS // width
                stream.ahead(i + 1, following)
                for c in range(width // P):
                    bank = psum.take()
                    pe.wait(d.ready, bank.free)
                    for a in range(n_k):
                        pe.wait(ready[a])
                        m = triple(bank.tile[:, 0:width_out], [w_[:, a, c * P:(c + 1) * P] for w_ in d.parts], rhs(a),
                                   a == 0, a == n_k - 1, a == n_k - 1)
                    if c == width // P - 1:
                        d.release(m)
                    bank.release(*evacuate(c_all, bank.tile[:, 0:width_out], m))
                    c_all += 1
                    yield

        def token_steps(stream, lhs, ready, evacuate, n_token_tiles, following=None):
            stream.ahead(0, None)
            for i, (_, _, n0, width) in enumerate(stream.specs):
                d = stream.split[i]
                stream.ahead(i + 1, following)
                for tk in range(n_token_tiles):
                    bank = psum.take()
                    pe.wait(d.ready, bank.free)
                    for a in range(CT):
                        pe.wait(ready[a])
                        m = triple(bank.tile[:, 0:width], [l_[:, tk * P:(tk + 1) * P] for l_ in lhs(a)],
                                   [w_[:, a, :] for w_ in d.parts], a == 0, a == CT - 1, a == CT - 1)
                    if tk == n_token_tiles - 1:
                        d.release(m)
                    bank.release(*evacuate(tk, n0 - stream.specs[0][2], bank.tile[:, 0:width], m))
                    yield

        def run(steps):
            for _ in steps:
                pass

        def product(*args, **kw):
            run(product_steps(*args, **kw))

        def into(dst):
            marks = {}

            def evacuate(c, ps, m):
                marks[c] = acopy(dst(c), ps, m) if c % 2 else vcopy(dst(c), ps, m)
                return [marks[c]]
            return evacuate, marks

        def split_to(hi, lo, src, *after):
            m = acopy(hi, src, *after)
            return [m, tt(lo, src, hi.bitcast(F32), ALU.subtract, m, *after)]

        def channel_sum(tiles, ready, matrix, n):
            bank = psum.take()
            pe.wait(bank.free)
            for i, tile in enumerate(tiles):
                m = mm(bank.tile[:, 0:n], matrix, tile, start=(i == 0), stop=(i == len(tiles) - 1),
                       after=[ready[i]], marked=True)
            return bank, m

        class SquareSum:

            def __init__(self, matrix, n, count):
                self.matrix, self.n, self.count, self.added, self.late = matrix, n, count, 0, []
                self.bank = psum.take()

            def add(self, tile, *ready):
                s = tmp.take()
                self.late.append((s, fn(s.tile[:, 0:self.n], tile, ACT.Square, s.free, ready)))
                if len(self.late) > 1:
                    self.sum_one()

            def sum_one(self):
                s, q = self.late.pop(0)
                m = mm(self.bank.tile[:, 0:self.n], self.matrix, s.tile[:, 0:self.n], start=(self.added == 0),
                       stop=(self.added == self.count - 1), after=[q, self.bank.free], marked=True)
                self.added += 1
                s.release(m)
                return m

            def result(self):
                while self.late:
                    m = self.sum_one()
                return self.bank, m

        def square_sum(tiles, ready, matrix, n):
            sums = SquareSum(matrix, n, len(tiles))
            for i, tile in enumerate(tiles):
                sums.add(tile, ready[i])
            return sums.result()

        def inverse_root(bank, mark, count, eps, n):
            warm = small.take()
            warm.release(fn(warm.tile[:, 0:1], one, ACT.Ln, warm.free))
            s = tmp.take()
            m = fn(s.tile[:, 0:n], bank.tile[:, 0:n], ACT.Ln, s.free, mark, scale=1.0 / count, bias=eps_of[eps])
            bank.release(m)
            m = fn(s.tile[:, 0:n], s.tile[:, 0:n], ACT.Exp, m, scale=-0.5)
            return s, m

        def center(tiles, ready, matrix, count, outs):
            bank, m = channel_sum(tiles, ready, matrix, T)
            marks = [stt(o, bank.tile, -1.0 / count, t, ALU.mult, ALU.add, m) for t, o in zip(tiles, outs)]
            bank.release(marks[-1])
            return marks

        def with_squares(marks, sums, tile):
            def evacuate(c, ps, m):
                marks[c] = vcopy(tile(c), ps, m)
                sums.add(tile(c), marks[c])
                return [marks[c]]
            return evacuate

        def add_branch(l, n, y_marks, x_marks, y_sums, more):
            bank, m = y_sums.result()
            r, rm = inverse_root(bank, m, D, NORM_EPS, T)
            sums = SquareSum(ones, T, CT) if more else None
            marks = [None] * CT
            order = [2, 0, 1, 5, 3, 4, 6, 7]
            for c in order:
                yt, g = y[:, c, :], col("norm_gains", (6 * l + n) * CT + c)
                if c in (2, 5):
                    m = fn(yt, yt, ACT.Identity, y_marks[c], scale=g)
                    m = ptt(yt, yt, r.tile, ALU.mult, m, rm)
                    pool_read = m
                    marks[c] = ptt(x[:, c, :], x[:, c, :], yt, ALU.add, m, x_marks[c])
                else:
                    m = stt(yt, yt, g, r.tile, ALU.mult, ALU.mult, rm, y_marks[c])
                    marks[c] = tt(x[:, c, :], x[:, c, :], yt, ALU.add, m, x_marks[c])
                    dve_read = m
            r.release(dve_read, pool_read)
            if more:
                for c in (0, 1, 2, 3, 4, 6, 5, 7):
                    sums.add(x[:, c, :], marks[c])
            space["x_sums"] = sums
            return marks

        def rms_split(tiles, ready, gain, n=T):
            sums = space.pop("x_sums", None)
            if sums is None:
                bank, m = square_sum(tiles, ready, ones, n)
            else:
                bank, m = sums.result()
            r, rm = inverse_root(bank, m, D, NORM_EPS, n)
            marks = []
            for i, t in enumerate(tiles):
                q, hi, lo = y[:, i, 0:n], h_hi[:, i, 0:n], h_lo[:, i, 0:n]
                m = stt(q, t, gain(i), r.tile[:, 0:n], ALU.mult, ALU.mult, rm, ready[i])
                mh = acopy(hi, q, m)
                lower = ptt if i in (1, 4, 6) else tt
                marks.append([mh, lower(lo, q, hi.bitcast(F32), ALU.subtract, mh)])
            r.release(m)
            return marks

        def pre_norm(l, n, x_marks):
            return rms_split([x[:, c, :] for c in range(CT)], x_marks,
                             lambda i: col("norm_gains", (6 * l + n) * CT + i))

        def h_tile(k):
            return h_hi[:, k, :], h_lo[:, k, :]

        def softmax(src, out_ap, scale, *after):
            s = small.take()
            mx, total = s.tile[:, 0:1], s.tile[:, 1:2]
            m = reduce(mx, src, ALU.max, s.free, after)
            m = ts(mx, mx, -scale, None, ALU.mult, None, m)
            exp_mark = fn(out_ap, src, ACT.Exp, m, after, scale=scale, bias=mx, accum_out=total)

            def divide():
                m = recip(total, total, exp_mark)
                m = ts(out_ap, out_ap, total, None, ALU.mult, None, m)
                s.release(m)
                return m
            return exp_mark, divide

        memory_marks = {}

        def memory_keys_steps(l, following):
            marks = memory_marks[l] = []

            def mem_tile(a):
                return h_hi[:, a, 0:M], h_lo[:, a, 0:M]

            def keep(dst, ps, m, width):
                s = mem_out.take()
                cp = acopy(s.tile[:, 0:width], ps, m, s.free)
                s.release(side_queue.move(dst, s.tile[:, 0:width], s.port, after=[cp]))
                marks.append(s.free[0])
                return [cp]
            values = Stream(dram["w_mem_kv"][l], n0=D, n_cols=D)
            keys = Stream(dram["w_mem_kv"][l], n_cols=D)
            keys.ahead(0, None)
            yield
            mem_marks = memory_marks["ready"]
            yield from product_steps(keys, mem_tile, mem_marks,
                                     lambda c, ps, m: keep(memory_k[l, c], ps, m, M), width_out=M, following=values)
            yield from token_steps(values, mem_tile, mem_marks,
                                   lambda tk, n0, ps, m: keep(memory_v[l, tk][:, n0:n0 + 256], ps, m, 256), M // P,
                                   following=following)

        def memory_attention(l, x_marks, following):
            w_o = Stream(dram["w_mem_o"][l])
            w_q = Stream(dram["w_mem_q"][l])
            w_q.ahead(0, None)
            h_marks = pre_norm(l, 2, x_marks)
            join()
            q = carve(0, CT * T).rearrange("p (c t) -> p c t", c=CT)
            k = carve(4096, CT * M).rearrange("p (c t) -> p c t", c=CT)
            v = carve(6144, 2 * D).rearrange("p (m c) -> p m c", m=2)
            probs = Ring([Slot(carve(8192 + i * M, M)) for i in range(4)])
            turned = Ring([Slot(carve(9216 + i * 2 * T, 2 * T).rearrange("p (m t) -> p m t", m=2)) for i in range(2)])
            kv_mark = [side_queue.move(k, memory_k[l].rearrange("c p t -> p c t"), side_ports[1], after=memory_marks[l]),
                       side_queue.move(v, memory_v[l].rearrange("m p c -> p m c"), side_ports[11],
                                       after=memory_marks[l])]
            put_q, q_marks = into(lambda c: q[:, c, :])
            product(w_q, h_tile, h_marks, put_q, following=w_o)
            q_read = pe.last()
            mixed = {}
            head = {}

            def score(hd, tq):
                sc = psum.take()
                pe.wait(sc.free, kv_mark)
                for j in range(MEM_TILES):
                    c = hd * MEM_TILES + j
                    m = mm(sc.tile[:, 0:M], q[:, c, tq * P:(tq + 1) * P], k[:, c, :], start=(j == 0),
                           stop=(j == MEM_TILES - 1), after=[q_marks[c]], marked=True)
                pr = probs.take()
                m, divide = softmax(sc.tile[:, 0:M], pr.tile, (D // MEM_HEADS) ** -0.5, m, pr.free)
                sc.release(m)
                return pr, divide

            def spread(hd, tq, pr, m):
                if tq == 0:
                    head["banks"] = [psum.take() for _ in range(2)]
                banks = head["banks"]
                for mt in range(2):
                    t_mark = turn(banks[mt].tile[:, tq * P:(tq + 1) * P], pr.tile[:, mt * P:(mt + 1) * P],
                                  after=[m, banks[mt].free], marked=True)
                pr.release(t_mark)
                if tq < TT - 1:
                    return
                pt = turned.take()
                turned_marks = []
                for mt in range(2):
                    cp = acopy(pt.tile[:, mt, :], banks[mt].tile, t_mark, pt.free)
                    banks[mt].release(cp)
                    turned_marks.append(cp)
                for j in range(MEM_TILES):
                    c = hd * MEM_TILES + j
                    o = psum.take()
                    pe.wait(o.free, turned_marks)
                    for mt in range(2):
                        m = mm(o.tile, v[:, mt, c * P:(c + 1) * P], pt.tile[:, mt, :], start=(mt == 0),
                               stop=(mt == 1), marked=True)
                    mixed[c] = split_to(h_hi[:, c, :], h_lo[:, c, :], o.tile, m, q_read)
                    o.release(mixed[c])
                pt.release(m)
            items = [(hd, tq) for hd in range(MEM_HEADS) for tq in range(TT)]
            flying = []
            for item in items:
                flying.append([*item, *score(*item)])
                if len(flying) > 1:
                    flying[-2][3] = flying[-2][3]()
                if len(flying) > 2:
                    spread(*flying.pop(0))
            flying[-1][3] = flying[-1][3]()
            for f in flying:
                spread(*f)
            y_marks, y_sums = {}, SquareSum(ones, T, CT)
            put_y = with_squares(y_marks, y_sums, lambda c: y[:, c, :])
            product(w_o, h_tile, mixed, put_y, following=following)
            return add_branch(l, 3, y_marks, x_marks, y_sums, True)

        def grouped_product(n_groups, first, second, make, following, on_y=lambda c, m: None):
            parts = Ring([Slot([space["hidden"][i][j] for j in range(2)]) for i in range(2)])
            y_marks, flying = [None] * CT, {}

            def one(g):
                slot, marks = parts.take(), {}
                hi, lo = slot.tile
                st, nxt = first(g)
                if st is None:
                    for c in range(GROUP):
                        marks[c], _ = make(g, c, None, None, hi[:, c, :], lo[:, c, :], slot.free)
                else:
                    def put(c, ps, m):
                        marks[c], read = make(g, c, ps, m, hi[:, c, :], lo[:, c, :], slot.free)
                        return read
                    product(st, h_tile, space["h_marks"], put, following=nxt)
                flying[g] = (slot, marks)

            def two(g, nxt):
                slot, marks = flying.pop(g)
                hi, lo = slot.tile

                def put(c, ps, m):
                    if g == 0:
                        y_marks[c] = vcopy(y[:, c, :], ps, m, space["y_free"])
                    else:
                        y_marks[c] = tt(y[:, c, :], y[:, c, :], ps, ALU.add, m, y_marks[c])
                    if g == n_groups - 1:
                        on_y(c, y_marks[c])
                    return [y_marks[c]]
                product(second(g), lambda k: (hi[:, k, :], lo[:, k, :]), marks, put, following=nxt)
                slot.release(pe.last())
            for g in range(n_groups):
                one(g)
                if g:
                    two(g - 1, first(g + 1)[0] if g + 1 < n_groups and first(g + 1)[0] else second(g))
            two(n_groups - 1, following)
            return y_marks

        def open_hidden(name, rest):
            space["arena_ctx"].close()
            c_ = ExitStack()
            space["hidden"] = [[c_.enter_context(nc.sbuf_tensor(f"{name}_{part}{i}", [P, GROUP * T], F32R))[:, :]
                                .rearrange("p (c t) -> p c t", c=GROUP) for part in ("high", "low")] for i in range(2)]
            space["arena"] = c_.enter_context(nc.sbuf_tensor(f"{name}_arena", [P, rest], F32))[:, :] if rest else None
            space["width"] = rest
            space["arena_ctx"] = c_

        def mlp(l, x_marks, following):
            w1 = [Stream(dram["w_ff1"][l], n0=g * GROUP * P, n_cols=GROUP * P) for g in range(FF // P // GROUP)]
            w2 = [Stream(dram["w_ff2"][l], k0=g * GROUP * P, width=512) for g in range(FF // P // GROUP)]
            w1[0].ahead(0, None)
            h_marks = pre_norm(l, 4, x_marks)
            join()
            open_hidden(f"hidden{l}", 0)
            space["h_marks"], space["y_free"] = h_marks, None

            def make(g, c, ps, m, hi, lo, free):
                s = tmp.take()
                m = fn(s.tile, ps, ACT.Relu, m, s.free)
                q = tt(s.tile, s.tile, s.tile, ALU.mult, m)
                marks = split_to(hi, lo, s.tile, q, free)
                s.release(marks)
                next(modulation_steps, None)
                return marks, [m]
            n = len(w1)
            y_sums = []

            def on_y(c, m):
                if not y_sums:
                    y_sums.append(SquareSum(ones, T, CT))
                y_sums[0].add(y[:, c, :], m)
            y_marks = grouped_product(n, lambda g: (w1[g], w2[g - 1] if g else w1[1]), lambda g: w2[g], make, following,
                                      on_y)
            x_marks = add_branch(l, 5, y_marks, x_marks, y_sums[0], l == 0)
            join()
            space["arena_ctx"].close()
            if l == 0:
                open_arena("arena_1")
            else:
                space["split_ctx"].close()
                open_arena("arena_2")
                open_split("split_2")
            return x_marks

        def even_mixer(x_marks, following):
            w = dram["w_in_ab"]
            w_u, w_q, w_f, w_i, w_g = [Stream(w, n0=i * 512, n_cols=512) for i in range(5)]
            w_o = Stream(dram["w_out_ab"])
            w_u.ahead(0, None)
            h_marks = pre_norm(0, 0, x_marks)
            join()
            masks_at = ARENA - 8 * P
            rec_masks, keep_tile = carve(masks_at, 8 * P), carve(masks_at - T, T)
            mask_mark = [side_queue.move(rec_masks, dram["rec_masks"], side_ports[3]),
                         side_queue.move(keep_tile, dram["keep_tile"], side_ports[4])]
            upad = carve(0, 4 * (POOL_PAD + T)).rearrange("p (g t) -> p g t", g=4)
            at = 4 * (POOL_PAD + T)
            q, k, b, v, gate = [carve(at + i * 4 * T, 4 * T).rearrange("p (g t) -> p g t", g=4) for i in range(5)]
            at += 5 * 4 * T
            win = [carve(at + i * (POOL_PAD + T), POOL_PAD + T) for i in range(2)]
            lb = carve(at + 2 * (POOL_PAD + T), 8)
            u_marks = {}
            pad = memset(upad[:, :, 0:POOL_PAD], 0.0)

            def put_u(c, ps, m):
                u_marks[c] = vcopy(upad[:, c, POOL_PAD:], ps, m)
                return [u_marks[c]]
            product(w_u, h_tile, h_marks, put_u, following=w_q)
            put_q, q_marks = into(lambda c: q[:, c, :])
            product(w_q, h_tile, h_marks, put_q, following=w_f)
            logit = columns[:, COLUMN_AT["rec_lb_logits"]:COLUMN_AT["rec_lb_logits"] + 4]
            m = tt(lb[:, 0:4], logit, logit, ALU.subtract)
            m = fn(lb[:, 0:4], lb[:, 0:4], ACT.Exp, m)
            m2 = recip(lb[:, 4:8], lb[:, 0:4], m)
            m = tt(lb[:, 0:4], lb[:, 0:4], lb[:, 4:8], ALU.mult, m2)
            m = tt(lb[:, 0:4], lb[:, 0:4], lb[:, 0:4], ALU.subtract, m)
            m = ts(lb[:, 0:4], lb[:, 0:4], 0.0, 1.0, ALU.max, ALU.min, m)
            lb_mark = ts(lb[:, 4:8], lb[:, 0:4], -1.0, 1.0, ALU.mult, ALU.add, m)
            b_marks, k_marks = {}, {}

            def put_f(c, ps, m):
                f, e, g = tmp.take(), tmp.take(), tmp.take()
                fm = ts(f.tile, ps, GATE_CLIP, -GATE_CLIP, ALU.min, ALU.max, m, f.free)
                km = fn(k[:, c, :], f.tile, ACT.Sigmoid, fm, scale=-1.0)
                k_marks[c] = ts(k[:, c, :], k[:, c, :], lb[:, 4 + c:5 + c], None, ALU.mult, None, km, lb_mark)
                em = fn(e.tile, f.tile, ACT.Abs, e.free, fm)
                em = fn(e.tile, e.tile, ACT.Exp, em, scale=-1.0)
                em = fn(e.tile, e.tile, ACT.Ln, em, bias=one)
                gm = fn(g.tile, f.tile, ACT.Exp, g.free, fm, scale=-1.0)
                gm = fn(g.tile, g.tile, ACT.Ln, gm, lb_mark, scale=lb[:, c:c + 1], bias=one)
                em = stt(e.tile, f.tile, 0.0, e.tile, ALU.min, ALU.subtract, em)
                em = tt(e.tile, e.tile, g.tile, ALU.add, em, gm)
                dve.wait(em, mask_mark)
                b_marks[c] = dve.mark(nc.vector.tensor_tensor_scan(
                    out=b[:, c, :], data0=keep_tile, data1=e.tile, initial=0.0,
                    op0=ALU.mult, op1=ALU.add))
                f.release(em, km, gm)
                e.release(b_marks[c])
                g.release(em)
                return [fm]
            product(w_f, h_tile, h_marks, put_f, following=w_i)
            v_marks = {}

            def put_v(tk, n0, ps, m):
                v_marks[tk] = acopy(v[:, tk, n0:n0 + 256], ps, m)
                return [v_marks[tk]]
            run(token_steps(w_i, h_tile, h_marks, put_v, TT, following=w_g))
            gate_marks = {}

            def put_g(c, ps, m):
                s = tmp.take()
                sm = fn(s.tile, ps, ACT.Sigmoid, m, s.free)
                gate_marks[c] = tt(gate[:, c, :], s.tile, ps, ALU.mult, sm)
                s.release(gate_marks[c])
                return [gate_marks[c]]
            product(w_g, h_tile, h_marks, put_g, following=w_o)
            h_read = pe.last()
            mixed = {}
            pool_w = tmp.take()
            pw_mark = side_queue.move(pool_w.tile.rearrange("p (g d) -> p g d", g=4),
                                      dram["pool_w"].rearrange("g c d -> c g d"), side_ports[2], after=pool_w.free)
            for g, wdw in enumerate(POOL_WINDOWS):
                src, m = upad[:, g, :], [u_marks[g], pad]
                shift, n = 1, 0
                while shift < wdw:
                    dst = win[n % 2]
                    m1 = vcopy(dst[:, 0:shift], src[:, 0:shift], m)
                    m = tt(dst[:, shift:], src[:, shift:], src[:, 0:POOL_PAD + T - shift], ALU.add, m)
                    m = [m, m1]
                    src, shift, n = dst, 2 * shift, n + 1
                s = tmp.take()
                m = ts(s.tile, src[:, POOL_PAD:], 1.0 / wdw, None, ALU.mult, None, m, s.free)
                m = tt(s.tile[:, 0:POOL_PAD], s.tile[:, 0:POOL_PAD],
                       const["pool_edge"][:, g * POOL_PAD:(g + 1) * POOL_PAD], ALU.mult, m)
                m = tt(s.tile, s.tile, upad[:, g, POOL_PAD:], ALU.subtract, m)
                o = psum.take()
                m = mm(o.tile, pool_w.tile[:, g * P:(g + 1) * P], s.tile, after=[m, o.free, pw_mark], marked=True)
                s.release(m)
                mh = fn(h_hi[:, g, :], o.tile, ACT.Identity, m, h_read, scale=col("pool_scale", g))
                mixed[g] = [mh, stt(h_lo[:, g, :], o.tile, col("pool_scale", g), h_hi[:, g, :].bitcast(F32),
                                    ALU.mult, ALU.subtract, mh, h_read)]
                o.release(mixed[g])
            pool_w.release(m)
            join()
            at += 8
            qd, sT, kT = [[carve(at + (2 * i + j) * T, T) for j in range(2)] for i in range(3)]
            lead = [carve(0 + j * T, T) for j in range(2)]
            state = [carve(2 * T + i * P, P) for i in range(2)]
            factor = Ring([Slot(y[:, i, :]) for i in range(CT)])
            head, head_read = {}, {}

            def decays(hd, lv):
                if lv == 0:
                    return None
                half = REC_LEVELS[lv - 1]
                s = factor.take()
                n = T // (2 * half)
                bl = b[:, hd, :].rearrange("p (n t) -> p n t", t=2 * half)
                m = tt(s.tile.rearrange("p (n t) -> p n t", t=2 * half), bl,
                       bl[:, :, half - 1:half].to_broadcast([P, n, 2 * half]), ALU.subtract, s.free)
                m = fn(s.tile, s.tile, ACT.Abs, m)
                s.ready = fn(s.tile, s.tile, ACT.Exp, m, scale=-1.0)
                return s

            def factors(hd, lv, s):
                if lv == 0:
                    return
                halves = "p (n o t) -> p n o t"
                f, kh, qh = [a_.rearrange(halves, o=2, t=REC_LEVELS[lv - 1]) for a_ in
                             (s.tile, k[:, hd, :], q[:, hd, :])]
                s.ready = [tt(f[:, :, 0, :], kh[:, :, 0, :], f[:, :, 0, :], ALU.mult, s.ready),
                           ptt(f[:, :, 1, :], qh[:, :, 1, :], f[:, :, 1, :], ALU.mult, s.ready)]

            def whole_tile(hd):
                j = hd % 2
                bh = b[:, hd, :]
                e_mark = fn(lead[j], bh, ACT.Exp, head_read.get(hd - 2))
                head["qd", hd] = tt(qd[j], q[:, hd, :], lead[j], ALU.mult, e_mark, head_read.get(hd - 2))
                s = tmp.take()
                b3 = bh.rearrange("p (n t) -> p n t", t=P)
                m = tt(s.tile.rearrange("p (n t) -> p n t", t=P), b3[:, :, P - 1:P].to_broadcast([P, TT, P]), b3,
                       ALU.subtract, s.free)
                m = fn(s.tile, s.tile, ACT.Exp, m)
                yield
                m = tt(s.tile, k[:, hd, :], s.tile, ALU.mult, m)
                yield
                bank = psum.take()
                for tk in range(TT):
                    t_mark = turn(bank.tile[:, tk * P:(tk + 1) * P], s.tile[:, tk * P:(tk + 1) * P],
                                  after=[m, bank.free], marked=True)
                s.release(t_mark)
                yield
                head["kT", hd] = acopy(kT[j], bank.tile, t_mark, head_read.get(hd - 2))
                bank.release(head["kT", hd])

            def pairs(hd, lv, s):
                j = hd % 2
                bank = psum.take()
                kl, ql, ready = (k[:, hd, :], q[:, hd, :], None) if lv == 0 else (s.tile, s.tile, s.ready)
                for tk in range(TT):
                    m = mm(bank.tile[:, tk * P:(tk + 1) * P], kl[:, tk * P:(tk + 1) * P],
                           ql[:, tk * P:(tk + 1) * P], after=[ready, bank.free], marked=True)
                if s is not None:
                    s.release(m)
                mask = rec_masks[:, lv * P:(lv + 1) * P]
                if lv:
                    mask = mask.bitcast(U32)
                mask = mask.rearrange("p (o t) -> p o t", o=1).to_broadcast([P, TT, P])
                ps3 = bank.tile.rearrange("p (n t) -> p n t", t=P)
                s3 = sT[j].rearrange("p (n t) -> p n t", t=P)
                if lv == 0:
                    m = tt(s3, ps3, mask, ALU.mult, m, head_read.get(hd - 2))
                else:
                    dve.wait(m, head["acc", hd])
                    m = dve.mark(nc.vector.copy_predicated(s3, mask, ps3))
                bank.release(m)
                head["acc", hd] = m

            def outputs(hd):
                j = hd % 2
                o = psum.take()
                st_mark = head_read.get(hd - 1)
                for tk in range(TT):
                    cur = slice(tk * P, (tk + 1) * P)
                    vh = v[:, tk, hd * P:(hd + 1) * P]
                    m = mm(o.tile[:, cur], vh, sT[j][:, cur], start=True, stop=(tk == 0),
                           after=[head["acc", hd], o.free], marked=True)
                    if tk:
                        m = mm(o.tile[:, cur], state[(tk - 1) % 2], qd[j][:, cur], start=False, stop=True,
                               after=[st_mark, head["qd", hd]], marked=True)
                    o_read = m
                    if tk < TT - 1:
                        u = psum.take()
                        m = mm(u.tile[:, 0:P], kT[j][:, cur], vh, after=[head["kT", hd], u.free], marked=True)
                        if tk == 0:
                            st_mark = vcopy(state[0], u.tile[:, 0:P], m, st_mark)
                        else:
                            st_mark = stt(state[tk % 2], state[(tk - 1) % 2], lead[j][:, (tk + 1) * P - 1:(tk + 1) * P],
                                          u.tile[:, 0:P], ALU.mult, ALU.add, m, st_mark, o_read)
                        u.release(st_mark)
                    yield
                s = tmp.take()
                cp = vcopy(s.tile, o.tile, o_read, s.free)
                o.release(cp)
                head_read[hd] = [o_read, st_mark, cp]
                yield
                bank, m = square_sum([s.tile], [cp], ones, T)
                rs, m = inverse_root(bank, m, P, NORM_EPS, T)
                yield
                m = stt(s.tile, s.tile, col("rec_out_gain"), rs.tile, ALU.mult, ALU.mult, m)
                rs.release(m)
                m = tt(s.tile, s.tile, gate[:, hd, :], ALU.mult, m)
                mixed[4 + hd] = split_to(h_hi[:, 4 + hd, :], h_lo[:, 4 + hd, :], s.tile, m)
                s.release(mixed[4 + hd])

            items = [(hd, lv) for hd in range(REC_HEADS) for lv in range(len(REC_LEVELS) + 1)]
            got, state_steps, output_steps = {}, iter(()), iter(())
            for i in range(len(items) + 4):
                if i < len(items):
                    got[i] = decays(*items[i])
                if 0 <= i - 2 < len(items):
                    factors(*items[i - 2], got[i - 2])
                if i - 4 >= 0:
                    hd, lv = items[i - 4]
                    if lv == 0:
                        state_steps = whole_tile(hd)
                        output_steps = outputs(hd - 1) if hd else iter(())
                    pairs(hd, lv, got.pop(i - 4))
                    next(output_steps, None)
                    next(state_steps, None)
                    if lv == len(REC_LEVELS):
                        run(output_steps)
                        run(state_steps)
            run(outputs(REC_HEADS - 1))
            y_marks, y_sums = {}, SquareSum(ones, T, CT)
            put_y = with_squares(y_marks, y_sums, lambda c: y[:, c, :])
            product(w_o, h_tile, mixed, put_y, following=following)
            return add_branch(0, 1, y_marks, x_marks, y_sums, True)

        def odd_mixer(x_marks, following):
            w = dram["w_qkv"]
            w_q, w_k, w_v = [Stream(w, n0=i * D, n_cols=D) for i in range(3)]
            w_o = Stream(dram["w_o_att"])
            w_q.ahead(0, None)
            h_marks = pre_norm(1, 0, x_marks)
            join()
            q, k = [carve(i * 4096, 4096).rearrange("p (c t) -> p c t", c=CT) for i in range(2)]
            v = y_buf.rearrange("p (n c) -> p n c", n=TT)
            bias = Ring([Slot(carve(8192 + i * T, T), side_ports[3 + i]) for i in range(2)])
            turned = Ring([Slot(carve(9216 + i * 4 * T, 4 * T).rearrange("p (j t) -> p j t", j=TT)) for i in range(2)])
            probs = Ring([Slot(carve(13312 + i * T, T)) for i in range(SCORES_AHEAD + 2)])
            put_q, q_marks = into(lambda c: q[:, c, :])
            product(w_q, h_tile, h_marks, put_q, following=w_k)
            put_k, k_marks = into(lambda c: k[:, c, :])
            product(w_k, h_tile, h_marks, put_k, following=w_v)
            v_marks = []

            def put_v(tk, n0, ps, m):
                v_marks.append(acopy(v[:, tk, n0:n0 + 256], ps, m))
                return [v_marks[-1]]
            run(token_steps(w_v, h_tile, h_marks, put_v, TT, following=w_o))
            h_read = pe.last()
            mixed, head = {}, {}

            def score(hd, tq):
                c, half = hd // 2, slice(64 * (hd % 2), 64 * (hd % 2) + 64)
                if tq == 0:
                    bs = head["bias", hd] = bias.take()
                    bm = side_queue.move(bs.tile, dram["rel_bias"][hd], bs.port, after=bs.free)
                    bs.ready = [bm, memset(bs.tile[0:CHUNK, T - CHUNK:T], MASK_VALUE, bm)]
                bs = head["bias", hd]
                n = (tq + 1) * P
                sc = psum.take()
                m = mm(sc.tile[:, 0:n], q[half, c, tq * P:(tq + 1) * P], k[half, c, 0:n],
                       after=[q_marks[c], k_marks[c], sc.free], marked=True)
                pr = probs.take()
                m = stt(pr.tile[:, 0:n], sc.tile[:, 0:n], ATT_DIM ** -0.5, bs.tile[:, T - n:T],
                        ALU.mult, ALU.add, m, bs.ready, pr.free)
                sc.release(m)
                if tq == TT - 1:
                    bs.release(m)
                return pr, softmax(pr.tile[:, 0:n], pr.tile[:, 0:n], 1.0, m)[1]

            def spread(hd, tq, pr, m):
                c, half = hd // 2, slice(64 * (hd % 2), 64 * (hd % 2) + 64)
                if tq == 0:
                    head["banks"] = [psum.take() for _ in range(TT)]
                banks = head["banks"]
                for j in range(tq + 1):
                    t_mark = turn(banks[j].tile[:, tq * P:(tq + 1) * P], pr.tile[:, j * P:(j + 1) * P],
                                  after=[m, banks[j].free], marked=True)
                pr.release(t_mark)
                if tq < TT - 1:
                    return
                pt = turned.take()
                cps = []
                for j in range(TT):
                    lane_copy = acopy if j % 2 else vcopy
                    cps.append(lane_copy(pt.tile[:, j, j * P:T], banks[j].tile[:, j * P:T], t_mark, pt.free))
                    banks[j].release(cps[-1])
                def output():
                    o = psum.take()
                    for j in range(TT):
                        m = mm(o.tile[0:64, j * P:T], v[:, j, hd * 64:(hd + 1) * 64], pt.tile[:, j, j * P:T],
                               start=(j == 0), stop=(j == TT - 1), after=[cps[j], o.free, v_marks], marked=True)
                    mixed[hd] = split_to(h_hi[half, c, :], h_lo[half, c, :], o.tile[0:64, :], m, h_read)
                    o.release(mixed[hd])
                    pt.release(m)
                outputs.append(output)
            flying, outputs = [], []

            def land():
                spread(*flying.pop(0))
                if len(outputs) > 1 or (outputs and not flying):
                    outputs.pop(0)()
            for hd in range(ATT_HEADS):
                for tq in range(TT):
                    flying.append([hd, tq, *score(hd, tq)])
                    if len(flying) > 1:
                        flying[-2][3] = flying[-2][3]()
                    if len(flying) > SCORES_AHEAD:
                        land()
                    if tq == SCORES_AHEAD % TT and len(outputs) == 1:
                        outputs.pop(0)()
            flying[-1][3] = flying[-1][3]()
            while flying:
                land()
            while outputs:
                outputs.pop(0)()
            y_marks, y_sums = {}, SquareSum(ones, T, CT)
            put_y = with_squares(y_marks, y_sums, lambda c: y[:, c, :])
            product(w_o, h_tile, [[mixed[2 * c], mixed[2 * c + 1]] for c in range(CT)], put_y, following=following)
            return add_branch(1, 1, y_marks, x_marks, y_sums, True)

        modulation_mark = []

        def modulate():
            g = scalars[:, 4:4 + 2 * CT]
            c_in = columns[:, COLUMN_AT["c_2"]:COLUMN_AT["c_2"] + CT]
            m = fn(g[:, 0:CT], c_in, ACT.Sigmoid)
            g_mark = tt(g[:, CT:2 * CT], g[:, 0:CT], c_in, ALU.mult, m)
            flying = []

            def over_partitions():
                j, total, m = flying.pop()
                bank = psum.take()
                pe.wait(m, bank.free)
                for c in range(2):
                    last = mm(bank.tile[:, c:c + 1], total.tile[:, c * P:(c + 1) * P], ones[:, 0:1], marked=(c == 1))
                total.release(last)
                b0 = COLUMN_AT["cond_b_2"] + j
                m = tt(mod[:, j:j + 2], bank.tile[:, 0:2], columns[:, b0:b0 + 2], ALU.add, last)
                bank.release(m)
            for n0 in range(0, 6 * D, 256):
                s = fetch(dram["cond_w"], 0, n0, 256)
                yield
                wt = s.tile.rearrange("p (a n) -> p a n", a=CT)
                total = tmp.take()
                acc = total.tile[:, 0:256]
                m = ts(acc, wt[:, 0, :], g[:, CT:CT + 1], None, ALU.mult, None, s.ready, g_mark, total.free)
                for a in range(1, CT):
                    m = stt(acc, wt[:, a, :], g[:, CT + a:CT + a + 1], acc, ALU.mult, ALU.add, m)
                    if a == CT // 2:
                        yield
                s.release(m)
                if flying:
                    over_partitions()
                flying.append((n0 // P, total, m))
            over_partitions()
            m = dve.last()
            ts(scale_1[:, 0:8], mod[:, 8:16], 1.0, None, ALU.add, None, m)
            modulation_mark.append(ts(scale_1[:, 8:16], mod[:, 32:40], 1.0, None, ALU.add, None, m))

        def ada_norm(x_marks, which, mod_mark):
            xs, hs = [x[:, c, :] for c in range(CT)], [y[:, c, :] for c in range(CT)]
            cm = center(xs, x_marks, ones, D, hs)
            bank, m = square_sum(hs, cm, ones, T)
            r, m = inverse_root(bank, m, D, LN_EPS, T)
            marks = []
            for c in range(CT):
                m2 = stt(hs[c], hs[c], scale_1[:, 8 * which + c:8 * which + c + 1], r.tile, ALU.mult, ALU.mult,
                         m, mod_mark)
                m3 = ts(hs[c], hs[c], mod[:, 24 * which + c:24 * which + c + 1], None, ALU.add, None, m2)
                mh = acopy(h_hi[:, c, :], hs[c], m3)
                lower = ptt if c % 2 else tt
                marks.append([mh, lower(h_lo[:, c, :], hs[c], h_hi[:, c, :].bitcast(F32), ALU.subtract, mh)])
            r.release(m2)
            return marks

        def close_block(x_marks, y_marks, which, gain, shift, mod_mark):
            xs, ys = [x[:, c, :] for c in range(CT)], [y[:, c, :] for c in range(CT)]
            marks = []
            for c in range(CT):
                g = mod[:, 24 * which + 16 + c:24 * which + 17 + c]
                m = ts(ys[c], ys[c], g, None, ALU.mult, None, y_marks[c], mod_mark)
                marks.append(stt(xs[c], xs[c], ALPHA, ys[c], ALU.mult, ALU.add, m, x_marks[c]))
            cm = center(xs, marks, ones, D, xs)
            bank, m = square_sum(xs, cm, ones, T)
            r, m = inverse_root(bank, m, D, LN_EPS, T)
            out_marks = []
            for c in range(CT):
                m2 = stt(xs[c], xs[c], col(gain, c), r.tile, ALU.mult, ALU.mult, m)
                out_marks.append(fn(xs[c], xs[c], ACT.Identity, m2, bias=col(shift, c)))
            r.release(m2)
            return out_marks

        def rw_mixer(h_marks, streams):
            NPT = 14
            CP = CONV_K - 1
            at = NPT * (T + 1)

            p = carve(0, NPT * (T + 1)).rearrange("p (c t) -> p c t", c=NPT)
            upad = carve(at, 4 * (CP + T)).rearrange("p (c t) -> p c t", c=4)
            conv = carve(at + 4 * (CP + T), 4 * T).rearrange("p (c t) -> p c t", c=4)
            pad = [memset(upad[:, :, 0:CP], 0.0), memset(p[:, :, 0:1], 0.0)]
            inv_at = at + 4 * 4 * T
            lora, g2, keep_chunk = [carve(inv_at + i * T, T) for i in range(3)]
            lm = [side_queue.move(lora, dram["lora"], side_ports[5]), side_queue.move(g2, dram["rw_g2"], side_ports[6])]
            keep_mark = side_queue.move(keep_chunk, dram["keep_chunk"], side_ports[8])
            w_a, w_b, w_p = streams
            a_marks, u_marks = {}, {}

            def put_a(c, ps, m):
                a_marks[c] = vcopy(upad[:, c, CP:], ps, m)
                return [a_marks[c]]
            product(w_a, h_tile, h_marks, put_a, following=w_b)

            def put_b(c, ps, m):
                s = tmp.take()
                m = fn(s.tile, ps, ACT.Sigmoid, m, s.free)
                u_marks[c] = tt(upad[:, c, CP:], upad[:, c, CP:], s.tile, ALU.mult, m, a_marks[c])
                s.release(u_marks[c])
                return [m]
            product(w_b, h_tile, h_marks, put_b, following=w_p)
            p_marks = {}
            cv = [None] * 4

            def convolve():
                for tap in range(CONV_K):
                    for c in range(4):
                        src = upad[:, c, tap:tap + T]
                        wc = col("conv_w_2", tap * 4 + c)
                        if tap == 0:
                            cv[c] = ts(conv[:, c, :], src, wc, col("conv_b_2", c), ALU.mult, ALU.add, u_marks[c], pad)
                        else:
                            cv[c] = stt(conv[:, c, :], src, wc, conv[:, c, :], ALU.mult, ALU.add, cv[c])
                    yield
            taps = convolve()
            mixed_p = {}

            def shift(c):
                s = tmp.take()
                m = ptt(s.tile, p[:, c, 0:T], p[:, c, 1:], ALU.subtract, p_marks[c], pad, s.free)
                mixed_p[c] = stt(p[:, c, 1:], s.tile, col("mu_shift_2", c), p[:, c, 1:], ALU.mult, ALU.add, m)
                s.release(mixed_p[c])

            def put_p(c, ps, m):
                p_marks[c] = acopy(p[:, c, 1:], ps, m)
                for _ in range(3):
                    next(taps, None)
                if c:
                    shift(c - 1)
                return [p_marks[c]]
            low_on["pool"] = 2
            product(w_p, h_tile, h_marks, put_p)
            low_on["pool"] = 1
            h_read = pe.last()
            mixed = {}
            shift(NPT - 1)
            run(taps)
            conv_done = []

            def finish_convolution():
                cs = [conv[:, c, :] for c in range(4)]
                marks = center(cs, cv, ones, 512, cs)
                yield
                bank, m = square_sum(cs, marks, ones, T)
                yield
                r, m = inverse_root(bank, m, 512, LN_EPS, T)
                yield
                m = [stt(cs[c], cs[c], col("conv_ln_g_2", c), r.tile, ALU.mult, ALU.mult, m) for c in range(4)]
                r.release(m[-1])
                m = [ts(cs[c], cs[c], col("conv_ln_b_2", c), None, ALU.add, None, m[c]) for c in range(4)]
                yield
                for c in range(4):
                    s = tmp.take()
                    m3 = fn(s.tile, cs[c], ACT.Sigmoid, m[c], s.free)
                    m3 = tt(s.tile, cs[c], s.tile, ALU.mult, m3)
                    mixed[c] = split_to(h_hi[:, c, :], h_lo[:, c, :], s.tile, m3, h_read)
                    s.release(mixed[c])
                conv_done.extend([dve.last(), act.last()])
            for lane in (dve, act, pool):
                lane.wait(h_read)
            space["split_ctx"].close()
            space["split_ctx"] = ExitStack()
            extra = space["split_ctx"].enter_context(nc.sbuf_tensor("rw_extra", [P, 4 * CHUNK_WORDS], F32))[:, :]

            rw_masks = extra[:, 6144:6144 + 15 * 64]
            M_T, RK_T, RB_T = [extra[:, i * 4 * T:(i + 1) * 4 * T].rearrange("p (c n) -> p c n", c=4) for i in range(3)]
            mask_mark = side_queue.move(rw_masks, dram["rw_masks"], side_ports[7])
            dve.wait(keep_mark)
            r_t, k_t, v_t = [[p[:, 4 * i + c, 1:] for c in range(4)] for i in range(3)]
            wd, ad, gd = p[0:64, 12, 1:], p[64:128, 12, 1:], p[:, 13, 1:]
            wm = fn(wd, wd, ACT.Tanh, mixed_p[12])
            gm = fn(gd, gd, ACT.Sigmoid, mixed_p[13])
            a_hat = carve(at, 4 * T).rearrange("p (c t) -> p c t", c=4)
            tok = carve(at + 4 * T, 3 * 4 * T).rearrange("p (k n c) -> p k n c", k=3, n=TT)
            v_tok, k_tok, b_tok = tok[:, 0], tok[:, 1], tok[:, 2]
            Y = p[:, 4:8, 1:]
            gate = y_buf[:, 0:4 * T].rearrange("p (c t) -> p c t", c=4)
            bonus = y_buf[:, 4 * T:8 * T].rearrange("p (c t) -> p c t", c=4)
            n_ch = T // RW_CHUNK
            ready = {}
            steps_tmp = Ring([Slot(extra[:, i * T:(i + 1) * T]) for i in range(10)])

            def prepare(c):
                cs_ = slice(c * P, (c + 1) * P)
                lw, kk, aa, nrm, total = [steps_tmp.take() for _ in range(5)]
                bank = psum.take()
                m = mm(bank.tile, lora[0:64, cs_], wd, after=[lm, wm, bank.free], marked=True)
                m = fn(lw.tile, bank.tile, ACT.Sigmoid, m, lw.free, bias=col("rw_w0_2", c))
                bank.release(m)
                lw_mark = ts(lw.tile, lw.tile, -math.exp(-0.5), None, ALU.mult, None, m)
                yield
                bank = psum.take()
                m = mm(bank.tile, lora[64:128, cs_], ad, after=[lm, mixed_p[12], bank.free], marked=True)
                a_mark = fn(aa.tile, bank.tile, ACT.Sigmoid, m, aa.free, bias=col("rw_a0_2", c))
                bank.release(a_mark)
                yield
                bank = psum.take()
                m = mm(bank.tile, g2[:, cs_], gd, after=[lm, gm, bank.free], marked=True)
                g_mark = acopy(gate[:, c, :], bank.tile, m)
                bank.release(g_mark)
                yield
                m = ts(kk.tile, k_t[c], col("rw_kk_2", c), None, ALU.mult, None, mixed_p[4 + c], kk.free)
                bank, sm = square_sum([kk.tile], [m], head_ones, T)
                m = fn(nrm.tile, bank.tile, ACT.Sqrt, sm, nrm.free)
                bank.release(m)
                yield
                m = ts(nrm.tile, nrm.tile, 1e-12, None, ALU.max, None, m)
                m = recip(nrm.tile, nrm.tile, m)
                kk_mark = tt(kk.tile, kk.tile, nrm.tile, ALU.mult, m)
                yield
                m = ts(nrm.tile, aa.tile, 1.0, col("rw_ka_2", c), ALU.subtract, ALU.mult, kk_mark, a_mark)
                k_mark = stt(k_t[c], nrm.tile, 1.0, k_t[c], ALU.add, ALU.mult, m)
                yield
                m = stt(nrm.tile, r_t[c], col("rw_rk_2", c), k_t[c], ALU.mult, ALU.mult, k_mark, mixed_p[c])
                bank, m = channel_sum([nrm.tile], [m], head_ones, T)
                yield
                bonus_mark = tt(bonus[:, c, :], bank.tile, v_t[c], ALU.mult, m, mixed_p[8 + c])
                bank.release(bonus_mark)
                yield
                bank = psum.take()
                for tk in range(TT):
                    m = turn(bank.tile[:, tk * P:(tk + 1) * P], v_t[c][:, tk * P:(tk + 1) * P],
                             after=[mixed_p[8 + c], bank.free], marked=True)
                v_read = m
                assert conv_done
                for lane in (act, dve):
                    lane.wait(conv_done)
                v_mark = acopy(v_tok[:, :, cs_], bank.tile.rearrange("p (n c) -> p n c", n=TT), m)
                bank.release(v_mark)
                yield
                dve.wait(lw_mark, total.free)
                m = dve.mark(nc.vector.tensor_tensor_scan(
                    out=total.tile, data0=keep_chunk, data1=lw.tile, initial=0.0,
                    op0=ALU.mult, op1=ALU.add))
                m1 = tt(lw.tile, total.tile, lw.tile, ALU.subtract, m)
                before = fn(lw.tile, lw.tile, ACT.Exp, m1)
                pm = fn(nrm.tile, total.tile, ACT.Exp, m, bonus_mark)
                yield
                ahat_mark = tt(a_hat[:, c, :], kk.tile, lw.tile, ALU.mult, before, kk_mark)
                r_mark = tt(r_t[c], r_t[c], nrm.tile, ALU.mult, pm, bonus_mark)
                ed_mark = vcopy(end_decay[:, c * n_ch:(c + 1) * n_ch],
                                nrm.tile.rearrange("p (n t) -> p n t", t=RW_CHUNK)[:, :, RW_CHUNK - 1], pm)
                yield
                im = fn(total.tile, total.tile, ACT.Exp, m1, pm, scale=-1.0)
                khat_mark = tt(k_t[c], k_t[c], total.tile, ALU.mult, im)
                m = stt(aa.tile, kk.tile, -1.0, aa.tile, ALU.mult, ALU.mult, a_mark, kk_mark)
                b_mark = tt(v_t[c], aa.tile, total.tile, ALU.mult, m, im, v_read, bonus_mark)
                yield
                lw.release(ahat_mark)
                kk.release(m)
                aa.release(b_mark)
                total.release(b_mark)
                nrm.release(ed_mark)
                yield
                for src, dst, mk in ((k_t[c], k_tok, khat_mark), (v_t[c], b_tok, b_mark)):
                    bank = psum.take()
                    for tk in range(TT):
                        m = turn(bank.tile[:, tk * P:(tk + 1) * P], src[:, tk * P:(tk + 1) * P],
                                 after=[mk, bank.free], marked=True)
                    m = acopy(dst[:, :, cs_], bank.tile.rearrange("p (n c) -> p n c", n=TT), m)
                    bank.release(m)
                ready[c] = [ahat_mark, khat_mark, b_mark, r_mark]
            convolution_steps = finish_convolution()
            for pair in range(2):
                both = [prepare(2 * pair + i) for i in range(2)]
                while both:
                    if pair == 0 and not conv_done:
                        next(convolution_steps, None)
                    both = [g_ for g_ in both if next(g_, both) is None]
            join()
            for lane in (dve, pool):
                lane.wait(mask_mark)
            b_hat = v_t
            rm = rw_masks.rearrange("p (k t) -> p k t", t=64)

            def wide(mask):
                return rm[:, mask:mask + 1, :].to_broadcast([P, 8, 64])

            def blocks(ap):
                return ap.rearrange("p (n t) -> p n t", t=64)

            def each():
                for hh in range(2):
                    for ch in range(n_ch):
                        yield hh, ch, slice(64 * (ch % 2), 64 * (ch % 2) + 64), \
                            slice((hh * TT + ch // 2) * 64, (hh * TT + ch // 2) * 64 + 64)

            def gram(rows, cols_, c, evacuate):
                marks = []
                for hh in range(2):
                    bank = psum.take()
                    pe.wait(bank.free, ready[c])
                    hs_ = slice(64 * hh, 64 * hh + 64)
                    for ch in range(n_ch):
                        part, cc = slice(64 * (ch % 2), 64 * (ch % 2) + 64), slice(ch // 2 * 64, ch // 2 * 64 + 64)
                        tsl = slice(ch * 64, ch * 64 + 64)
                        m = mm(bank.tile[part, cc], rows[hs_, tsl], cols_[hs_, tsl], marked=(ch == n_ch - 1))
                    marks.append(evacuate(slice(hh * 4 * 64, (hh + 1) * 4 * 64), bank.tile[:, 0:256], m))
                    bank.release(marks[-1])
                return marks

            def small_products(lhs, rhs, *after):
                bank = psum.take()
                pe.wait(bank.free, *after)
                for hh, ch, part, cc in each():
                    m = mm(bank.tile[part, cc], lhs[part, cc], rhs(part, cc, hh, ch // 2),
                           marked=(hh == 1 and ch == n_ch - 1))
                return bank, m

            def plain(ap):
                return lambda part, cc, hh, tk: ap[part, cc]

            for c in range(4):
                for rows, cols_, mask, dst in ((k_t[c], a_hat[:, c, :], 0, M_T), (k_t[c], r_t[c], 1, RK_T),
                                               (b_hat[c], r_t[c], 1, RB_T)):
                    tri = rm[:, mask:mask + 1, :].to_broadcast([P, 4, 64])
                    gram(rows, cols_, c, lambda cc, ps, m: tt(blocks(dst[:, c, cc]), blocks(ps), tri, ALU.mult, m))
            gram_read = pe.last()
            n_ = [carve(inv_at + c * T, T) for c in range(4)]
            x_ = b_hat
            xm, nm, ym = {}, {}, {}

            def transposed(dst, src, *after):
                bank = psum.take()
                pe.wait(bank.free)
                for i in range(4):
                    m = turn(bank.tile[:, i * P:(i + 1) * P], src[:, i * P:(i + 1) * P], after=after, marked=(i == 3))
                to = dst.rearrange("p (i o t) -> p i o t", o=2, t=64)
                of = bank.tile.rearrange("p (i e t) -> p i e t", e=2, t=64)
                half = [slice(0, 64), slice(64, 128)]
                marks = [(vcopy if o else acopy)(to[half[e], :, o, :], of[half[o], :, e, :], m)
                         for e in range(2) for o in range(2)]
                bank.release(marks)
                return marks
            for c in range(4):
                nm[c] = gram(b_hat[c], a_hat[:, c, :], c, lambda cc, ps, m: acopy(n_[c][:, cc], ps, m))
                m = tt(blocks(Y[:, c, :]), blocks(n_[c]), wide(3), ALU.mult, nm[c], gram_read)
                ym[c] = tt(blocks(Y[:, c, :]), blocks(Y[:, c, :]), wide(2), ALU.add, m)
                if c:
                    xm[c - 1] = transposed(x_[c - 1], Y[:, c - 1, :], ym[c - 1])
            xm[3] = transposed(x_[3], Y[:, 3, :], ym[3])
            for lv in range(1, len(RW_LEVELS)):
                part = {}
                for c in range(4):
                    s1 = tmp.take()
                    m = ptt(blocks(s1.tile), blocks(n_[c]), wide(3 + lv), ALU.mult, s1.free, nm[c])
                    part[c] = s1, m
                for c in range(4):
                    s1, m = part[c]
                    bank, m = small_products(s1.tile, plain(x_[c]), m, xm[c])
                    m = acopy(s1.tile, bank.tile, m)
                    bank.release(m)
                    part[c] = s1, m
                for c in range(5):
                    if c < 4:
                        s1, m = part[c]
                        bank, m = small_products(Y[:, c, :], plain(s1.tile), m, ym[c])
                        s1.release(m)
                        xm[c] = tt(x_[c], x_[c], bank.tile, ALU.add, m, xm[c])
                        bank.release(xm[c])
                    if c:
                        ym[c - 1] = transposed(Y[:, c - 1, :], x_[c - 1], xm[c - 1])
            for c in range(4):
                s1, s2 = tmp.take(), tmp.take()
                bank, m = small_products(M_T[:, c, :], lambda part, cc, hh, tk:
                                         v_tok[part, tk, c * P + hh * 64:c * P + hh * 64 + 64])
                e = acopy(s1.tile, bank.tile, m, s1.free)
                bank.release(e)
                bank2 = psum.take()
                for tk in range(TT):
                    m2 = turn(bank2.tile[:, tk * P:(tk + 1) * P], a_hat[:, c, tk * P:(tk + 1) * P],
                              after=[bank2.free], marked=True)
                e2 = vcopy(s2.tile, bank2.tile, m2, s2.free)
                bank2.release(e2)
                bank, m = small_products(Y[:, c, :], plain(s1.tile), e, ym[c])
                e = acopy(M_T[:, c, :], bank.tile, m)
                bank.release(e)
                s1.release(m)
                for odd in range(2):
                    bank = psum.take()
                    part = slice(64 * odd, 64 * odd + 64)
                    pe.wait(bank.free, e2)
                    for hh in range(2):
                        for tk in range(TT):
                            o = slice(64 * hh, 64 * hh + 64)
                            m = mm(bank.tile[o, tk * 64:(tk + 1) * 64],
                                   s2.tile[part, tk * P + hh * 64:tk * P + hh * 64 + 64],
                                   Y[part, c, (hh * TT + tk) * 64:(hh * TT + tk) * 64 + 64],
                                   marked=(hh == 1 and tk == TT - 1))
                    w2 = a_hat[:, c, :].rearrange("p (n o t) -> p n o t", o=2, t=64)[:, :, odd, :]
                    e3 = acopy(w2, bank.tile[:, 0:256].rearrange("p (n t) -> p n t", t=64), m)
                    bank.release(e3)
                s2.release(m)
            join()
            st = [carve(inv_at + i * 256, 256).rearrange("p (c v) -> p c v", c=4) for i in range(2)]
            uus = [carve(inv_at + 512 + i * T, T) for i in range(2)]
            out_rw = a_hat
            st_mark = memset(st[0], 0.0)
            u_read = [None, None]
            for ch in range(n_ch):
                part, tk = slice(64 * (ch % 2), 64 * (ch % 2) + 64), ch // 2
                tsl = slice(ch * 64, ch * 64 + 64)
                old, new = st[ch % 2], st[(ch + 1) % 2]
                uu = uus[ch % 2]

                def heads():
                    for hd in range(RW_HEADS):
                        c, hh = hd // 2, hd % 2
                        yield hd, c, slice(64 * hh, 64 * hh + 64), slice(hd * 64, hd * 64 + 64), \
                            slice((hh * TT + tk) * 64, (hh * TT + tk) * 64 + 64)
                um = []
                for hh in range(2):
                    bank = psum.take()
                    pe.wait(bank.free, st_mark)
                    hp = slice(64 * hh, 64 * hh + 64)
                    for c in range(4):
                        m = mm(bank.tile[part, c * 64:(c + 1) * 64], a_hat[hp, c, tsl], old[hp, c, :], marked=(c == 3))
                    u4 = uu[part, :].rearrange("p (c o v) -> p c o v", c=4, o=2)[:, :, hh, :]
                    um.append(tt(u4, bank.tile[part, 0:256].rearrange("p (c v) -> p c v", c=4),
                                 M_T[part, :, (hh * TT + tk) * 64:(hh * TT + tk) * 64 + 64], ALU.add, m,
                                 u_read[ch % 2]))
                    bank.release(um[-1])
                bank = psum.take()
                pe.wait(bank.free, um)
                for hd, c, hp, hv, cc in heads():
                    o = bank.tile[hp, c * 64:(c + 1) * 64]
                    mm(o, k_tok[part, tk, hv], v_tok[part, tk, hv], start=True, stop=False)
                    m = mm(o, b_tok[part, tk, hv], uu[part, hv], start=False, stop=True, marked=(hd == RW_HEADS - 1))
                b3 = bank.tile[:, 0:256].rearrange("p (c v) -> p c v", c=4)
                hm = tt(new, old, b3, ALU.add, m, st_mark)
                bank.release(hm)
                ed = end_decay[:, :].rearrange("p (c n) -> p c n", c=4)[:, :, ch:ch + 1].to_broadcast([P, 4, 64])
                st_new = tt(new, new, ed, ALU.mult, hm)
                bank, bank2 = psum.take(), psum.take()
                pe.wait(bank.free, bank2.free)
                for hd, c, hp, hv, cc in heads():
                    m1 = mm(bank.tile[hp, c * 64:(c + 1) * 64], old[hp, c, :], r_t[c][hp, tsl],
                            marked=(hd == RW_HEADS - 1))
                for hd, c, hp, hv, cc in heads():
                    o = bank2.tile[hp, c * 64:(c + 1) * 64]
                    mm(o, v_tok[part, tk, hv], RK_T[part, c, cc], start=True, stop=False)
                    m = mm(o, uu[part, hv], RB_T[part, c, cc], start=False, stop=True, marked=(hd == RW_HEADS - 1))
                u_read[ch % 2] = m
                yc_ = out_rw[:, :, tsl]
                ym_ = acopy(yc_, bank.tile[:, 0:256].rearrange("p (c v) -> p c v", c=4), m1)
                bank.release(ym_)
                ym_ = tt(yc_, yc_, bank2.tile[:, 0:256].rearrange("p (c v) -> p c v", c=4), ALU.add, m, ym_)
                bank2.release(ym_)
                st_mark = [st_new, m]
            join()
            space["split_ctx"].close()
            open_split("split_3")
            w_o = Stream(dram["w_out"])
            w_o.ahead(0, None)
            cm = [center([out_rw[:, c, :]], [ym_], head_ones, 64, [out_rw[:, c, :]]) for c in range(4)]
            sq = [square_sum([out_rw[:, c, :]], cm[c], head_ones, T) for c in range(4)]
            roots = [inverse_root(bank, m, 64, GN_EPS, T) for bank, m in sq]
            for c in range(4):
                yc, (r, m) = out_rw[:, c, :], roots[c]
                m = stt(yc, yc, col("rw_lnx_g_2", c), r.tile, ALU.mult, ALU.mult, m)
                r.release(m)
                m = stt(yc, yc, col("rw_lnx_b_2", c), bonus[:, c, :], ALU.add, ALU.add, m)
                m = tt(yc, yc, gate[:, c, :], ALU.mult, m)
                mixed[4 + c] = split_to(h_hi[:, 4 + c, :], h_lo[:, 4 + c, :], yc, m, h_read)
            put_y, y_marks = into(lambda c: y[:, c, :])
            product(w_o, h_tile, mixed, put_y)
            join()
            space["split_ctx"].close()
            space["arena_ctx"].close()
            open_split("split_4")
            open_arena("arena_3")
            return y_marks

        def peer(h_marks, w_query):
            join()
            NQ = 2 * PEER_HEADS
            HK = PEER_HEADS * TOPK
            n_groups = NKEYS // GROUP
            q = carve(0, NQ * T).rearrange("p (c t) -> p c t", c=NQ)
            works = [carve(8192 + i * 2048, 2048) for i in range(2)]
            keys = [carve(12288 + i * 1024, 1024) for i in range(2)]
            at = 14336
            top_v = carve(at, NQ * TOPK).rearrange("p (g k) -> p g k", g=NQ)
            top_i = carve(at + 256, NQ * TOPK).rearrange("p (g k) -> p g k", g=NQ)
            idx = carve(at + 512, 256).bitcast(U32)
            best_v = carve(at + 768, HK)
            parts = carve(at + 896, HK * 3)
            half_f = carve(at + 1280, 2 * HK)
            total = carve(at + 1536, 8)
            turned = carve(at + 1544, 3 * T).rearrange("p (k t) -> p k t", k=3)
            km = [side_queue.move(keys[i], dram[f"peer_k{i + 1}"], side_ports[7 + i]) for i in range(2)]
            w_in = [Stream(dram["peer_u"], n0=g * GROUP * P, n_cols=GROUP * P) for g in range(n_groups)]
            w_outs = [Stream(dram["peer_v"], k0=g * GROUP * P, width=512) for g in range(n_groups)]
            put_q, q_marks = into(lambda c: q[:, c, :])
            product(w_query, h_tile, h_marks, put_q, following=w_in[0])
            counter = const["counter"]
            early = Ring([Slot(y[:, c, :], early_ports[c]) for c in range(CT)])
            early_marks = {}

            def early_steps():
                for g in range(EARLY_GROUPS):
                    def put(c, ps, m, g=g):
                        s = early.take()
                        m = fn(s.tile, ps, ACT.Gelu, m, s.free)
                        s.release(weight_queue.move(early_table[g * GROUP + c], s.tile, s.port, after=[m]))
                        early_marks[g, c] = s.free[0]
                        return [m]
                    yield from product_steps(w_in[g], h_tile, h_marks, put,
                                             following=w_in[g + 1])
            ahead = early_steps()
            low_on["pool"] = 2

            def fill(n):
                for _ in range(n):
                    next(ahead, None)
            prev, work_free = [], [None, None]

            def top16(src, vals, inds, *after):
                dve.wait(*after)
                m = dve.mark(nc.vector.max(vals[:, 0:8], src))
                dve.wait(m)
                m = dve.mark(nc.vector.max_index(inds[:, 0:8], vals[:, 0:8], src))
                dve.wait(m)
                m = dve.mark(nc.vector.match_replace(src, vals[:, 0:8], src, LOWEST))
                dve.wait(m)
                m = dve.mark(nc.vector.max(vals[:, 8:16], src))
                dve.wait(m)
                return dve.mark(nc.vector.max_index(inds[:, 8:16], vals[:, 8:16], src))

            def scores(tk):
                sc = works[tk % 2].rearrange("p (g n) -> p g n", g=NQ)
                s_marks = []
                for g4 in range(NQ // 4):
                    bank = psum.take()
                    pe.wait(bank.free, km)
                    for j in range(4):
                        g = g4 * 4 + j
                        m = mm(bank.tile[:, j * P:(j + 1) * P], q[:, g, tk * P:(tk + 1) * P],
                               keys[g % 2][:, (g // 2) * P:(g // 2 + 1) * P], after=[q_marks[g]], marked=(j == 3))
                    cp = acopy(sc[:, g4 * 4:g4 * 4 + 4, :], bank.tile.rearrange("p (g n) -> p g n", g=4), m,
                               work_free[tk % 2])
                    bank.release(cp)
                    s_marks.append(cp)
                return s_marks
            s_marks = scores(0)
            for tk in range(TT):
                work = works[tk % 2]
                sc = work.rearrange("p (g n) -> p g n", g=NQ)
                m = prev
                for g in range(NQ):
                    m1 = top16(sc[:, g, :], top_v[:, g, :], idx[:, g * TOPK:(g + 1) * TOPK], s_marks[g // 4], m)
                    if g % 4 == 3:
                        fill(1)
                m = vcopy(top_i.rearrange("p g k -> p (g k)"), idx, m1)
                if tk < TT - 1:
                    s_marks = scores(tk + 1)
                cand = work.rearrange("p (h n) -> p h n", h=PEER_HEADS)
                tv = top_v.rearrange("p (h s) k -> p h s k", s=2)
                c4 = cand.rearrange("p h (i j) -> p h i j", i=TOPK)
                for hd in range(PEER_HEADS):
                    m2 = tt(c4[:, hd], tv[:, hd, 0, :].unsqueeze(2).to_broadcast([P, TOPK, TOPK]),
                            tv[:, hd, 1, :].unsqueeze(1).to_broadcast([P, TOPK, TOPK]), ALU.add, m)
                for hd in range(PEER_HEADS):
                    m3 = top16(cand[:, hd, :], best_v[:, hd * TOPK:(hd + 1) * TOPK],
                               idx[:, hd * TOPK:(hd + 1) * TOPK], m2)
                    if hd % 2:
                        fill(1)
                ci = idx[:, 0:HK]
                m_hi = ts(idx[:, HK:2 * HK], ci, 4, None, ALU.logical_shift_right, None, m3)
                m_a = vcopy(half_f[:, 0:HK], idx[:, HK:2 * HK], m_hi)
                m_lo = ts(idx[:, HK:2 * HK], ci, 15, None, ALU.bitwise_and, None, m_a)
                m_b = vcopy(half_f[:, HK:2 * HK], idx[:, HK:2 * HK], m_lo)
                pk = work.rearrange("p (n i) -> p n i", i=TOPK)
                ti = top_i.rearrange("p (h s) k -> p h s k", s=2)
                m = m_b
                for side in range(2):
                    place = half_f[:, side * HK:(side + 1) * HK].unsqueeze(2).to_broadcast([P, HK, TOPK])
                    count = counter[:, 0:TOPK].unsqueeze(1).to_broadcast([P, HK, TOPK])
                    m = tt(pk, place, count, ALU.is_equal, m, prev)
                    for hd in range(PEER_HEADS):
                        pv = pk[:, hd * TOPK:(hd + 1) * TOPK, :]
                        m4 = tt(pv, pv, ti[:, hd, side, :].unsqueeze(1).to_broadcast([P, TOPK, TOPK]), ALU.mult, m)
                    m = reduce(parts[:, side * HK:(side + 1) * HK], pk, ALU.add, m4)
                    fill(1)
                work_free[tk % 2] = m
                b3 = best_v.rearrange("p (h k) -> p h k", h=PEER_HEADS)
                g3 = parts[:, 2 * HK:3 * HK].rearrange("p (h k) -> p h k", h=PEER_HEADS)
                m = tt(g3, b3, b3[:, :, 0:1].to_broadcast([P, PEER_HEADS, TOPK]), ALU.subtract, m)
                m = fn(g3, g3, ACT.Exp, m)
                m = reduce(total, g3, ALU.add, m)
                m = recip(total, total, m)
                m = tt(g3, g3, total.unsqueeze(2).to_broadcast([P, PEER_HEADS, TOPK]), ALU.mult, m)
                bank = psum.take()
                for j in range(3):
                    mt = turn(bank.tile[:, j * P:(j + 1) * P], parts[:, j * HK:(j + 1) * HK],
                              after=[m, bank.free], marked=True)
                cp = acopy(turned[:, :, tk * P:(tk + 1) * P],
                           bank.tile[:, 0:3 * P].rearrange("p (k t) -> p k t", k=3), mt)
                bank.release(cp)
                prev = [cp, m1]
            join()
            stages = Ring([Slot(carve(i * 4096, 4096).rearrange("p (a t) -> p a t", t=STAGE_TOKENS), side_ports[9 + i])
                           for i in range(2)])
            hots = Ring([Slot(carve(8192 + i * 256, 256)) for i in range(24)])
            table_marks = []
            batch = 0
            for block in range(T // STAGE_TOKENS):
                sg = stages.take()
                for t4 in range(0, STAGE_TOKENS, 4):
                    bank = psum.take()
                    pe.wait(bank.free)
                    for j in range(4):
                        t = block * STAGE_TOKENS + t4 + j
                        hot = hots.take()
                        key2, key1 = hot.tile[:, 0:P], hot.tile[:, P:2 * P]
                        m = ts(key2, counter[:, :], turned[:, 1, t:t + 1], None, ALU.is_equal, None, hot.free)
                        m = ts(key1, counter[:, :], turned[:, 0, t:t + 1], turned[:, 2, t:t + 1],
                               ALU.is_equal, ALU.mult, hot.free)
                        m = mm(bank.tile[:, j * P:(j + 1) * P], key2, key1, after=[m], marked=True)
                        hot.release(m)
                    cp = acopy(sg.tile[:, :, t4:t4 + 4], bank.tile.rearrange("p (t a) -> p a t", t=4), m, sg.free)
                    bank.release(cp)
                    batch += 1
                    if batch % 4 == 0:
                        fill(1)
                wr = weight_queue.move(gate_table[block], sg.tile.rearrange("p a t -> p (a t)"), sg.port, after=[cp])
                sg.release(wr)
                table_marks.append(wr)
            run(ahead)
            low_on["pool"] = 1
            join()
            for lane in (dve, act, pool):
                lane.wait(table_marks)
            open_hidden("experts", 2 * 4096)
            gates = Ring([Slot(carve(i * 2048, 2048).rearrange("p (b a t) -> p b a t", a=GROUP, t=STAGE_TOKENS),
                               side_ports[7 + i]) for i in range(2)])
            lates = Ring([Slot(carve(4096 + i * 2048, 2048).rearrange("p (c t) -> p c t", t=T), side_ports[1 + i])
                          for i in range(2)])
            for s in gates.slots + lates.slots:
                s.free = table_marks[:]
            space["h_marks"], space["y_free"] = h_marks, [early_marks[k_] for k_ in early_marks]
            n_late = n_groups - EARLY_GROUPS
            order = sorted(range(n_groups), key=lambda g: ((g + 1) / EARLY_GROUPS if g < EARLY_GROUPS
                                                           else (g - EARLY_GROUPS) / n_late))
            held = {}

            def load_group(n):
                g = order[n]
                gt = gates.take()
                gt.ready = side_queue.move(gt.tile.rearrange("p b a t -> p b (a t)"),
                                           gate_table.rearrange("b p n -> p b n")
                                           [:, :, g * GROUP * STAGE_TOKENS:(g + 1) * GROUP * STAGE_TOKENS],
                                           gt.port, after=[gt.free, table_marks])
                lt = None
                if g < EARLY_GROUPS:
                    lt = lates.take()
                    lt.ready = side_queue.move(lt.tile, early_table[g * GROUP:(g + 1) * GROUP]
                                               .rearrange("c p t -> p c t"), lt.port,
                                               after=[lt.free, [early_marks[g, c_] for c_ in range(GROUP)]])
                held[n] = gt, lt
            load_group(0)

            def make(n, c, ps, m, hi, lo, free):
                if c == 0:
                    held["gate"], held["late"] = held.pop(n)
                    if n + 1 < n_groups:
                        load_group(n + 1)
                gt = held["gate"]
                s = tmp.take()
                if ps is None:
                    src, sm = held["late"].tile[:, c, :], held["late"].ready
                else:
                    src, sm = s.tile, fn(s.tile, ps, ACT.Gelu, m, s.free)
                blocks_ = "p (b t) -> p b t"
                q_ = tt(s.tile.rearrange(blocks_, t=STAGE_TOKENS), src.rearrange(blocks_, t=STAGE_TOKENS),
                        gt.tile[:, :, c, :], ALU.mult, sm, gt.ready, s.free)
                marks = split_to(hi, lo, s.tile, q_, free)
                s.release(marks)
                if c == GROUP - 1:
                    gt.release(q_)
                    if ps is None:
                        held["late"].release(q_)
                return marks, [sm] if ps is not None else []

            def first(n):
                if n >= n_groups or order[n] < EARLY_GROUPS:
                    return None, None
                return w_in[order[n]], (w_outs[order[n - 1]] if n else first(1)[0] or w_outs[order[0]])
            return grouped_product(n_groups, first, lambda n: w_outs[order[n]], make, None)

        mem_out = Ring([Slot(carve(i * 256, 256), side_ports[5 + i]) for i in range(4)])
        memory_keys = [memory_keys_steps(l, None) for l in range(2)]
        next(memory_keys[0])
        mem_marks = rms_split([mem_raw[:, c, :] for c in range(CT)], [mem_in] * CT, lambda i: col("mem_norm_gain", i),
                              n=M)
        for l in range(2):
            memory_marks["ready"] = mem_marks
            run(memory_keys[l])
        join()
        for lane in (dve, act, pool):
            lane.wait([s.free for s in mem_out.slots])
        modulation_steps = modulate()
        xm = [x_in] * CT
        xm = even_mixer(xm, None)
        xm = memory_attention(0, xm, None)
        xm = mlp(0, xm, None)
        xm = odd_mixer(xm, None)
        xm = memory_attention(1, xm, None)
        xm = mlp(1, xm, None)
        run(modulation_steps)
        mod_mark = modulation_mark[0]
        w_in_streams = [Stream(dram["w_in"], n0=n0, n_cols=n) for n0, n in ((0, 512), (512, 512), (1024, 1792))]
        w_in_streams[0].ahead(0, None)
        hm = ada_norm(xm, 0, mod_mark)
        join()
        ym = rw_mixer(hm, w_in_streams)
        xm = close_block(xm, ym, 0, "ln1_g_2", "ln1_b_2", mod_mark)
        w_query = Stream(dram["peer_wq"])
        w_query.ahead(0, None)
        hm = ada_norm(xm, 1, mod_mark)
        ym = peer(hm, w_query)
        xm = close_block(xm, ym, 1, "ln2_g_2", "ln2_b_2", mod_mark)
        done = weight_queue.move(out.rearrange("(c p) t -> p c t", p=P), x, out_port, after=[xm])
        sp.wait(done)
        for prt in side_ports + early_ports:
            if prt.count:
                sp.wait((prt.sem, prt.count))


def layouts(i):
    a = {k: np.asarray(v) for k, v in i.items()}
    cols = [a[n].reshape(-1, P).T for n, _ in COLUMNS]
    p_, u_ = np.arange(P)[:, None], np.arange(T)[None, :]
    dist = np.clip(p_ + T - P - u_, -REL_CLIP, REL_CLIP) + REL_CLIP
    out = {
        "columns": np.concatenate(cols, axis=1),
        "x": a["x"][0].T, "mem": a["mem"][0].T,
        "w_in_ab": a["w_in_ab"][0], "pool_w": a["pool_w"][0], "w_out_ab": a["w_out_ab"][0],
        "w_qkv": a["w_qkv"][0], "rel_bias": a["rel_bias"][0][:, dist], "w_o_att": a["w_o_att"][0],
        "w_mem_q": a["w_mem_q"], "w_mem_kv": a["w_mem_kv"], "w_mem_o": a["w_mem_o"],
        "w_ff1": a["w_ff1"], "w_ff2": a["w_ff2"],
        "cond_w": a["cond_w_2"], "w_in": a["w_in_2"], "w_out": a["w_out_2"],
        "lora": np.concatenate([a["rw_w2_2"], a["rw_a2_2"]], axis=0), "rw_g2": a["rw_g2_2"],
        "peer_wq": a["peer_wq_2"],
        "peer_k1": a["peer_k1_2"].transpose(2, 0, 1).reshape(P, -1),
        "peer_k2": a["peer_k2_2"].transpose(2, 0, 1).reshape(P, -1),
        "peer_u": a["peer_u_2"].T, "peer_v": a["peer_v_2"],
    }
    out.update(shape_constants())
    return {k: np.ascontiguousarray(v) for k, v in out.items()}


def kernel(**inputs):
    import concourse.bacc as bacc
    from concourse.bass_utils import run_bass_kernel_spmd
    arrays = layouts(inputs)
    nc = bacc.Bacc("TRN2", target_bir_lowering=False, num_devices=1)
    dram = {k: nc.dram_tensor(f"in_{k}", v.shape, F32, kind="ExternalInput").ap() for k, v in arrays.items()}
    scratch = [nc.dram_tensor(k, shape, F32, kind="Internal").ap() for k, shape in SCRATCH.items()]
    out = nc.dram_tensor("out", (D, T), F32, kind="ExternalOutput").ap()
    build(nc, dram, out, *scratch)
    r = run_bass_kernel_spmd(nc, [{f"in_{k}": v for k, v in arrays.items()}], core_ids=[0])
    return np.ascontiguousarray(r.results[0]["out"].T)[None]
```
